# Optimizing a Trainium2 kernel written in Bass

```python
import math
import jax, jax.numpy as jnp
from jax import lax
import numpy as np

D_MODEL = 2048
BATCH = 1
SEQ = 256
DEPTH = 1

CHUNK = 64
Q_BLOCK = 128
N_MEM = 256

SB_HEADS = 8
SB_HEAD_DIM = 128
DSA_HEADS = 8
DSA_HEAD_DIM = 128
IDX_HEADS = 8
IDX_HEAD_DIM = 64
DSA_TOPK_MAX = 256
MEM_HEADS = 4
MEM_HEAD_DIM = 256

N_BRANCH = 3
SB_W = SB_HEADS * SB_HEAD_DIM
DSA_W = DSA_HEADS * DSA_HEAD_DIM
MEM_W = MEM_HEADS * MEM_HEAD_DIM
BRANCH_WIDTH = 1024
IDX_Q_W = IDX_HEADS * IDX_HEAD_DIM
GATE_W = N_BRANCH * D_MODEL
D_IN = 3 * SB_W + 3 * DSA_W + MEM_W + IDX_Q_W + IDX_HEAD_DIM + IDX_HEADS + GATE_W

D_FF = 5504
CONV_WIDTH = 3
ROPE_THETA = 10000.0
NORM_EPS = 1e-6


def _rmsnorm(x, g):
    x32 = x.astype(jnp.float32)
    y = x32 * lax.rsqrt(jnp.mean(x32 * x32, axis=-1, keepdims=True) + NORM_EPS)
    return (y * g.astype(jnp.float32)).astype(x.dtype)

def _rope(x, positions):
    half = x.shape[-1] // 2
    inv = ROPE_THETA ** (-jnp.arange(half, dtype=jnp.float32) / half)
    ang = positions.astype(jnp.float32)[..., None] * inv
    cos = jnp.cos(ang)[:, :, None, :]
    sin = jnp.sin(ang)[:, :, None, :]
    x1 = x[..., :half].astype(jnp.float32)
    x2 = x[..., half:].astype(jnp.float32)
    out = jnp.concatenate([x1 * cos - x2 * sin, x2 * cos + x1 * sin], axis=-1)
    return out.astype(x.dtype)

def _to_blocks(a):
    B, S = a.shape[:2]
    return a.reshape((B, S // Q_BLOCK, Q_BLOCK) + a.shape[2:]).swapaxes(0, 1)

def _from_blocks(a):
    nb, B, qb, H, Dh = a.shape
    return a.swapaxes(0, 1).reshape(B, nb * qb, H * Dh)

def _stick_breaking(q, k, v):
    B, S, H, Dh = q.shape
    nb = S // Q_BLOCK
    starts = jnp.arange(nb, dtype=jnp.int32) * Q_BLOCK
    key_pos = jnp.arange(S, dtype=jnp.int32)
    scale = Dh ** -0.5

    def block(args):
        qb, t0 = args
        qpos = t0 + jnp.arange(Q_BLOCK, dtype=jnp.int32)
        visible = key_pos[None, :] < qpos[:, None]
        z = jnp.einsum('bqhd,bkhd->bhqk', qb, k).astype(jnp.float32) * scale
        sp = jnp.where(visible, jax.nn.softplus(z), 0.0)
        tail = lax.cumsum(sp, axis=3, reverse=True) - sp
        a = jnp.where(visible, jnp.exp(jax.nn.log_sigmoid(z) - tail), 0.0)
        return jnp.einsum('bhqk,bkhd->bqhd', a.astype(v.dtype), v)

    out = lax.map(block, (_to_blocks(q), starts))
    return _from_blocks(out)

def _dsa(q, k, v, q_idx, k_idx, w_idx, topk):
    B, S, H, Dh = q.shape
    nb = S // Q_BLOCK
    starts = jnp.arange(nb, dtype=jnp.int32) * Q_BLOCK
    key_chunk = jnp.arange(S, dtype=jnp.int32) // CHUNK
    idx_scale = IDX_HEAD_DIM ** -0.5
    scale = Dh ** -0.5

    def block(args):
        qb, qib, wib, t0 = args
        qchunk = (t0 + jnp.arange(Q_BLOCK, dtype=jnp.int32)) // CHUNK
        admissible = key_chunk[None, :] <= qchunk[:, None]
        logits = jnp.einsum('bqhd,bkd->bqhk', qib, k_idx).astype(jnp.float32) * idx_scale
        score = jnp.einsum('bqhk,bqh->bqk', jax.nn.relu(logits), wib.astype(jnp.float32))
        score = jnp.where(admissible[None], score, -jnp.inf)
        _, sel = lax.top_k(score, topk)
        valid = (sel // CHUNK) <= qchunk[None, :, None]
        k_sel = jax.vmap(lambda kk, ii: kk[ii])(k, sel)
        v_sel = jax.vmap(lambda vv, ii: vv[ii])(v, sel)
        s = jnp.einsum('bqhd,bqkhd->bhqk', qb, k_sel).astype(jnp.float32) * scale
        s = jnp.where(valid[:, None], s, -jnp.inf)
        p = jax.nn.softmax(s, axis=-1).astype(v.dtype)
        return jnp.einsum('bhqk,bqkhd->bqhd', p, v_sel)

    out = lax.map(block, (_to_blocks(q), _to_blocks(q_idx), _to_blocks(w_idx), starts))
    return _from_blocks(out)

def _mem_attn(q, mk, mv):
    B, S, H, Dh = q.shape
    s = jnp.einsum('bqhd,bmhd->bhqm', q, mk).astype(jnp.float32) * (Dh ** -0.5)
    p = jax.nn.softmax(s, axis=-1).astype(mv.dtype)
    return jnp.einsum('bhqm,bmhd->bqhd', p, mv).reshape(B, S, H * Dh)

def _causal_dwconv(u, w, b):
    S = u.shape[1]
    up = jnp.pad(u, ((0, 0), (CONV_WIDTH - 1, 0), (0, 0)))
    out = b
    for j in range(CONV_WIDTH):
        out = out + up[:, j:j + S] * w[j]
    return out

def _layer(x, mem, positions, attn_norm, mem_norm, w_in, b_gate, dsa_q_norm, dsa_k_norm,
           mem_q_norm, mem_k_norm, w_mem_kv, w_branch, w_out, ffn_norm, w_up, conv_w,
           conv_b, w_down, topk):
    B, S, D = x.shape
    h = _rmsnorm(x, attn_norm)
    proj = h @ w_in
    sizes = [SB_W, SB_W, SB_W, DSA_W, DSA_W, DSA_W, MEM_W, IDX_Q_W, IDX_HEAD_DIM,
             IDX_HEADS, GATE_W]
    cuts = [int(c) for c in np.cumsum(sizes)[:-1]]
    qa, ka, va, qb, kb, vb, qm, qi, ki, wi, gl = jnp.split(proj, cuts, axis=-1)

    sb_shape = (B, S, SB_HEADS, SB_HEAD_DIM)
    o_sb = _stick_breaking(qa.reshape(sb_shape), ka.reshape(sb_shape), va.reshape(sb_shape))

    dsa_shape = (B, S, DSA_HEADS, DSA_HEAD_DIM)
    qb = _rope(_rmsnorm(qb.reshape(dsa_shape), dsa_q_norm), positions)
    kb = _rope(_rmsnorm(kb.reshape(dsa_shape), dsa_k_norm), positions)
    vb = vb.reshape(dsa_shape)
    qi = _rope(qi.reshape(B, S, IDX_HEADS, IDX_HEAD_DIM), positions)
    ki = _rope(ki[:, :, None, :], positions)[:, :, 0, :]
    wi = wi * (IDX_HEADS ** -0.5)
    o_dsa = _dsa(qb, kb, vb, qi, ki, wi, topk)

    mh = _rmsnorm(mem, mem_norm)
    mk, mv = jnp.split(mh @ w_mem_kv, 2, axis=-1)
    mem_shape = (B, mem.shape[1], MEM_HEADS, MEM_HEAD_DIM)
    mk = _rmsnorm(mk.reshape(mem_shape), mem_k_norm)
    mv = mv.reshape(mem_shape)
    qm = _rmsnorm(qm.reshape(B, S, MEM_HEADS, MEM_HEAD_DIM), mem_q_norm)
    o_mem = _mem_attn(qm, mk, mv)

    gates = jax.nn.sigmoid((gl + b_gate).astype(jnp.float32)).astype(x.dtype)
    gates = gates.reshape(B, S, N_BRANCH, D)
    merged = (gates[:, :, 0] * (o_sb @ w_branch[0])
              + gates[:, :, 1] * (o_dsa @ w_branch[1])
              + gates[:, :, 2] * (o_mem @ w_branch[2]))
    x = x + merged @ w_out

    h2 = _rmsnorm(x, ffn_norm)
    u = _causal_dwconv(h2 @ w_up, conv_w, conv_b)
    g, val = jnp.split(u, 2, axis=-1)
    return x + (jax.nn.silu(g) * val) @ w_down

def first_inputs(seed: int = 0) -> dict:
    key = jax.random.key(seed)
    ks = jax.random.split(key, 20)
    f32 = jnp.float32
    nrm = lambda k, shape, s: jax.random.normal(k, shape, f32) * s
    gain = lambda k, shape: 1.0 + 0.02 * jax.random.normal(k, shape, f32)
    offset = jax.random.randint(ks[2], (BATCH, 1), 0, 64, dtype=jnp.int32) * CHUNK
    positions = offset + jnp.arange(SEQ, dtype=jnp.int32)[None, :]
    return {
        "x": nrm(ks[0], (BATCH, SEQ, D_MODEL), 1.0),
        "mem": nrm(ks[1], (BATCH, N_MEM, D_MODEL), 1.0),
        "positions": positions,
        "attn_norm": gain(ks[3], (DEPTH, D_MODEL)),
        "mem_norm": gain(ks[4], (DEPTH, D_MODEL)),
        "w_in": nrm(ks[5], (DEPTH, D_MODEL, D_IN), D_MODEL ** -0.5),
        "b_gate": nrm(ks[6], (DEPTH, GATE_W), 0.02),
        "dsa_q_norm": gain(ks[7], (DEPTH, DSA_HEAD_DIM)),
        "dsa_k_norm": gain(ks[8], (DEPTH, DSA_HEAD_DIM)),
        "mem_q_norm": gain(ks[9], (DEPTH, MEM_HEAD_DIM)),
        "mem_k_norm": gain(ks[10], (DEPTH, MEM_HEAD_DIM)),
        "w_mem_kv": nrm(ks[11], (DEPTH, D_MODEL, 2 * MEM_W), D_MODEL ** -0.5),
        "w_branch": nrm(ks[12], (DEPTH, N_BRANCH, BRANCH_WIDTH, D_MODEL), BRANCH_WIDTH ** -0.5),
        "w_out": nrm(ks[13], (DEPTH, D_MODEL, D_MODEL), D_MODEL ** -0.5),
        "ffn_norm": gain(ks[14], (DEPTH, D_MODEL)),
        "w_up": nrm(ks[15], (DEPTH, D_MODEL, 2 * D_FF), D_MODEL ** -0.5),
        "conv_w": nrm(ks[16], (DEPTH, CONV_WIDTH, 2 * D_FF), CONV_WIDTH ** -0.5),
        "conv_b": nrm(ks[17], (DEPTH, 2 * D_FF), 0.02),
        "w_down": nrm(ks[18], (DEPTH, D_FF, D_MODEL), D_FF ** -0.5),
    }

def first_block(x, mem, positions, attn_norm, mem_norm, w_in, b_gate, dsa_q_norm, dsa_k_norm,
              mem_q_norm, mem_k_norm, w_mem_kv, w_branch, w_out, ffn_norm, w_up, conv_w,
              conv_b, w_down):
    topk = min(DSA_TOPK_MAX, x.shape[1] // 4)
    for l in range(DEPTH):
        x = _layer(x, mem, positions, attn_norm[l], mem_norm[l], w_in[l], b_gate[l],
                   dsa_q_norm[l], dsa_k_norm[l], mem_q_norm[l], mem_k_norm[l],
                   w_mem_kv[l], w_branch[l], w_out[l], ffn_norm[l], w_up[l], conv_w[l],
                   conv_b[l], w_down[l], topk)
    return x


DEPTH_2 = 2

N_MIXERS = 2

GLA_HEADS = 4
GLA_QK = D_MODEL // 2
GLA_V = D_MODEL
GLA_DK = GLA_QK // GLA_HEADS
GLA_DV = GLA_V // GLA_HEADS
GLA_GATE_RANK = 16
GLA_GATE_TAU = 16.0
GLA_CHUNK = 64
GLA_IN = 2 * GLA_QK + 2 * GLA_V + GLA_GATE_RANK

MLA_HEADS = 16
MLA_Q_RANK = 512
MLA_KV_RANK = 512
MLA_NOPE = 128
MLA_ROPE = 64
MLA_V = 128
MLA_WIDTH = MLA_HEADS * MLA_V
MLA_IN = MLA_Q_RANK + MLA_KV_RANK + MLA_ROPE + MLA_WIDTH


def rms_norm(x, g, eps=NORM_EPS):
    xf = x.astype(jnp.float32)
    y = xf * lax.rsqrt(jnp.mean(xf * xf, axis=-1, keepdims=True) + eps)
    return (y * g.astype(jnp.float32)).astype(x.dtype)

def _to_chunks(t, n_chunks):
    B, S, H, D = t.shape
    return t.reshape(B, n_chunks, S // n_chunks, H, D).transpose(0, 3, 1, 2, 4)

def gla_mixer(h, w_in, w_gk2, b_gk, g_onorm, w_out):
    B, S, _ = h.shape
    nC = S // GLA_CHUNK
    proj = h @ w_in
    q, k, v, gate, gk_low = jnp.split(
        proj, [GLA_QK, 2 * GLA_QK, 2 * GLA_QK + GLA_V, 2 * GLA_QK + 2 * GLA_V], axis=-1)
    gk = gk_low @ w_gk2 + b_gk
    log_a = jax.nn.log_sigmoid(gk.astype(jnp.float32)) / GLA_GATE_TAU

    q = _to_chunks(q.reshape(B, S, GLA_HEADS, GLA_DK), nC) * (GLA_DK ** -0.5)
    k = _to_chunks(k.reshape(B, S, GLA_HEADS, GLA_DK), nC)
    v = _to_chunks(v.reshape(B, S, GLA_HEADS, GLA_DV), nC)
    log_a = _to_chunks(log_a.reshape(B, S, GLA_HEADS, GLA_DK), nC)

    b = jnp.cumsum(log_a, axis=3)
    b_last = b[..., -1:, :]
    q_e = q * jnp.exp(b)
    k_e = k * jnp.exp(-b)
    k_last = k * jnp.exp(b_last - b)

    A = jnp.einsum('bhncd,bhnsd->bhncs', q_e, k_e)
    causal = jnp.tril(jnp.ones((GLA_CHUNK, GLA_CHUNK), dtype=bool))
    A = jnp.where(causal, A, 0.0)
    o_intra = jnp.einsum('bhncs,bhnsv->bhncv', A, v.astype(A.dtype))

    def step(state, xs):
        q_c, kl_c, v_c, dl_c = xs
        o_c = jnp.einsum('bhcd,bhdv->bhcv', q_c, state)
        state = state * dl_c[..., :, None] + jnp.einsum('bhcd,bhcv->bhdv', kl_c, v_c)
        return state, o_c

    state0 = jnp.zeros((B, GLA_HEADS, GLA_DK, GLA_DV), dtype=jnp.float32)
    xs = (jnp.moveaxis(q_e, 2, 0).astype(jnp.float32),
          jnp.moveaxis(k_last, 2, 0).astype(jnp.float32),
          jnp.moveaxis(v, 2, 0).astype(jnp.float32),
          jnp.moveaxis(jnp.exp(b_last[..., 0, :]), 2, 0).astype(jnp.float32))
    _, o_inter = lax.scan(step, state0, xs)
    o = o_intra + jnp.moveaxis(o_inter, 0, 2)

    o = o.transpose(0, 2, 3, 1, 4).reshape(B, S, GLA_HEADS, GLA_DV).astype(h.dtype)
    o = rms_norm(o, g_onorm).reshape(B, S, GLA_V)
    return (o * jax.nn.silu(gate)) @ w_out

def _rope_2(t, cos, sin):
    half = t.shape[-1] // 2
    t1, t2 = t[..., :half], t[..., half:]
    return jnp.concatenate([t1 * cos - t2 * sin, t2 * cos + t1 * sin], axis=-1)

def mla_mixer(h, positions, w_in, g_qa, w_qb, g_kva, w_kvb, w_out):
    B, S, _ = h.shape
    proj = h @ w_in
    c_q, c_kv, k_rope, gate = jnp.split(
        proj, [MLA_Q_RANK, MLA_Q_RANK + MLA_KV_RANK, MLA_Q_RANK + MLA_KV_RANK + MLA_ROPE], axis=-1)
    q = (rms_norm(c_q, g_qa) @ w_qb).reshape(B, S, MLA_HEADS, MLA_NOPE + MLA_ROPE)
    kv = (rms_norm(c_kv, g_kva) @ w_kvb).reshape(B, S, MLA_HEADS, MLA_NOPE + MLA_V)
    q_nope, q_rope = q[..., :MLA_NOPE], q[..., MLA_NOPE:]
    k_nope, v = kv[..., :MLA_NOPE], kv[..., MLA_NOPE:]

    inv_freq = ROPE_THETA ** (-jnp.arange(0, MLA_ROPE, 2, dtype=jnp.float32) / MLA_ROPE)
    ang = positions.astype(jnp.float32)[..., None] * inv_freq
    cos, sin = jnp.cos(ang), jnp.sin(ang)
    q_rope = _rope_2(q_rope, cos[:, :, None, :], sin[:, :, None, :]).astype(h.dtype)
    k_rope = _rope_2(k_rope, cos, sin).astype(h.dtype)
    q = jnp.concatenate([q_nope, q_rope], axis=-1)
    k = jnp.concatenate(
        [k_nope, jnp.broadcast_to(k_rope[:, :, None, :], (B, S, MLA_HEADS, MLA_ROPE))], axis=-1)
    scale = (MLA_NOPE + MLA_ROPE) ** -0.5

    n_blocks = S // Q_BLOCK
    q_blocks = q.reshape(B, n_blocks, Q_BLOCK, MLA_HEADS, -1).transpose(1, 0, 2, 3, 4)
    starts = jnp.arange(n_blocks, dtype=jnp.int32) * Q_BLOCK
    k_idx = jnp.arange(S, dtype=jnp.int32)

    def attend(args):
        qb, start = args
        s = jnp.einsum('bqhd,bkhd->bhqk', qb, k).astype(jnp.float32) * scale
        q_idx = start + jnp.arange(Q_BLOCK, dtype=jnp.int32)
        s = jnp.where(k_idx[None, :] <= q_idx[:, None], s, jnp.finfo(jnp.float32).min)
        p = jax.nn.softmax(s, axis=-1).astype(v.dtype)
        return jnp.einsum('bhqk,bkhv->bqhv', p, v)

    o = lax.map(attend, (q_blocks, starts))
    o = o.transpose(1, 0, 2, 3, 4).reshape(B, S, MLA_WIDTH)
    return (o * jax.nn.silu(gate)) @ w_out

def second_inputs(seed: int = 0) -> dict:
    key = jax.random.key(seed)
    ks = jax.random.split(key, 16)

    def w(k, shape):
        return jax.random.normal(k, shape, jnp.float32) * (shape[0] ** -0.5)

    def gain(k, n):
        return 1.0 + 0.05 * jax.random.normal(k, (n,), jnp.float32)

    x = jax.random.normal(ks[0], (BATCH, SEQ, D_MODEL), jnp.float32)
    positions = jnp.broadcast_to(jnp.arange(SEQ, dtype=jnp.int32)[None, :], (BATCH, SEQ))
    return {
        "x": x,
        "positions": positions,
        "l0_pre_norm": gain(ks[1], D_MODEL),
        "l0_gla_w_in": w(ks[2], (D_MODEL, GLA_IN)),
        "l0_gla_w_gk2": w(ks[3], (GLA_GATE_RANK, GLA_QK)),
        "l0_gla_b_gk": 0.1 * jax.random.normal(ks[4], (GLA_QK,), jnp.float32),
        "l0_gla_g_onorm": gain(ks[5], GLA_DV),
        "l0_gla_w_out": w(ks[6], (GLA_V, D_MODEL)),
        "l0_post_norm": gain(ks[7], D_MODEL),
        "l1_pre_norm": gain(ks[8], D_MODEL),
        "l1_mla_w_in": w(ks[9], (D_MODEL, MLA_IN)),
        "l1_mla_g_qa": gain(ks[10], MLA_Q_RANK),
        "l1_mla_w_qb": w(ks[11], (MLA_Q_RANK, MLA_HEADS * (MLA_NOPE + MLA_ROPE))),
        "l1_mla_g_kva": gain(ks[12], MLA_KV_RANK),
        "l1_mla_w_kvb": w(ks[13], (MLA_KV_RANK, MLA_HEADS * (MLA_NOPE + MLA_V))),
        "l1_mla_w_out": w(ks[14], (MLA_WIDTH, D_MODEL)),
        "l1_post_norm": gain(ks[15], D_MODEL),
    }

def second_block(x, positions,
              l0_pre_norm, l0_gla_w_in, l0_gla_w_gk2, l0_gla_b_gk, l0_gla_g_onorm, l0_gla_w_out,
              l0_post_norm,
              l1_pre_norm, l1_mla_w_in, l1_mla_g_qa, l1_mla_w_qb, l1_mla_g_kva, l1_mla_w_kvb,
              l1_mla_w_out, l1_post_norm):
    layers = [
        (l0_pre_norm, (l0_gla_w_in, l0_gla_w_gk2, l0_gla_b_gk, l0_gla_g_onorm, l0_gla_w_out),
         l0_post_norm),
        (l1_pre_norm, (l1_mla_w_in, l1_mla_g_qa, l1_mla_w_qb, l1_mla_g_kva, l1_mla_w_kvb,
                       l1_mla_w_out), l1_post_norm),
    ]
    for i in range(DEPTH_2):
        g_pre, params, g_post = layers[i]
        h = rms_norm(x, g_pre)
        if i % N_MIXERS == 0:
            y = gla_mixer(h, *params)
        else:
            y = mla_mixer(h, positions, *params)
        x = x + rms_norm(y, g_post)
    return x


def setup_inputs(seed=0):
    out = dict(first_inputs(seed))
    for name, value in second_inputs(seed + 1).items():
        if name != "x":
            out[name + "_2"] = value
    return out


def reference(
    x, mem, positions, attn_norm, mem_norm, w_in, b_gate, dsa_q_norm, dsa_k_norm, mem_q_norm,
    mem_k_norm, w_mem_kv, w_branch, w_out, ffn_norm, w_up, conv_w, conv_b, w_down, positions_2,
    l0_pre_norm_2, l0_gla_w_in_2, l0_gla_w_gk2_2, l0_gla_b_gk_2, l0_gla_g_onorm_2,
    l0_gla_w_out_2, l0_post_norm_2, l1_pre_norm_2, l1_mla_w_in_2, l1_mla_g_qa_2, l1_mla_w_qb_2,
    l1_mla_g_kva_2, l1_mla_w_kvb_2, l1_mla_w_out_2, l1_post_norm_2,
):
    x = first_block(
        x, mem, positions, attn_norm, mem_norm, w_in, b_gate, dsa_q_norm, dsa_k_norm,
        mem_q_norm, mem_k_norm, w_mem_kv, w_branch, w_out, ffn_norm, w_up, conv_w, conv_b,
        w_down,
    )
    return second_block(
        x, positions_2, l0_pre_norm_2, l0_gla_w_in_2, l0_gla_w_gk2_2, l0_gla_b_gk_2,
        l0_gla_g_onorm_2, l0_gla_w_out_2, l0_post_norm_2, l1_pre_norm_2, l1_mla_w_in_2,
        l1_mla_g_qa_2, l1_mla_w_qb_2, l1_mla_g_kva_2, l1_mla_w_kvb_2, l1_mla_w_out_2,
        l1_post_norm_2,
    )


_drawn_inputs = setup_inputs


def setup_inputs(seed=0):
    import zlib

    import numpy as np

    out = dict(_drawn_inputs(seed))
    spreads = {}
    factors = {'mem_norm': 8.0,
     'b_gate': 8.0,
     'dsa_q_norm': 22.821,
     'dsa_k_norm': 8.0,
     'mem_q_norm': 8.0,
     'mem_k_norm': 8.0,
     'ffn_norm': 8.0,
     'conv_b': 8.0,
     'l0_gla_b_gk_2': 5.695,
     'l0_gla_g_onorm_2': 39.368,
     'l0_post_norm_2': 39.672,
     'l1_pre_norm_2': 2.689,
     'l1_mla_g_qa_2': 5.688,
     'l1_mla_g_kva_2': 3.844,
     'l1_post_norm_2': 43.864,
     'l0_pre_norm_2': 3.43,
     'l0_gla_w_gk2_2': 4.282}
    for name, (base, spread) in spreads.items():
        noise = np.random.default_rng([zlib.crc32(name.encode()), seed]).standard_normal(out[name].shape)
        drawn = base * np.exp(spread * noise) if base else spread * noise
        out[name] = __import__('jax').numpy.asarray(drawn.astype(out[name].dtype))
    for name, factor in factors.items():
        out[name] = (out[name] * factor).astype(out[name].dtype)
    return out
```

```python
from contextlib import ExitStack
from math import lcm

import numpy as np

import concourse.bass as bass
from concourse import mybir

P = 128
ALU = mybir.AluOpType
ACT = mybir.ActivationFunctionType
F32 = mybir.dt.float32
F32R = mybir.dt.float32r
I32 = mybir.dt.int32
AX = mybir.AxisListType

EPS = 1e-6
HIDDEN = -1e30
NEG_INADMISSIBLE = -3.0e38
NEG_TAKEN = -3.4e38

RING = 4
TK, TC = 4, 256
PSUM_RING = 2


class Phase:

    def __init__(self, name, kind, blocks, ktiles, cols, src):
        self.name, self.kind, self.blocks, self.ktiles = name, kind, blocks, ktiles
        self.cols, self.src = cols, src
        self.bt = len(ktiles)
        self.n = blocks * self.bt
        self.period = lcm(PSUM_RING * self.bt, RING)


class Plan:

    def __init__(self, phases):
        self.phases = {}
        self.shape = []
        self.end_of = []
        b = 0
        for ph in phases:
            ph.t0, ph.b0 = len(self.shape), b
            for j in range(ph.n):
                nk = ph.ktiles[j % ph.bt]
                self.shape.append((nk, ph.cols, len(ph.src(j // ph.bt, j % ph.bt))))
            b += ph.blocks
            self.phases[ph.name] = ph
        self.tiles = len(self.shape)
        total = [0] * RING
        self.landed = []
        for t, (_, _, dmas) in enumerate(self.shape):
            total[t % RING] += 16 * dmas
            self.landed.append(total[t % RING])

    def rounds(self, ph, ahead):
        n = 0
        while (n + 1) * ph.period <= ph.n:
            for j in range(ph.period):
                a, b = ph.t0 + j + ahead, ph.t0 + n * ph.period + j + ahead
                if b >= self.tiles or self.shape[a] != self.shape[b]:
                    return n
                if self.landed[b] - self.landed[a] != n * (self.landed[a + ph.period] - self.landed[a]):
                    return n
            n += 1
        return n

    def landed_at(self, t, period, i):
        if isinstance(i, int):
            return self.landed[t + i * period]
        return i * (self.landed[t + period] - self.landed[t]) + self.landed[t]


def steps(eng, plan, ph, ahead, whole, tile, from_round=0):
    n = 0 if whole else plan.rounds(ph, ahead)
    if n - from_round >= 2:
        for i in range(from_round):
            for j in range(ph.period):
                tile(j, i)
        with eng.Fori(from_round, n) as i:
            for j in range(ph.period):
                tile(j, i)
    else:
        n = 0
    for t in range(n * ph.period, ph.n):
        tile(t % ph.period, t // ph.period)


D = 2048
S = 256
KD = D // P
NT = S // P
W = 1024
KW = W // P
HEADS, HD = 8, 128
IH, ID = 8, 64
TOPK = S // 4
MH, MD = 4, 256
DFF = 5504
KF = DFF // P
GATE0 = 3 * W + 3 * W + W + IH * ID + ID + IH
DECAY_RANK = 16
GH, GK, GV = 4, 256, 512
CH = 64
GTAU = 16.0
LH, LR, LN, LV = 16, 64, 128, 128
LRANK = 512
KL = LRANK // P
ROUNDER = 1.5 * 2.0 ** 23
TURN = (6.28125, float(np.float32(round((2 * np.pi - 6.28125) * 2 ** 21) / 2 ** 21)))
TURN += (2 * np.pi - sum(TURN),)
PI_BELOW = 3.1415925
TRI = 384

ROWS = {}
_at = 0
for _name, _n in (("attn_norm", KD), ("mem_norm", KD), ("b_gate", 3 * KD), ("ffn_norm", KD),
                  ("l0_pre", KD), ("l0_post", KD),
                  ("l1_pre", KD), ("l1_post", KD), ("g_qa", KL), ("g_kva", KL), ("g_onorm", GV // P),
                  ("mem_q_norm", MD // P), ("mem_k_norm", MD // P),
                  ("conv_w0", 2 * KF), ("conv_w1", 2 * KF), ("conv_w2", 2 * KF), ("conv_b", 2 * KF)):
    ROWS[_name] = (_at, _n)
    _at += _n
NVEC = _at
STAGES = [("attn_norm", "mem_norm", "b_gate", "ffn_norm", "l0_pre", "l0_post"),
          ("l1_pre", "l1_post", "g_qa", "g_kva", "g_onorm", "mem_q_norm", "mem_k_norm"),
          ("conv_w0",), ("conv_w1",), ("conv_w2",), ("conv_b",)]


def build_program(nc, x, mem, positions, attn_norm, mem_norm, w_in, b_gate, dsa_q_norm, dsa_k_norm,
                  mem_q_norm, mem_k_norm, w_mem_kv, w_branch, w_out, ffn_norm, w_up, conv_w, conv_b,
                  w_down, positions_2, l0_pre, gla_w_in, gla_w_gk2, gla_b_gk, g_onorm, gla_w_out,
                  l0_post, l1_pre, mla_w_in, g_qa, w_qb, g_kva, w_kvb, mla_w_out, l1_post,
                  inv64, inv32, out):

    def rows_of(w):
        return w.rearrange("(k p) n -> p k n", p=P)

    def cols_from(w, col0, kts, cols=TC, width=TC):
        w3 = rows_of(w)
        k0 = [sum(kts[:j]) for j in range(len(kts))]

        def src(b, kt):
            return [(slice(0, cols), w3[:, k0[kt]:k0[kt] + kts[kt], bass.ds(b * width + col0, cols)])]
        return src

    def pair_from(w, kts, col_a, col_b, step):
        w3 = rows_of(w)

        def src(b, kt):
            k = slice(TK * kt, TK * kt + kts[kt])
            return [(slice(0, P), w3[:, k, bass.ds(b * step + col_a, P)]),
                    (slice(P, 2 * P), w3[:, k, bass.ds(b * step + col_b, P)])]
        return src

    K16, K8, K4 = [TK] * 4, [TK] * 2, [TK]
    win, wup = w_in[0], w_up[0]
    down = [w_down[0][0:16 * P, :], w_down[0][16 * P:32 * P, :], w_down[0][32 * P:KF * P, :]]
    ROPE0 = LN

    def qrope_src(b, kt):
        w3 = rows_of(w_qb)
        hw = LN + LR
        return [(slice(LR * h, LR * h + LR), w3[:, 0:TK, bass.ds(b * (4 * hw) + h * hw + ROPE0, LR)])
                for h in range(4)]

    phases = [
        Phase("memk", "tm", 4, K16, TC, cols_from(w_mem_kv[0], 0, K16)),
        Phase("memv", "tm", 4, K16, TC, cols_from(w_mem_kv[0], W, K16)),
        Phase("qm", "tm", 4, K16, TC, cols_from(win, 6 * W, K16)),
        Phase("gate2", "fm", 8, K16, TC, cols_from(win, GATE0 + 2 * D, K16)),
        Phase("branch2", "fm", 8, K8, TC, cols_from(w_branch[0, 2], 0, K8)),
        Phase("sbqk", "fm", 8, K16, TC, cols_from(win, 0, K16)),
        Phase("sbv", "tm", 4, K16, TC, cols_from(win, 2 * W, K16)),
        Phase("gate0", "fm", 8, K16, TC, cols_from(win, GATE0, K16)),
        Phase("branch0", "fm", 8, K8, TC, cols_from(w_branch[0, 0], 0, K8)),
        Phase("qi", "tm", 2, K16, TC, cols_from(win, 7 * W, K16)),
        Phase("kiwi", "tm", 1, K16, ID + IH, cols_from(win, 7 * W + IH * ID, K16, ID + IH)),
        Phase("qb", "tm", 4, K16, TC, cols_from(win, 3 * W, K16)),
        Phase("kb", "tm", 4, K16, TC, cols_from(win, 4 * W, K16)),
        Phase("vb", "tm", 4, K16, TC, cols_from(win, 5 * W, K16)),
        Phase("gate1", "fm", 8, K16, TC, cols_from(win, GATE0 + D, K16)),
        Phase("branch1", "fm", 8, K8, TC, cols_from(w_branch[0, 1], 0, K8)),
        Phase("wout", "fm", 8, K16, TC, cols_from(w_out[0], 0, K16)),
    ]
    FFN = [(0, 16), (16, 16), (32, KF - 32)]
    for f, (c0, nf) in enumerate(FFN):
        kts = [min(TK, nf - k) for k in range(0, nf, TK)]
        phases += [
            Phase(f"up{f}", "fm", nf, K16, TC, pair_from(wup, K16, c0 * P, DFF + c0 * P, P)),
            Phase(f"down{f}", "fm", 8, kts, TC, cols_from(down[f], 0, kts)),
        ]
    phases += [
        Phase("decay", "tm", 1, K16, DECAY_RANK, cols_from(gla_w_in, 3 * D, K16, DECAY_RANK)),
        Phase("glaqk", "fm", 8, K16, TC, cols_from(gla_w_in, 0, K16)),
        Phase("glav", "tm", 8, K16, TC, cols_from(gla_w_in, D, K16)),
        Phase("glagate", "fm", 8, K16, TC, cols_from(gla_w_in, 2 * D, K16)),
        Phase("glaout", "fm", 8, K16, TC, cols_from(gla_w_out, 0, K16)),
        Phase("latent", "fm", 4, K16, TC, cols_from(mla_w_in, 0, K16)),
        Phase("krope", "tm", 1, K16, LR, cols_from(mla_w_in, 2 * LRANK, K16, LR)),
        Phase("qrope", "tm", 4, K4, TC, qrope_src),
    ]
    for r in range(2):
        hw = LN + LR
        phases += [
            Phase(f"qnope{r}", "fm", 4, K4, TC,
                  pair_from(w_qb, K4, 8 * r * hw, 8 * r * hw + hw, 2 * hw)),
            Phase(f"kv{r}", "kv", 8, K4, TC, cols_from(w_kvb, 8 * r * TC, K4)),
            Phase(f"mlagate{r}", "fm", 4, K16, TC,
                  cols_from(mla_w_in, 2 * LRANK + LR + r * 8 * P, K16)),
        ]
    phases += [Phase("mlaout", "fm", 8, K16, TC, cols_from(mla_w_out, 0, K16))]
    plan = Plan(phases)
    PH = plan.phases

    def chunk_rows(v, n):
        return v.rearrange("(c p) -> c p", p=P)

    VEC_SRC = {n: chunk_rows(v, n) for n, v in (
        ("attn_norm", attn_norm[0]), ("mem_norm", mem_norm[0]), ("b_gate", b_gate[0]),
        ("ffn_norm", ffn_norm[0]), ("l0_pre", l0_pre), ("l0_post", l0_post), ("l1_pre", l1_pre),
        ("l1_post", l1_post), ("g_qa", g_qa), ("g_kva", g_kva), ("g_onorm", g_onorm),
        ("mem_q_norm", mem_q_norm[0]), ("mem_k_norm", mem_k_norm[0]), ("conv_w0", conv_w[0, 0]),
        ("conv_w1", conv_w[0, 1]), ("conv_w2", conv_w[0, 2]), ("conv_b", conv_b[0]))}
    N_VEC_DMAS = len(VEC_SRC)

    with ExitStack() as ctx:
        def sb(name, shape, dt=F32):
            return ctx.enter_context(nc.sbuf_tensor(name, shape, dt))

        def sem(name):
            return ctx.enter_context(nc.semaphore(name))

        weight_raw = sb("weight_raw", [P, RING, TK, TC])
        weight_hi = sb("weight_hi", [P, RING, TK, TC], F32R)
        weight_lo = sb("weight_lo", [P, RING, TK, TC], F32R)
        xT = sb("xT", [P, KD, S])
        h_hi, h_lo = (sb(n, [P, KD, S], F32R) for n in ("h_hi", "h_lo"))
        u_hi, u_lo = (sb(n, [P, KD, S], F32R) for n in ("u_hi", "u_lo"))
        ident = sb("ident", [P, P])
        ones = sb("ones", [P, P])
        tri_ge = sb("tri_ge", [P, P])
        tri_chunk = sb("tri_chunk", [P, P])
        vec = sb("vec", [P, NVEC])
        small = sb("small", [P, 208])
        rstd = sb("rstd", [P, S])
        arena = sb("arena", [P, 18048])

        def area(at, *shape):
            n = int(np.prod(shape))
            v = arena[:, at:at + n]
            if len(shape) == 1:
                return v
            names = "abcd"[:len(shape)]
            return v.rearrange(f"p ({' '.join(names)}) -> p {' '.join(names)}",
                               **{k: s for k, s in zip(names, shape)})

        blk = ctx.enter_context(nc.psum_tensor("blk", [P, PSUM_RING, 2, 512], F32))
        pa = ctx.enter_context(nc.psum_tensor("pa", [P, 4, 512], F32))

        rows_x = area(0, NT, D)
        rows_mem = area(4096, NT, D)
        memT = area(8192, KD, S)
        squares = area(12288, KD, S)
        stage = area(16384, len(STAGES), P)
        angle, turns = area(17152, 256), area(17408, 256)
        gates = xT
        merged = area(0, KD, S)
        mem_k, mem_q = area(4096, NT, MH, MD), area(6144, NT, MH, MD)
        mem_v = area(8192, NT, MH, MD)
        mem_kT, mem_qT = area(10240, KW, S), area(12288, KW, S)
        mem_sq = area(14336, NT, MH, MD)
        mem_p = area(14336, 4, 512)
        mem_pT = area(4096, 4, 512)
        qkT = area(4096, 2 * KW, S)
        val = area(8192, NT, W)
        T = 10240
        sb_z, sb_l, sb_sp = (area(T + n * 4 * TRI, 4, TRI) for n in range(3))
        qi, ki_wi = area(T, NT, IH * ID), area(T + 1024, NT, ID + IH)
        qiT, kiT = area(T + 2048, IH, S), area(T + 4096, S)
        logits = area(T + 4352, 2048)
        rope_a, rope_b = area(T + 4352, 1024), area(T + 5376, 1024)
        score, left, chosen = (area(T + 6400 + n * TRI, TRI) for n in range(3))
        kb_rows = area(T, NT, W)
        dsa_sq = area(T + 2048, NT, W)
        probs, probsT = area(T, 4, TRI), area(T + 4 * TRI, 4, TRI)
        conv = area(0, 2, 2, S)
        gated = area(1024, 2, S)
        ff = area(1536, 2, S)
        g_q, g_k, g_v = area(0, 2 * GH, S), area(2048, 2 * GH, S), area(4096, NT, D)
        g_gate = area(8192, KD, S)
        g_la = area(12288, NT, W)
        g_ke = area(12288, 2 * GH, S)
        g_e = area(14336, 2 * GH, S)
        g_a = area(14336, 4, TRI)
        g_rstd = area(16384, GH, S)
        w_decay = area(16384, W)
        low_rows = area(17408, NT, DECAY_RANK)
        lowT = area(17440, S)
        g_o = area(0, KD, S)
        y_gla = area(4096, KD, S)
        latent, latent_sq = area(0, 2 * KL, S), area(2048, 2 * KL, S)
        q_nope, k_nope, l_v = area(0, KW, S), area(2048, KW, S), area(4096, NT, W)
        l_o, l_gate = area(6144, KD, S), area(10240, KW, S)
        q_rope = area(6144, NT, LH * LR)
        q_ropeT = area(12288, KW, S)
        l_rope_a, l_rope_b = area(14336, 1024), area(15360, 1024)
        causal = area(17408, TRI)
        k_rope, k_ropeT = area(4096, NT, 2 * LR), area(17792, S)
        lprobs, lprobsT = area(14336, 4, TRI), area(15872, 4, TRI)
        y_mla = area(0, KD, S)
        rows_out = area(4096, NT, D)
        pos_i = sb("pos_i", [P, 2 * NT], I32)
        pos_f = sb("pos_f", [P, 2 * NT])
        inv = sb("inv", [P, 96])
        qk_gain = sb("qk_gain", [P, 2, HD])
        cos, sin = sb("cos", [P, 256]), sb("sin", [P, 256])

        def table(t, which, tt):
            at, half = ((0, 64), (128, 32), (192, 32))[which]
            return t[:, at + tt * half:at + (tt + 1) * half]

        def col(name, c, n=1):
            return vec[:, bass.ds(ROWS[name][0] + c, n)]

        weight_landed = [sem(f"weight_landed{r}") for r in range(RING)]
        hi_made, lo_made = sem("hi_made"), sem("lo_made")
        tile_used = sem("tile_used")
        block_out = sem("block_out")
        mem_in, x_in, vec_in, small_in = sem("mem_in"), sem("x_in"), sem("vec_in"), sem("small_in")
        again_in, decay_in, stored = sem("again_in"), sem("decay_in"), sem("stored")
        consts = sem("consts")
        act_own, dve_own, pool_own = sem("act_own"), sem("dve_own"), sem("pool_own")
        vec_turned, vec_ready = sem("vec_turned"), sem("vec_ready")
        turned, turned_out = sem("turned"), sem("turned_out")
        angles, sines, tables = sem("angles"), sem("sines"), sem("tables")
        NORM = {k: sem(f"norm_{k}") for k in ("sq", "sum", "inv", "rstd", "hn", "hi", "done")}
        HEADN = {k: sem(f"head_norm_{k}") for k in ("sq", "inv", "rstd", "scaled", "turned", "out")}
        base, at = {}, dict.fromkeys(NORM, 0)
        for n, chunks, splits in (("mem", KD, 1), ("x", KD, 1), ("ffn", KD, 1), ("pre0", KD, 1),
                                  ("post0", KD, 0), ("pre1", KD, 1), ("qa", KL, 1), ("kva", KL, 1),
                                  ("post1", KD, 0)):
            base[n] = dict(at)
            for k, inc in (("sq", 4), ("sum", 1), ("inv", 1), ("rstd", 1), ("hn", chunks * splits),
                           ("hi", 4 * splits), ("done", 4)):
                at[k] += inc
        at = dict.fromkeys(HEADN, 0)
        for n, parts in (("memk", 2), ("memq", 2), ("dsaq", 1), ("dsak", 1)):
            base[n] = dict(at)
            for k in HEADN:
                at[k] += parts if k in ("scaled", "out") else 1

        def norm_at(eng, n, k, v):
            eng.wait_ge((HEADN if n in ("memk", "memq", "dsaq", "dsak") else NORM)[k], base[n][k] + v)

        ATT = {k: {x: sem(f"attend_{k}_{x}") for x in ("scores", "masked", "exp", "probs", "turned",
                                               "probsT", "pv", "hi", "lo")}
               for k in ("mem", "dsa", "mla")}
        SB = {x: sem(f"sb_{x}") for x in ("z", "abs", "exp", "zs", "ln", "sp", "spm", "cum", "u",
                                         "um", "a", "pv", "hi", "lo")}
        IX = {x: sem(f"index_{x}") for x in ("roped", "turned", "qT", "kturned", "kT", "logits",
                                            "relu", "score", "chosen")}
        merged_out, merged_hi, merged_ready = sem("merged_out"), sem("merged_hi"), sem("merged_ready")
        gate_done = sem("gate_done")
        conv_mid, conv_one, conv_out, silu_out, ff_out, ff_hi, ff_ready = (
            sem(n) for n in ("conv_mid", "conv_one", "conv_out", "silu_out", "ff_out", "ff_hi", "ff_ready"))
        GL = {x: sem(f"gla_{x}") for x in ("low", "lowT", "gk", "abs", "l", "la", "cum", "last", "eb",
                                          "q", "enb", "ke", "diff", "el", "kl", "rows", "step", "a",
                                          "am", "o", "oout", "sq", "sum", "inv", "rstd", "on", "out",
                                          "hi", "ready", "bias_row")}
        ML = {x: sem(f"mla_{x}") for x in ("k_roped", "kturned", "kT", "q_roped", "qturned", "qT",
                                          "out", "gated", "hi", "ready")}
        oturned, orows = sem("oturned"), sem("orows")

        block = ctx.enter_context(nc.Block())

        @block.sync
        def _(sp):
            sp.dma_start(rows_mem, mem[0].rearrange("(t p) d -> p t d", p=P)).then_inc(mem_in, 16)
            at = 0
            for g, names in enumerate(STAGES):
                at = 0
                for n in names:
                    rows = VEC_SRC[n]
                    sp.dma_start(stage[at:at + ROWS[n][1], g, :], rows).then_inc(vec_in, 16)
                    at += ROWS[n][1]
            sp.dma_start(rows_x, x[0].rearrange("(t p) d -> p t d", p=P)).then_inc(x_in, 16)

            def load(ph):
                def tile(j, i):
                    t = ph.t0 + j
                    if not isinstance(i, int):
                        sp.wait_ge(lo_made, i * ph.period + (t - RING + 1))
                    elif t + i * ph.period >= RING:
                        sp.wait_ge(lo_made, t + i * ph.period - RING + 1)
                    b = i * (ph.period // ph.bt) + j // ph.bt
                    nk = ph.ktiles[j % ph.bt]
                    for c, dram in ph.src(b, j % ph.bt):
                        sp.dma_start(weight_raw[:, t % RING, 0:nk, c], dram).then_inc(
                            weight_landed[t % RING], 16)
                steps(sp, plan, ph, 0, False, tile, from_round=int(ph.t0 == 0))

            for ph in phases:
                load(ph)
                if ph.name == "gate1":
                    sp.wait_ge(ATT["dsa"]["lo"], 2)
                    sp.dma_start(area(4096, NT, D), x[0].rearrange("(t p) d -> p t d", p=P)).then_inc(again_in, 16)
                if ph.name == "up2":
                    sp.dma_start(w_decay[0:DECAY_RANK, :], gla_w_gk2).then_inc(decay_in, 16)
                    sp.dma_start(w_decay[DECAY_RANK:DECAY_RANK + 1, :],
                                 gla_b_gk.rearrange("(a n) -> a n", a=1)).then_inc(decay_in, 16)
            for t in range(NT):
                sp.wait_ge(orows, 4 * (t + 1))
                sp.dma_start(out[0, t * P:(t + 1) * P, :], rows_out[:, t, :]).then_inc(stored, 16)
            sp.wait_ge(stored, 16 * NT)

        @block.gpsimd
        def _(pool):
            own = [0]

            def link(ins):
                own[0] += 1
                ins.then_inc(pool_own, 1)
                pool.wait_ge(pool_own, own[0])

            pool.dma_start(pos_i[:, 0:NT], positions.rearrange("a (t p) -> p (a t)", p=P),
                           allow_slow_non_contiguous=True).then_inc(small_in, 16)
            pool.dma_start(pos_i[:, NT:2 * NT], positions_2.rearrange("a (t p) -> p (a t)", p=P),
                           allow_slow_non_contiguous=True).then_inc(small_in, 16)
            pool.dma_start(inv[:, 0:64], inv64.partition_broadcast(P)).then_inc(small_in, 16)
            pool.dma_start(inv[:, 64:96], inv32.partition_broadcast(P)).then_inc(small_in, 16)
            pool.dma_start(qk_gain[:, 0, :], dsa_q_norm[0].partition_broadcast(P)).then_inc(small_in, 16)
            pool.dma_start(qk_gain[:, 1, :], dsa_k_norm[0].partition_broadcast(P)).then_inc(small_in, 16)
            link(nc.gpsimd.memset(ident[:], 0.0))
            nc.gpsimd.affine_select(out=ident[:], in_=ident[:], compare_op=ALU.not_equal, fill=1.0,
                                    base=0, pattern=[[-1, P]], channel_multiplier=1).then_inc(consts, 1)
            nc.gpsimd.memset(ones[:], 1.0).then_inc(consts, 1)
            link(nc.gpsimd.memset(tri_ge[:], 1.0))
            nc.gpsimd.affine_select(out=tri_ge[:], in_=tri_ge[:], compare_op=ALU.is_ge, fill=0.0,
                                    base=0, pattern=[[-1, P]], channel_multiplier=1).then_inc(consts, 1)
            link(nc.gpsimd.memset(tri_chunk[:], 1.0 / GTAU))
            link(nc.gpsimd.affine_select(out=tri_chunk[:], in_=tri_chunk[:], compare_op=ALU.is_ge,
                                         fill=0.0, base=0, pattern=[[1, P]], channel_multiplier=-1))
            nc.gpsimd.memset(tri_chunk[0:CH, CH:P], 0.0).then_inc(consts, 1)

            def diagonal(v, base, fill, signal):
                for c in (0, 2 * P):
                    b = v[:, :, c:c + P]
                    nc.gpsimd.affine_select(out=b, in_=b, compare_op=ALU.is_ge, fill=fill,
                                            base=base, pattern=[[0, 4], [1, P]],
                                            channel_multiplier=-1).then_inc(signal, 1)

            for g in range(2):
                pool.wait_ge(SB["sp"], g + 1)
                diagonal(sb_sp, -1, 0.0, SB["spm"])
                pool.wait_ge(SB["u"], g + 1)
                diagonal(sb_z, -1, HIDDEN, SB["um"])
            pool.wait_ge(GL["a"], 1)
            diagonal(g_a, 0, 0.0, GL["am"])
            link(nc.gpsimd.memset(causal, 0.0))
            for c in (0, 2 * P):
                nc.gpsimd.affine_select(out=causal[:, c:c + P], in_=causal[:, c:c + P],
                                        compare_op=ALU.is_ge, fill=HIDDEN, base=0,
                                        pattern=[[-1, P]], channel_multiplier=1).then_inc(consts, 1)

        @block.tensor
        def _(pe):
            def project(ph, x_hi, x_lo, side=None, x_wait=None):
                def tile(j, i):
                    t = ph.t0 + j
                    kt, jb = j % ph.bt, j // ph.bt
                    b = ph.b0 + jb
                    nb = ph.period // ph.bt
                    pe.wait_ge(lo_made, i * ph.period + (t + 1))
                    if kt == 0:
                        if not isinstance(i, int) or b + i * nb >= PSUM_RING:
                            pe.wait_ge(block_out, i * nb + (b - PSUM_RING + 1))
                    if isinstance(i, int) and i * nb + jb == 0 and x_wait is not None:
                        x_wait(kt)
                    nk = ph.ktiles[kt]
                    hi, lo = weight_hi[:, t % RING], weight_lo[:, t % RING]
                    for c in range(2):
                        tok = slice(c * P, c * P + P)
                        if ph.kind == "fm":
                            o = blk[:, b % PSUM_RING, c, 0:S]
                            ops = [(w[:, k, c * P:c * P + P], v[:, TK * kt + k, :])
                                   for k in range(nk) for w, v in ((hi, x_hi), (hi, x_lo), (lo, x_hi))]
                            groups = [(o, ops)]
                        elif ph.kind == "tm":
                            o = blk[:, b % PSUM_RING, c, 0:ph.cols]
                            ops = [(v[:, TK * kt + k, tok], w[:, k, 0:ph.cols])
                                   for k in range(nk) for w, v in ((hi, x_hi), (lo, x_hi), (hi, x_lo))]
                            groups = [(o, ops)]
                        elif c == 0:
                            groups = [(blk[:, b % PSUM_RING, 0, 0:S],
                                       [(w[:, k, 0:P], v[:, k, :])
                                        for k in range(nk) for w, v in ((hi, x_hi), (hi, x_lo), (lo, x_hi))])]
                        else:
                            groups = [(blk[:, b % PSUM_RING, 1, q * P:q * P + P],
                                       [(v[:, k, q * P:q * P + P], w[:, k, P:2 * P])
                                        for k in range(nk) for w, v in ((hi, x_hi), (lo, x_hi), (hi, x_lo))])
                                      for q in range(NT)]
                        for o, ops in groups:
                            for m, (lhsT, rhs) in enumerate(ops):
                                mm = nc.tensor.matmul(o, lhsT, rhs, start=(kt == 0 and m == 0),
                                                      stop=(kt == ph.bt - 1 and m == len(ops) - 1))
                    mm.then_inc(tile_used, 1)
                    if side is not None:
                        side(j + i * ph.period)
                steps(pe, plan, ph, 0, side is not None, tile,
                      from_round=int(ph.t0 == 0 or x_wait is not None))

            def turn_rows(rows, r, done):
                if done + r >= 2:
                    pe.wait_ge(turned_out, done + r - 1)
                for c in range(4):
                    for t in range(NT):
                        mm = nc.tensor.transpose(
                            pa[:, 2 * (r % 2) + c // 2, (c % 2) * S + t * P:(c % 2) * S + (t + 1) * P],
                            rows[:, t, (4 * r + c) * P:(4 * r + c + 1) * P], ident[:])
                mm.then_inc(turned, 1)

            def norm_sum(n, sq, chunks):
                q = chunks // 4
                for c in range(chunks):
                    if c % q == 0:
                        norm_at(pe, n, "sq", c // q + 1)
                    mm = nc.tensor.matmul(pa[:, 0, 0:S], ones[:], sq[:, c, :], start=(c == 0),
                                          stop=(c == chunks - 1))
                mm.then_inc(NORM["sum"], 1)

            def norm_ready(n):
                def wait(kt):
                    norm_at(pe, n, "done", kt + 1)
                return wait

            def turn_heads(src, signal, width=P):
                for c in range(KW):
                    for t in range(NT):
                        mm = nc.tensor.transpose(
                            pa[:, c // 2, (c % 2) * S + t * P:(c % 2) * S + (t + 1) * P],
                            src[:, t, c * P:(c + 1) * P], ident[:])
                mm.then_inc(signal, 1)

            def causal_pv(probs_T, values, heads, signal):
                for h in range(4):
                    v = slice((heads + h) * P, (heads + h + 1) * P)
                    nc.tensor.matmul(pa[:, h, 0:S], values[:, 0, v], probs_T[:, h, 0:S],
                                     start=True, stop=False)
                    mm = nc.tensor.matmul(pa[:, h, P:S], values[:, 1, v], probs_T[:, h, S:TRI],
                                          start=False, stop=True)
                mm.then_inc(signal, 1)

            def causal_turn(p, signal):
                for h in range(4):
                    for c in range(3):
                        mm = nc.tensor.transpose(pa[:, h, c * P:(c + 1) * P], p[:, h, c * P:(c + 1) * P],
                                                 ident[:])
                mm.then_inc(signal, 1)

            pe.wait_ge(consts, 4)
            pe.wait_ge(vec_in, 16 * N_VEC_DMAS)
            at = 0
            for g, names in enumerate(STAGES):
                n = sum(ROWS[v][1] for v in names)
                mm = nc.tensor.transpose(pa[:, g // 4, (g % 4) * P:(g % 4) * P + n], stage[0:n, g, :],
                                         ident[0:n, 0:n])
            mm.then_inc(vec_turned, 1)
            pe.wait_ge(vec_ready, 1)
            pe.wait_ge(mem_in, 16)
            for r in range(4):
                turn_rows(rows_mem, r, 0)
            norm_sum("mem", squares, KD)

            def side_x(j):
                if j < 4:
                    if j == 0:
                        pe.wait_ge(x_in, 16)
                        norm_at(pe, "mem", "inv", 1)
                    turn_rows(rows_x, j, 4)
                if j == 6:
                    norm_sum("x", squares, KD)
            project(PH["memk"], u_hi, u_lo, side=side_x, x_wait=norm_ready("mem"))

            def side_memk(j):
                if j == 7:
                    norm_at(pe, "memk", "scaled", 2)
                    turn_heads(mem_k.rearrange("p t h d -> p t (h d)"), HEADN["turned"])
            project(PH["memv"], u_hi, u_lo, side=side_memk)
            project(PH["qm"], h_hi, h_lo, x_wait=norm_ready("x"))

            def side_mem(j):
                if j == 5:
                    norm_at(pe, "memk", "out", 2)
                    norm_at(pe, "memq", "scaled", 2)
                    turn_heads(mem_q.rearrange("p t h d -> p t (h d)"), HEADN["turned"])
                if j == 8:
                    norm_at(pe, "memq", "out", 2)
                    for h in range(MH):
                        for t in range(NT):
                            for c in range(2):
                                mm = nc.tensor.matmul(pa[:, h, t * S:(t + 1) * S],
                                                      mem_qT[:, 2 * h + c, t * P:(t + 1) * P],
                                                      mem_kT[:, 2 * h + c, :], start=(c == 0), stop=(c == 1))
                    mm.then_inc(ATT["mem"]["scores"], 1)
                if j == 16:
                    pe.wait_ge(ATT["mem"]["probs"], 1)
                    for h in range(MH):
                        for k in range(2):
                            for t in range(NT):
                                mm = nc.tensor.transpose(pa[:, h, k * S + t * P:k * S + (t + 1) * P],
                                                         mem_p[:, h, t * S + k * P:t * S + (k + 1) * P],
                                                         ident[:])
                    mm.then_inc(ATT["mem"]["turned"], 1)
                if j == 19:
                    pe.wait_ge(ATT["mem"]["probsT"], 1)
                    for h in range(MH):
                        for v in range(2):
                            for k in range(2):
                                mm = nc.tensor.matmul(pa[:, h, v * S:(v + 1) * S],
                                                      mem_v[:, k, h, v * P:(v + 1) * P],
                                                      mem_pT[:, h, k * S:(k + 1) * S],
                                                      start=(k == 0), stop=(k == 1))
                    mm.then_inc(ATT["mem"]["pv"], 1)
            project(PH["gate2"], h_hi, h_lo, side=side_mem)

            def out_ready(signal, n):
                def wait(kt):
                    if kt == 0:
                        pe.wait_ge(signal, n)
                return wait
            project(PH["branch2"], u_hi, u_lo, x_wait=out_ready(ATT["mem"]["lo"], 1))
            project(PH["sbqk"], h_hi, h_lo)
            project(PH["sbv"], h_hi, h_lo)

            def side_sb(j):
                g, s = (0, j) if j < 12 else (1, j - 12)
                if s == 0:
                    pe.wait_ge(block_out, PH["gate0"].b0)
                    if g == 0:
                        pe.wait_ge(ATT["mem"]["lo"], 1)
                    else:
                        pe.wait_ge(SB["lo"], g)
                    for h in range(4):
                        c = 4 * g + h
                        nc.tensor.matmul(pa[:, h, 0:S], qkT[:, KW + c, 0:P], qkT[:, c, :],
                                         start=True, stop=True)
                        mm = nc.tensor.matmul(pa[:, h, S:TRI], qkT[:, KW + c, P:S], qkT[:, c, P:S],
                                              start=True, stop=True)
                    mm.then_inc(SB["z"], 1)
                if s == 6:
                    pe.wait_ge(SB["spm"], 2 * (g + 1))
                    pe.wait_ge(SB["zs"], g + 1)
                    for h in range(4):
                        nc.tensor.matmul(pa[:, h, 0:S], tri_ge[:], sb_sp[:, h, 0:S], start=True, stop=False)
                        nc.tensor.matmul(pa[:, h, P:S], ones[:], sb_sp[:, h, S:TRI], start=False, stop=True)
                        mm = nc.tensor.matmul(pa[:, h, S:TRI], tri_ge[:], sb_sp[:, h, S:TRI],
                                              start=True, stop=True)
                    mm.then_inc(SB["cum"], 1)
                if s == 10:
                    pe.wait_ge(SB["a"], g + 1)
                    causal_pv(sb_l, val, 4 * g, SB["pv"])
            project(PH["gate0"], h_hi, h_lo, side=side_sb)
            project(PH["branch0"], u_hi, u_lo, x_wait=out_ready(SB["lo"], 2))
            project(PH["qi"], h_hi, h_lo)
            project(PH["kiwi"], h_hi, h_lo)

            def index_logits(t):
                keys = P * (t + 1)
                for h in range(IH):
                    o = pa[:, h // 4, (h % 4) * P:(h % 4 + 1) * P] if t == 0 else \
                        pa[:, h // 2, (h % 2) * S:(h % 2 + 1) * S]
                    mm = nc.tensor.matmul(o, qiT[0:ID, h, t * P:(t + 1) * P], kiT[0:ID, 0:keys],
                                          start=True, stop=True)
                mm.then_inc(IX["logits"], 1)

            def side_index(j):
                if j == 4:
                    pe.wait_ge(IX["roped"], 1)
                    pe.wait_ge(SB["lo"], 2)
                    for h in range(IH):
                        for t in range(NT):
                            mm = nc.tensor.transpose(
                                pa[0:ID, h // 2, (h % 2) * S + t * P:(h % 2) * S + (t + 1) * P],
                                qi[:, t, h * ID:(h + 1) * ID], ident[:])
                    mm.then_inc(IX["turned"], 1)
                if j == 6:
                    pe.wait_ge(IX["qT"], 1)
                    for t in range(NT):
                        mm = nc.tensor.transpose(pa[0:ID, 0, t * P:(t + 1) * P], ki_wi[:, t, 0:ID], ident[:])
                    mm.then_inc(IX["kturned"], 1)
                if j == 8:
                    pe.wait_ge(IX["kT"], 1)
                    index_logits(0)
                if j == 11:
                    pe.wait_ge(IX["relu"], 1)
                    index_logits(1)
            project(PH["qb"], h_hi, h_lo, side=side_index)

            def side_dsaq(j):
                if j == 14:
                    pe.wait_ge(IX["relu"], 2)
                    norm_at(pe, "dsaq", "scaled", 1)
                    turn_heads(val, HEADN["turned"])
            project(PH["kb"], h_hi, h_lo, side=side_dsaq)

            def side_dsak(j):
                if j == 14:
                    norm_at(pe, "dsaq", "out", 1)
                    norm_at(pe, "dsak", "scaled", 1)
                    turn_heads(kb_rows, HEADN["turned"])
            project(PH["vb"], h_hi, h_lo, side=side_dsak)

            def causal_attention(a, g, s, first_free, score_ops, probs_, probsT_, values, v0):
                if s == 0:
                    pe.wait_ge(*first_free)
                    for h in range(4):
                        for t, (q, k, o) in enumerate(((slice(0, P), slice(0, P), slice(0, P)),
                                                       (slice(P, S), slice(0, S), slice(P, TRI)))):
                            ops = score_ops(h, q, k)
                            for m, (lhsT, rhs) in enumerate(ops):
                                mm = nc.tensor.matmul(pa[:, h, o], lhsT, rhs, start=(m == 0),
                                                      stop=(m == len(ops) - 1))
                    mm.then_inc(ATT[a]["scores"], 1)
                if s == 1:
                    pe.wait_ge(ATT[a]["probs"], g + 1)
                    causal_turn(probs_, ATT[a]["turned"])
                if s == 2:
                    pe.wait_ge(ATT[a]["probsT"], g + 1)
                    causal_pv(probsT_, values, v0, ATT[a]["pv"])

            def side_dsa(j):
                g, s = (0, j) if j < 13 else (1, j - 13)
                part = {1: 0, 9: 1, 11: 2}.get(s)
                if part is None or j >= 26:
                    return
                if j == 1:
                    pe.wait_ge(block_out, PH["gate1"].b0)
                causal_attention("dsa", g, part,
                                 (HEADN["out"], base["dsak"]["out"] + 1) if g == 0 else (ATT["dsa"]["lo"], g),
                                 lambda h, q, k: [(qkT[:, 4 * g + h, q], qkT[:, KW + 4 * g + h, k])],
                                 probs, probsT, val, 4 * g)
            project(PH["gate1"], h_hi, h_lo, side=side_dsa)
            project(PH["branch1"], u_hi, u_lo, x_wait=out_ready(ATT["dsa"]["lo"], 2))
            pe.wait_ge(again_in, 16)
            for r in range(4):
                turn_rows(area(4096, NT, D), r, 8)

            def merged_wait(kt):
                pe.wait_ge(merged_ready, kt + 1)
            project(PH["wout"], h_hi, h_lo, x_wait=merged_wait)

            norm_sum("ffn", squares, KD)
            for f in range(3):
                first = norm_ready("ffn") if f == 0 else None
                project(PH[f"up{f}"], h_hi, h_lo, x_wait=first)

                def ff_wait(kt, f=f):
                    pe.wait_ge(ff_ready, min(FFN[f][0] + TK * (kt + 1), FFN[f][0] + FFN[f][1]))
                project(PH[f"down{f}"], u_hi, u_lo, x_wait=ff_wait)

            norm_sum("pre0", squares, KD)
            project(PH["decay"], h_hi, h_lo, x_wait=norm_ready("pre0"))
            project(PH["glaqk"], h_hi, h_lo)

            def side_decay(j):
                if j == 0:
                    pe.wait_ge(block_out, PH["glaqk"].b0)
                    for t in range(NT):
                        mm = nc.tensor.transpose(pa[0:DECAY_RANK, 0, t * P:(t + 1) * P], low_rows[:, t, :],
                                                 ident[:])
                    mm.then_inc(GL["low"], 1)
                if j == 1:
                    pe.wait_ge(GL["lowT"], 1)
                    pe.wait_ge(decay_in, 32)
                    for t in range(NT):
                        for c in range(2):
                            mm = nc.tensor.matmul(pa[:, 2 * t + c, :], lowT[0:DECAY_RANK + 1, t * P:(t + 1) * P],
                                                  w_decay[0:DECAY_RANK + 1, c * 512:(c + 1) * 512],
                                                  start=True, stop=True)
                    mm.then_inc(GL["gk"], 1)
                if j == 7:
                    pe.wait_ge(GL["la"], 1)
                    for c in range(2 * GH):
                        for t in range(NT):
                            mm = nc.tensor.matmul(
                                pa[:, c // 2, (c % 2) * S + t * P:(c % 2) * S + (t + 1) * P],
                                g_la[:, t, c * P:(c + 1) * P], tri_chunk[:], start=True, stop=True)
                    mm.then_inc(GL["cum"], 1)
            project(PH["glav"], h_hi, h_lo, side=side_decay)

            def side_gla(j):
                if j in (0, 2, 4, 6):
                    n = j // 2
                    if n == 0:
                        pe.wait_ge(GL["kl"], 1)
                    else:
                        pe.wait_ge(GL["step"], n)
                    for h in range(GH):
                        for t in range(n // 2 + 1):
                            at = n * CH if t == 0 else S + (n - 2) * CH
                            for c in range(2):
                                mm = nc.tensor.matmul(pa[:, h, at:at + CH],
                                                      g_ke[:, 2 * h + c, t * P:(t + 1) * P],
                                                      g_q[:, 2 * h + c, n * CH:(n + 1) * CH],
                                                      start=(c == 0), stop=(c == 1))
                    mm.then_inc(GL["rows"], 1)
                if j in (10, 13):
                    r = (j - 10) // 3
                    if r == 0:
                        pe.wait_ge(GL["am"], 2)
                        pe.wait_ge(block_out, PH["glagate"].b0)
                    else:
                        pe.wait_ge(GL["oout"], r)
                    for c in range(2 * 4):
                        h, o = 2 * r + c // 4, pa[:, c // 2, (c % 2) * S:(c % 2 + 1) * S]
                        v = slice((8 * r + c) * P, (8 * r + c + 1) * P)
                        nc.tensor.matmul(o, g_v[:, 0, v], g_a[:, h, 0:S], start=True, stop=False)
                        mm = nc.tensor.matmul(pa[:, c // 2, (c % 2) * S + P:(c % 2 + 1) * S], g_v[:, 1, v],
                                              g_a[:, h, S:TRI], start=False, stop=True)
                    mm.then_inc(GL["o"], 1)
                if j == 18:
                    pe.wait_ge(GL["sq"], 1)
                    for c in range(KD):
                        h = c // 4
                        mm = nc.tensor.matmul(pa[:, h // 2, (h % 2) * S:(h % 2 + 1) * S], ones[:],
                                              squares[:, c, :], start=(c % 4 == 0), stop=(c % 4 == 3))
                    mm.then_inc(GL["sum"], 1)
            project(PH["glagate"], h_hi, h_lo, side=side_gla)

            def gla_ready(kt):
                pe.wait_ge(GL["ready"], kt + 1)
            project(PH["glaout"], u_hi, u_lo, x_wait=gla_ready)

            norm_sum("post0", squares, KD)
            norm_sum("pre1", squares, KD)
            project(PH["latent"], h_hi, h_lo, x_wait=norm_ready("pre1"))
            project(PH["krope"], h_hi, h_lo)
            norm_sum("qa", latent_sq[:, 0:KL, :], KL)
            norm_at(pe, "qa", "inv", 1)
            norm_sum("kva", latent_sq[:, KL:2 * KL, :], KL)
            project(PH["qrope"], u_hi, u_lo, x_wait=lambda kt: norm_at(pe, "qa", "done", 4))
            pe.wait_ge(ML["k_roped"], 1)
            norm_at(pe, "kva", "inv", 1)
            for t in range(NT):
                mm = nc.tensor.transpose(pa[:, 0, t * P:(t + 1) * P], k_rope[:, t, :], ident[:])
            mm.then_inc(ML["kturned"], 1)

            def turn_q():
                pe.wait_ge(ML["q_roped"], 1)
                pe.wait_ge(ML["kT"], 1)
                turn_heads(q_rope, ML["qturned"])

            for r in range(2):
                project(PH[f"qnope{r}"], u_hi, u_lo)
                if r == 0:
                    norm_at(pe, "kva", "done", 4)
                project(PH[f"kv{r}"], u_hi[:, KL:2 * KL], u_lo[:, KL:2 * KL])
                if r == 0:
                    turn_q()

                def side_mla(j, r=r):
                    g, s = (0, j) if j < 8 else (1, j - 8)
                    part = {0: 0, 5: 1, 7: 2}.get(s)
                    if part is None:
                        return
                    if j == 0:
                        pe.wait_ge(block_out, PH[f"mlagate{r}"].b0)
                    if j == 0 and r == 0:
                        free = (ML["qT"], 1)
                    else:
                        free = (ML["out"], 2 * r + g)

                    def ops(h, q, k):
                        c = 4 * g + h
                        half = slice(0, LR) if h % 2 == 0 else slice(LR, 2 * LR)
                        return [(q_nope[:, c, q], k_nope[:, c, k]),
                                (q_ropeT[half, 4 * r + c // 2, q], k_ropeT[half, k])]
                    causal_attention("mla", 2 * r + g, part, free, ops, lprobs, lprobsT, l_v, 4 * g)
                project(PH[f"mlagate{r}"], h_hi, h_lo, side=side_mla)

            def mla_ready(kt):
                pe.wait_ge(ML["ready"], kt + 1)
            project(PH["mlaout"], u_hi, u_lo, x_wait=mla_ready)
            norm_sum("post1", squares, KD)
            for t in range(NT):
                for r in range(4):
                    if t == 0:
                        norm_at(pe, "post1", "done", r + 1)
                    if 4 * t + r >= 2:
                        pe.wait_ge(orows, 4 * t + r - 1)
                    for c in range(4):
                        mm = nc.tensor.transpose(pa[:, 2 + r % 2, c * P:(c + 1) * P],
                                                 xT[:, 4 * r + c, t * P:(t + 1) * P], ident[:])
                    mm.then_inc(oturned, 1)

        @block.scalar
        def _(act):
            own = [0]

            def link(ins):
                own[0] += 1
                ins.then_inc(act_own, 1)
                act.wait_ge(act_own, own[0])

            def split_hi(t, period, i):
                nk, cols, _ = plan.shape[t + i * period if isinstance(i, int) else t]
                r = t % RING
                act.wait_ge(weight_landed[r], plan.landed_at(t, period, i))
                nc.scalar.activation(weight_hi[:, r, 0:nk, 0:cols], weight_raw[:, r, 0:nk, 0:cols],
                                     ACT.Copy).then_inc(hi_made, 1)

            def project(ph, out_of_psum=None, side=None, inc=1, mid=None):
                if out_of_psum is not None and inc:
                    act.wait_ge(block_out, ph.b0)

                def tile(j, i):
                    t = ph.t0 + j
                    act.wait_ge(tile_used, i * ph.period + (t + 1))
                    if not isinstance(i, int) or t + i * ph.period + RING < plan.tiles:
                        split_hi(t + RING, ph.period, i)
                    if j % ph.bt == ph.bt - 1 and out_of_psum is not None:
                        b = i * (ph.period // ph.bt) + j // ph.bt
                        ins = out_of_psum(b, (ph.b0 + j // ph.bt) % PSUM_RING)
                        if inc:
                            ins.then_inc(block_out, 1)
                    if mid is not None:
                        mid(j, i)
                    if side is not None:
                        side(j + i * ph.period)
                steps(act, plan, ph, RING, side is not None, tile, from_round=int(mid is not None))

            def rows_to(dst, cols=TC):
                def go(b, r):
                    return nc.scalar.activation(dst[:, :, bass.ds(b * cols, cols)], blk[:, r, :, 0:cols], ACT.Copy)
                return go

            def chunks_to(dst):
                def go(b, r):
                    return nc.scalar.activation(dst[:, bass.ds(b * 2, 2), :], blk[:, r, :, 0:S], ACT.Copy)
                return go

            def gate_tanh(g):
                def go(b, r):
                    for c in range(2):
                        ins = nc.scalar.activation(gates[:, bass.ds(b * 2 + c, 1), :], blk[:, r, c:c + 1, 0:S],
                                                   ACT.Tanh, bias=col("b_gate", b * 2 + (g * KD + c)), scale=0.5)
                    return ins
                return go

            def silu_to(dst):
                def go(b, r):
                    return nc.scalar.activation(dst[:, bass.ds(b * 2, 2), :], blk[:, r, :, 0:S], ACT.Silu)
                return go

            def turned_rows_out(r, done, dst):
                act.wait_ge(turned, done + r + 1)
                nc.scalar.activation(dst[:, 4 * r:4 * r + 4, :].rearrange("p (b c) s -> p b (c s)", b=2),
                                     pa[:, 2 * (r % 2):2 * (r % 2) + 2, :], ACT.Copy).then_inc(turned_out, 1)

            def norm(n, s, src, sq, chunks, x_hi=None):
                q = chunks // 4
                if s == 0:
                    for k in range(4):
                        nc.scalar.activation(sq[:, k * q:(k + 1) * q, :], src[:, k * q:(k + 1) * q, :],
                                             ACT.Square).then_inc(NORM["sq"], 1)
                elif s == 1:
                    norm_at(act, n, "inv", 1)
                    nc.scalar.activation(rstd[:], rstd[:], ACT.Sqrt).then_inc(NORM["rstd"], 1)
                elif x_hi is not None:
                    k = s - 2
                    norm_at(act, n, "hn", (k + 1) * q)
                    nc.scalar.activation(x_hi[:, k * q:(k + 1) * q, :], sq[:, k * q:(k + 1) * q, :],
                                         ACT.Copy).then_inc(NORM["hi"], 1)

            def head_norm(n, s, src, sq, at, heads):
                if s == 0:
                    nc.scalar.activation(sq, src, ACT.Square).then_inc(HEADN["sq"], 1)
                else:
                    norm_at(act, n, "inv", 1)
                    nc.scalar.activation(small[:, at:at + NT * heads], small[:, at:at + NT * heads],
                                         ACT.Sqrt).then_inc(HEADN["rstd"], 1)

            def mem_turned_out(n, gain, dst):
                norm_at(act, n, "turned", 1)
                for c in range(2):
                    nc.scalar.activation(dst[:, c:KW:2, :], pa[:, :, c * S:(c + 1) * S], ACT.Copy,
                                         scale=col(gain, c)).then_inc(HEADN["out"], 1)

            def heads_turned_out(signal, value, done, dst):
                act.wait_ge(signal, value)
                nc.scalar.activation(dst.rearrange("p (b c) s -> p b (c s)", b=4), pa[:, :, :],
                                     ACT.Copy).then_inc(done, 1)

            for t in range(RING):
                split_hi(t, 1, 0)
            act.wait_ge(vec_turned, 1)
            nc.scalar.activation(vec[:, 0:P * 2 - 80], pa[:, 0, 0:P * 2 - 80], ACT.Copy).then_inc(act_own, 1)
            nc.scalar.activation(vec[:, 176:176 + 2 * KF], pa[:, 0, 2 * P:2 * P + 2 * KF], ACT.Copy).then_inc(act_own, 1)
            nc.scalar.activation(vec[:, 176 + 2 * KF:176 + 4 * KF], pa[:, 0, 3 * P:3 * P + 2 * KF], ACT.Copy).then_inc(act_own, 1)
            own[0] += 3
            link(nc.scalar.activation(vec[:, 176 + 4 * KF:176 + 8 * KF].rearrange("p (a b) -> p a b", a=2),
                                      pa[:, 1, 0:2 * P].rearrange("p (a b) -> p a b", a=2)[:, :, 0:2 * KF],
                                      ACT.Copy))
            nc.scalar.activation(col("b_gate", 0, 3 * KD), col("b_gate", 0, 3 * KD), ACT.Copy,
                                 scale=0.5).then_inc(vec_ready, 1)
            for r in range(4):
                turned_rows_out(r, 0, memT)
            act.wait_ge(turned_out, 4)
            norm("mem", 0, memT, squares, KD)
            norm("mem", 1, memT, squares, KD)
            for k in range(4):
                norm("mem", 2 + k, memT, squares, KD, u_hi)

            act.wait_ge(angles, 1)
            nc.scalar.activation(sin[:], angle, ACT.Sin).then_inc(sines, 1)
            nc.scalar.activation(cos[:], angle, ACT.Sin, scale=0.5).then_inc(sines, 1)

            def side_x(j):
                if j < 4:
                    turned_rows_out(j, 4, xT)
                if j == 4:
                    act.wait_ge(turned_out, 8)
                    norm_at(act, "mem", "done", 4)
                    norm("x", 0, xT, squares, KD)
                if j == 7:
                    norm("x", 1, xT, squares, KD)
                if 9 <= j < 13:
                    norm("x", 2 + j - 9, xT, squares, KD, h_hi)
            project(PH["memk"], rows_to(mem_k.rearrange("p t h d -> p t (h d)")), side=side_x)

            def side_memk(j):
                if j == 1:
                    act.wait_ge(block_out, PH["memv"].b0)
                    norm_at(act, "x", "done", 4)
                    head_norm("memk", 0, mem_k, mem_sq, 0, MH)
                if j == 3:
                    head_norm("memk", 1, mem_k, mem_sq, 0, MH)
                if j == 8:
                    mem_turned_out("memk", "mem_k_norm", mem_kT)
            project(PH["memv"], rows_to(mem_v.rearrange("p t h d -> p t (h d)")), side=side_memk)
            project(PH["qm"], rows_to(mem_q.rearrange("p t h d -> p t (h d)")))

            def split_out(a, g, n):
                act.wait_ge(a["pv"], g + 1)
                if n == 8:
                    nc.scalar.activation(u_hi[:, 0:KW, :].rearrange("p (b c) s -> p b (c s)", b=4), pa[:, :, :],
                                         ACT.Copy).then_inc(a["hi"], 1)
                else:
                    nc.scalar.activation(u_hi[:, 4 * g:4 * g + 4, :], pa[:, :, 0:S],
                                         ACT.Copy).then_inc(a["hi"], 1)

            def exps(a, g, src, dst, scale, cols):
                act.wait_ge(ATT[a]["masked"], g + 1)
                for h in range(4):
                    for t, c in enumerate(cols):
                        nc.scalar.activation(dst[:, h, c], src[:, h, c], ACT.Exp,
                                             bias=small[:, 32 + 4 * t + h:33 + 4 * t + h], scale=scale,
                                             accum_out=small[:, 40 + 4 * t + h:41 + 4 * t + h]).then_inc(
                                                 ATT[a]["exp"], 1)

            def probs_turned_out(a, g, dst, width):
                act.wait_ge(ATT[a]["turned"], g + 1)
                nc.scalar.activation(dst, pa[:, :, 0:width], ACT.Copy).then_inc(ATT[a]["probsT"], 1)

            def side_mem(j):
                if j == 1:
                    act.wait_ge(block_out, PH["gate2"].b0)
                    norm_at(act, "memk", "scaled", 2)
                    head_norm("memq", 0, mem_q, mem_sq, 8, MH)
                if j == 3:
                    head_norm("memq", 1, mem_q, mem_sq, 8, MH)
                if j == 6:
                    mem_turned_out("memq", "mem_q_norm", mem_qT)
                if j == 11:
                    exps("mem", 0, pa, mem_p, MD ** -0.5, (slice(0, S), slice(S, 2 * S)))
                if j == 17:
                    probs_turned_out("mem", 0, mem_pT, 512)
                if j == 20:
                    split_out(ATT["mem"], 0, 8)
            project(PH["gate2"], gate_tanh(2), side=side_mem)
            project(PH["branch2"])
            project(PH["sbqk"], chunks_to(qkT))
            project(PH["sbv"], rows_to(val))

            def side_sb(j):
                g, s = (0, j) if j < 12 else (1, j - 12)
                if j >= 24:
                    return
                if s == 1:
                    act.wait_ge(SB["z"], g + 1)
                    nc.scalar.activation(sb_l, pa[:, :, 0:TRI], ACT.Abs, scale=HD ** -0.5).then_inc(SB["abs"], 1)
                if s == 2:
                    act.wait_ge(SB["abs"], g + 1)
                    link(nc.scalar.activation(sb_l, sb_l, ACT.Exp, scale=-1.0))
                    nc.scalar.activation(sb_l, sb_l, ACT.Ln, bias=1.0).then_inc(SB["ln"], 1)
                if s == 8:
                    act.wait_ge(SB["um"], 2 * (g + 1))
                    nc.scalar.activation(sb_l, sb_z, ACT.Exp).then_inc(SB["a"], 1)
                if s == 11:
                    split_out(SB, g, 4)
            project(PH["gate0"], gate_tanh(0), side=side_sb)
            project(PH["branch0"])
            project(PH["qi"], rows_to(qi))
            project(PH["kiwi"], rows_to(ki_wi, ID + IH))

            def side_index(j):
                if j == 5:
                    act.wait_ge(IX["turned"], 1)
                    nc.scalar.activation(qiT[0:ID].rearrange("p (b c) s -> p b (c s)", b=4), pa[0:ID, :, :],
                                         ACT.Copy).then_inc(IX["qT"], 1)
                if j == 7:
                    act.wait_ge(IX["kturned"], 1)
                    nc.scalar.activation(kiT[0:ID, :], pa[0:ID, 0, 0:S], ACT.Copy).then_inc(IX["kT"], 1)
                if j == 9:
                    act.wait_ge(IX["logits"], 1)
                    nc.scalar.activation(logits[:, 0:IH * P].rearrange("p (b c) -> p b c", b=2), pa[:, 0:2, :],
                                         ACT.Relu, scale=ID ** -0.5).then_inc(IX["relu"], 1)
                if j == 12:
                    act.wait_ge(IX["logits"], 2)
                    act.wait_ge(IX["score"], 1)
                    nc.scalar.activation(logits.rearrange("p (b c) -> p b c", b=4), pa[:, :, :],
                                         ACT.Relu, scale=ID ** -0.5).then_inc(IX["relu"], 1)
            project(PH["qb"], rows_to(val), side=side_index)

            def heads(v):
                return v.rearrange("p t (h d) -> p t h d", d=HD)

            def side_dsaq(j):
                if j == 1:
                    act.wait_ge(block_out, PH["kb"].b0)
                    act.wait_ge(IX["score"], 2)
                    head_norm("dsaq", 0, heads(val), heads(dsa_sq), 64, HEADS)
                if j == 3:
                    head_norm("dsaq", 1, None, None, 64, HEADS)
                if j == 15:
                    heads_turned_out(HEADN["turned"], base["dsaq"]["turned"] + 1, HEADN["out"], qkT[:, 0:KW, :])
            project(PH["kb"], rows_to(kb_rows), side=side_dsaq)

            def side_dsak(j):
                if j == 1:
                    act.wait_ge(block_out, PH["vb"].b0)
                    norm_at(act, "dsaq", "scaled", 1)
                    head_norm("dsak", 0, heads(kb_rows), heads(dsa_sq), 80, HEADS)
                if j == 3:
                    head_norm("dsak", 1, None, None, 80, HEADS)
                if j == 15:
                    heads_turned_out(HEADN["turned"], base["dsak"]["turned"] + 1, HEADN["out"], qkT[:, KW:2 * KW, :])
            project(PH["vb"], rows_to(val), side=side_dsak)

            def causal_attention(a, g, s, p, pT):
                if s == 0:
                    exps(a, g, p, p, 1.0, (slice(0, P), slice(P, TRI)))
                if s == 1:
                    probs_turned_out(a, g, pT, TRI)

            def side_dsa(j):
                g, s = (0, j) if j < 13 else (1, j - 13)
                if j >= 26:
                    return
                if s == 5:
                    causal_attention("dsa", g, 0, probs, probsT)
                if s == 10:
                    causal_attention("dsa", g, 1, probs, probsT)
                if s == 12:
                    split_out(ATT["dsa"], g, 4)
            project(PH["gate1"], gate_tanh(1), side=side_dsa)
            project(PH["branch1"])
            for k in range(4):
                act.wait_ge(merged_out, 8 + 2 * (k + 1))
                nc.scalar.activation(h_hi[:, 4 * k:4 * k + 4, :], merged[:, 4 * k:4 * k + 4, :],
                                     ACT.Copy).then_inc(merged_hi, 1)
                if k == 0:
                    act.wait_ge(merged_out, 16)
                turned_rows_out(k, 8, xT)
            project(PH["wout"])

            act.wait_ge(block_out, PH["wout"].b0 + 8)
            norm("ffn", 0, xT, squares, KD)
            norm("ffn", 1, xT, squares, KD)
            for k in range(4):
                norm("ffn", 2 + k, xT, squares, KD, h_hi)

            def conv_taps(f):
                def go(b, r):
                    g0 = FFN[f][0]
                    if not isinstance(b, int) or b + g0 >= 2:
                        act.wait_ge(ff_out, b + (g0 - 1))
                    for c in range(2):
                        at = c * KF + g0
                        nc.scalar.activation(conv[:, r, c, :], blk[:, r, c, 0:S], ACT.Identity,
                                             bias=col("conv_b", b + at), scale=col("conv_w2", b + at)).then_inc(conv_mid, 1)
                return go

            def conv_rest(f):
                ph, g0 = PH[f"up{f}"], FFN[f][0]

                def silu(b, r):
                    act.wait_ge(conv_out, b + (g0 + 1))
                    nc.scalar.activation(gated[:, r, :], conv[:, r, 0, :], ACT.Silu).then_inc(silu_out, 1)

                def round_hi(b, r):
                    act.wait_ge(ff_out, b + (g0 + 1))
                    nc.scalar.activation(u_hi[:, bass.ds(b, 1), :], ff[:, r:r + 1, :], ACT.Copy).then_inc(ff_hi, 1)

                def mid(j, i):
                    b = i * (ph.period // ph.bt) + j // ph.bt
                    if isinstance(b, int) and b == 0:
                        return
                    r = (ph.b0 + j // ph.bt + 1) % 2
                    if j % ph.bt == 0:
                        silu(b - 1, r)
                    if j % ph.bt == 2:
                        round_hi(b - 1, r)
                return mid, silu, round_hi
            for f in range(3):
                ph = PH[f"up{f}"]
                mid, silu, round_hi = conv_rest(f)
                project(ph, conv_taps(f), inc=0, mid=mid)
                r = (ph.b0 + ph.blocks - 1) % 2
                silu(ph.blocks - 1, r)
                round_hi(ph.blocks - 1, r)
                project(PH[f"down{f}"])

            act.wait_ge(block_out, PH["down2"].b0 + 8)
            norm("pre0", 0, xT, squares, KD)
            norm("pre0", 1, xT, squares, KD)
            for k in range(4):
                norm("pre0", 2 + k, xT, squares, KD, h_hi)
            project(PH["decay"], rows_to(low_rows, DECAY_RANK))
            project(PH["glaqk"], chunks_to(area(0, 4 * GH, S)))
            allpa = pa[:, :, :]

            def in_banks(v):
                return v.rearrange("p (b c) s -> p b (c s)", b=4)

            def side_decay(j):
                if j == 0:
                    act.wait_ge(GL["low"], 1)
                    act.wait_ge(GL["bias_row"], 1)
                    nc.scalar.activation(lowT[0:DECAY_RANK, :], pa[0:DECAY_RANK, 0, 0:S], ACT.Copy).then_inc(GL["lowT"], 1)
                if j == 2:
                    act.wait_ge(GL["gk"], 1)
                    link(nc.scalar.activation(g_la.rearrange("p t (b c) -> p (t b) c", b=2), allpa, ACT.Abs))
                if j == 3:
                    link(nc.scalar.activation(g_la, g_la, ACT.Exp, scale=-1.0))
                if j == 4:
                    nc.scalar.activation(g_la, g_la, ACT.Ln, bias=1.0).then_inc(GL["l"], 1)
                if j == 8:
                    act.wait_ge(GL["last"], 1)
                    nc.scalar.activation(in_banks(g_e), allpa, ACT.Exp).then_inc(GL["eb"], 1)
                if j == 11:
                    act.wait_ge(GL["q"], 1)
                    nc.scalar.activation(in_banks(g_e), allpa, ACT.Exp, scale=-1.0).then_inc(GL["enb"], 1)
                if j == 14:
                    act.wait_ge(GL["diff"], 2 * GH)
                    nc.scalar.activation(g_e, g_e, ACT.Exp).then_inc(GL["el"], 1)
                    act.wait_ge(GL["last"], 1)
                    nc.scalar.activation(small[:, 128:160], small[:, 96:128], ACT.Exp).then_inc(GL["el"], 1)
            project(PH["glav"], rows_to(g_v), side=side_decay)

            def side_gla(j):
                if j == 8:
                    act.wait_ge(GL["rows"], 4)
                    nc.scalar.activation(g_a, pa[:, :, 0:TRI], ACT.Copy).then_inc(GL["a"], 1)
                if j in (11, 14):
                    r = (j - 11) // 3
                    act.wait_ge(GL["o"], r + 1)
                    nc.scalar.activation(in_banks(g_o[:, 8 * r:8 * r + 8, :]), allpa, ACT.Copy).then_inc(GL["oout"], 1)
                if j == 16:
                    act.wait_ge(GL["oout"], 2)
                    nc.scalar.activation(squares, g_o, ACT.Square).then_inc(GL["sq"], 1)
                if j == 20:
                    act.wait_ge(GL["inv"], 1)
                    nc.scalar.activation(g_rstd, g_rstd, ACT.Sqrt).then_inc(GL["rstd"], 1)
            project(PH["glagate"], silu_to(g_gate), side=side_gla)
            for k in range(4):
                act.wait_ge(GL["on"], k + 1)
                nc.scalar.activation(u_hi[:, 4 * k:4 * k + 4, :], g_o[:, 4 * k:4 * k + 4, :], ACT.Copy).then_inc(GL["hi"], 1)
            project(PH["glaout"], chunks_to(y_gla))

            act.wait_ge(block_out, PH["glaout"].b0 + 8)
            norm("post0", 0, y_gla, squares, KD)
            norm("post0", 1, y_gla, squares, KD)
            norm_at(act, "post0", "done", 4)
            norm("pre1", 0, xT, squares, KD)
            norm("pre1", 1, xT, squares, KD)
            for k in range(4):
                norm("pre1", 2 + k, xT, squares, KD, h_hi)
            project(PH["latent"], chunks_to(latent))
            project(PH["krope"], rows_to(k_rope[:, :, 0:LR], LR))
            act.wait_ge(block_out, PH["krope"].b0 + 1)
            for n, at in (("qa", 0), ("kva", KL)):
                src, sq = latent[:, at:at + KL, :], latent_sq[:, at:at + KL, :]
                norm(n, 0, src, sq, KL)
                norm(n, 1, src, sq, KL)
                for k in range(4):
                    norm(n, 2 + k, src, sq, KL, u_hi[:, at:at + KL])
            project(PH["qrope"], rows_to(q_rope))
            act.wait_ge(ML["kturned"], 1)
            nc.scalar.activation(k_ropeT, pa[:, 0, 0:S], ACT.Copy).then_inc(ML["kT"], 1)
            for r in range(2):
                project(PH[f"qnope{r}"], chunks_to(q_nope))

                def kv_out(b, r):
                    nc.scalar.activation(k_nope[:, bass.ds(b, 1), :], blk[:, r, 0:1, 0:S], ACT.Copy).then_inc(act_own, 1)
                    return nc.scalar.activation(l_v[:, :, bass.ds(b * P, P)],
                                                blk[:, r, 1, 0:S].rearrange("p (t v) -> p t v", t=2), ACT.Copy)
                project(PH[f"kv{r}"], kv_out)
                own[0] += PH[f"kv{r}"].blocks
                if r == 0:
                    heads_turned_out(ML["qturned"], 1, ML["qT"], q_ropeT)

                def side_mla(j, r=r):
                    g, s = (0, j) if j < 8 else (1, j - 8)
                    if s == 2:
                        causal_attention("mla", 2 * r + g, 0, lprobs, lprobsT)
                    if s == 6:
                        causal_attention("mla", 2 * r + g, 1, lprobs, lprobsT)
                    if s == 7:
                        act.wait_ge(ATT["mla"]["pv"], 2 * r + g + 1)
                        nc.scalar.activation(l_o[:, 4 * (2 * r + g):4 * (2 * r + g) + 4, :], pa[:, :, 0:S],
                                             ACT.Copy).then_inc(ML["out"], 1)
                if r == 1:
                    act.wait_ge(ML["gated"], 1)
                project(PH[f"mlagate{r}"], silu_to(l_gate), side=side_mla)
            for k in range(4):
                act.wait_ge(ML["gated"], k // 2 + 1)
                nc.scalar.activation(u_hi[:, 4 * k:4 * k + 4, :], l_o[:, 4 * k:4 * k + 4, :], ACT.Copy).then_inc(ML["hi"], 1)
            project(PH["mlaout"], chunks_to(y_mla))
            act.wait_ge(block_out, PH["mlaout"].b0 + 8)
            norm("post1", 0, y_mla, squares, KD)
            norm("post1", 1, y_mla, squares, KD)
            for t in range(NT):
                for r in range(4):
                    act.wait_ge(oturned, 4 * t + r + 1)
                    nc.scalar.activation(rows_out[:, t, 4 * r * P:4 * (r + 1) * P], pa[:, 2 + r % 2, :],
                                         ACT.Copy).then_inc(orows, 1)

        @block.vector
        def _(dve):
            own = [0]

            def link(ins):
                own[0] += 1
                ins.then_inc(dve_own, 1)
                dve.wait_ge(dve_own, own[0])

            def tt(out_, a, b, op):
                return nc.vector.tensor_tensor(out_, a, b, op)

            def split_lo(t, i, period):
                nk, cols, _ = plan.shape[t + i * period if isinstance(i, int) else t]
                r = t % RING
                dve.wait_ge(hi_made, i * period + (t + 1))
                tt(weight_lo[:, r, 0:nk, 0:cols], weight_raw[:, r, 0:nk, 0:cols],
                   weight_hi[:, r, 0:nk, 0:cols].bitcast(F32), ALU.subtract).then_inc(lo_made, 1)

            def project(ph, out_of_psum=None, side=None, mid=None, first=0):
                if out_of_psum is not None:
                    dve.wait_ge(block_out, ph.b0)

                def tile(j, i):
                    t = ph.t0 + j
                    if not isinstance(i, int) or t + i * ph.period + RING < plan.tiles:
                        split_lo(t + RING, i, ph.period)
                    if j % ph.bt == ph.bt - 1 and out_of_psum is not None:
                        dve.wait_ge(tile_used, i * ph.period + (t + 1))
                        out_of_psum(i * (ph.period // ph.bt) + j // ph.bt, (ph.b0 + j // ph.bt) % PSUM_RING)
                    if mid is not None:
                        mid(j, i)
                    if side is not None:
                        side(j + i * ph.period)
                steps(dve, plan, ph, RING, side is not None, tile, from_round=first)

            def inverse(out_, src, dim):
                link(nc.vector.tensor_scalar(out_, src, 1.0 / dim, EPS, ALU.mult, ALU.add))
                return nc.vector.reciprocal(out_, out_)

            def norm(n, s, src, sq, chunks, gain, x_hi=None, x_lo=None, dim=D, add=False):
                q = chunks // 4
                if s == 1:
                    norm_at(dve, n, "sum", 1)
                    inverse(rstd[:], pa[:, 0, 0:S], dim).then_inc(NORM["inv"], 1)
                if s < 2:
                    return
                k = s - 2
                norm_at(dve, n, "rstd", 1)
                part = slice(k * q, (k + 1) * q)
                for c in range(k * q, (k + 1) * q):
                    ins = nc.vector.scalar_tensor_tensor(sq[:, c, :], src[:, c, :], col(gain, c), rstd[:],
                                                         ALU.mult, ALU.mult)
                    if add:
                        own[0] += 1
                        ins.then_inc(dve_own, 1)
                    else:
                        ins.then_inc(NORM["hn"], 1)
                if add:
                    dve.wait_ge(dve_own, own[0])
                    tt(xT[:, part, :], xT[:, part, :], sq[:, part, :], ALU.add).then_inc(NORM["done"], 1)
                else:
                    norm_at(dve, n, "hi", k + 1)
                    tt(x_lo[:, part, :], sq[:, part, :], x_hi[:, part, :].bitcast(F32),
                       ALU.subtract).then_inc(NORM["done"], 1)

            def head_inverse(n, sq, at, heads, dim):
                norm_at(dve, n, "sq", 1)
                v = small[:, at:at + NT * heads]
                link(nc.vector.reduce_sum(v.rearrange("p (t h) -> p t h", t=NT), sq, AX.X))
                inverse(v, v, dim).then_inc(HEADN["inv"], 1)

            def mem_scale(n, rows, at, t):
                norm_at(dve, n, "rstd", 1)
                tt(rows[:, t], rows[:, t],
                   small[:, at + 4 * t:at + 4 * t + 4].unsqueeze(2).to_broadcast([P, MH, MD]),
                   ALU.mult).then_inc(HEADN["scaled"], 1)

            def rope(v, heads, half, which, t, a, b, signal=None):
                v4 = v.rearrange("p (h two j) -> p h two j", h=heads, two=2)
                a4 = a[:, 0:2 * heads * half].rearrange("p (h two j) -> p h two j", h=heads, two=2)
                b4 = b[:, 0:2 * heads * half].rearrange("p (h two j) -> p h two j", h=heads, two=2)
                c, s = (table(w, which, t).unsqueeze(1).to_broadcast([P, heads, half]) for w in (cos, sin))
                for two in range(2):
                    tt(a4[:, :, two, :], v4[:, :, two, :], c, ALU.mult).then_inc(dve_own, 1)
                    tt(b4[:, :, two, :], v4[:, :, 1 - two, :], s, ALU.mult).then_inc(dve_own, 1)
                own[0] += 4
                dve.wait_ge(dve_own, own[0])
                first = tt(v4[:, :, 0, :], a4[:, :, 0, :], b4[:, :, 0, :], ALU.subtract)
                last = tt(v4[:, :, 1, :], a4[:, :, 1, :], b4[:, :, 1, :], ALU.add)
                own[0] += 1
                first.then_inc(dve_own, 1)
                if signal is None:
                    link(last)
                else:
                    dve.wait_ge(dve_own, own[0])
                    last.then_inc(signal, 1)

            for t in range(RING):
                split_lo(t, 0, 1)
            dve.wait_ge(small_in, 16 * 6)
            link(nc.vector.tensor_copy(pos_f[:], pos_i[:]))
            for at, half, f0, p0 in ((0, 64, 0, 0), (128, 32, 64, 0), (192, 32, 64, NT)):
                for t in range(NT):
                    a = at + t * half
                    nc.vector.tensor_scalar(angle[:, a:a + half], inv[:, f0:f0 + half],
                                            pos_f[:, p0 + t:p0 + t + 1], None, ALU.mult).then_inc(dve_own, 1)
                    own[0] += 1
            dve.wait_ge(dve_own, own[0])
            link(nc.vector.tensor_scalar(turns, angle, 1.0 / (2.0 * np.pi), ROUNDER, ALU.mult, ALU.add))
            link(nc.vector.tensor_scalar(turns, turns, -ROUNDER, None, ALU.add))
            for part in TURN:
                link(nc.vector.scalar_tensor_tensor(angle, turns, -part, angle, ALU.mult, ALU.add))
            nc.vector.tensor_scalar(angle, angle, PI_BELOW, -PI_BELOW, ALU.min, ALU.max).then_inc(angles, 1)

            norm("mem", 1, memT, squares, KD, "mem_norm")
            for k in range(4):
                norm("mem", 2 + k, memT, squares, KD, "mem_norm", u_hi, u_lo)
            dve.wait_ge(sines, 2)
            link(tt(cos[:], cos[:], cos[:], ALU.mult))
            link(nc.vector.tensor_scalar(cos[:], cos[:], -2.0, 1.0, ALU.mult, ALU.add))

            def side_x(j):
                if j == 6:
                    norm("x", 1, xT, squares, KD, "attn_norm")
                if 9 <= j < 13:
                    norm("x", 2 + j - 9, xT, squares, KD, "attn_norm", h_hi, h_lo)
            project(PH["memk"], side=side_x)

            def side_memk(j):
                if j == 2:
                    head_inverse("memk", mem_sq, 0, MH, MD)
                if j in (4, 5):
                    mem_scale("memk", mem_k, 0, j - 4)
            project(PH["memv"], side=side_memk)
            project(PH["qm"])

            def gates_of(ph):
                def mid(j, i):
                    if j % ph.bt == ph.bt - 1:
                        b = i * (ph.period // ph.bt) + j // ph.bt
                        v = gates[:, bass.ds(b * 2, 2), :]
                        dve.wait_ge(block_out, b + (ph.b0 + 1))
                        nc.vector.tensor_scalar(v, v, 0.5, 0.5, ALU.mult, ALU.add).then_inc(gate_done, 1)
                return mid

            def negative_max(a, g, src, scale, cols):
                m = small[:, 160:168].rearrange("p (t h) -> p t h", t=NT)
                for t, c in enumerate(cols):
                    own[0] += 1
                    nc.vector.tensor_reduce(m[:, t, :], src[:, :, c], AX.X, ALU.max).then_inc(dve_own, 1)
                dve.wait_ge(dve_own, own[0])
                if g > 0:
                    dve.wait_ge(ATT[a]["exp"], 8 * g)
                nc.vector.tensor_scalar(small[:, 32:40], small[:, 160:168], -scale, None,
                                        ALU.mult).then_inc(ATT[a]["masked"], 1)

            def normalise(a, g, p, cols):
                dve.wait_ge(ATT[a]["exp"], 8 * (g + 1))
                link(nc.vector.reciprocal(small[:, 48:56], small[:, 40:48]))
                for t, c in enumerate(cols):
                    n = c.stop - c.start
                    ins = tt(p[:, :, c], p[:, :, c],
                             small[:, 48 + 4 * t:52 + 4 * t].unsqueeze(2).to_broadcast([P, 4, n]), ALU.mult)
                    if t == 0:
                        own[0] += 1
                        ins.then_inc(dve_own, 1)
                dve.wait_ge(dve_own, own[0])
                ins.then_inc(ATT[a]["probs"], 1)

            def split_out(a, g, n):
                dve.wait_ge(a["hi"], g + 1)
                if n == 8:
                    v = (slice(0, KW), pa[:, :, :].rearrange("p b (c s) -> p (b c) s", c=2))
                else:
                    v = (slice(4 * g, 4 * g + 4), pa[:, :, 0:S])
                tt(u_lo[:, v[0], :], v[1], u_hi[:, v[0], :].bitcast(F32), ALU.subtract).then_inc(a["lo"], 1)

            HALVES = (slice(0, S), slice(S, 2 * S))
            TRIS = (slice(0, P), slice(P, TRI))

            def side_mem(j):
                if j == 2:
                    head_inverse("memq", mem_sq, 8, MH, MD)
                if j in (3, 4):
                    mem_scale("memq", mem_q, 8, j - 3)
                if j == 10:
                    dve.wait_ge(ATT["mem"]["scores"], 1)
                    negative_max("mem", 0, pa, MD ** -0.5, HALVES)
                if j == 14:
                    normalise("mem", 0, mem_p, HALVES)
                if j == 21:
                    split_out(ATT["mem"], 0, 8)
            project(PH["gate2"], side=side_mem, mid=gates_of(PH["gate2"]))

            def branch(n):
                def go(b, r):
                    g, m = gates[:, bass.ds(b * 2, 2), :], merged[:, bass.ds(b * 2, 2), :]
                    if n == 0:
                        tt(m, blk[:, r, :, 0:S], g, ALU.mult).then_inc(block_out, 1)
                        return
                    tt(g, blk[:, r, :, 0:S], g, ALU.mult).then_inc(block_out, 1)
                    dve.wait_ge(block_out, b + (PH[("branch2", "branch0", "branch1")[n]].b0 + 1))
                    tt(m, m, g, ALU.add).then_inc(merged_out, 1)
                return go
            dve.wait_ge(gate_done, 8)
            project(PH["branch2"], branch(0))
            project(PH["sbqk"])
            project(PH["sbv"])

            def side_sb(j):
                g, s = (0, j) if j < 12 else (1, j - 12)
                if j >= 24:
                    return
                if s == 1:
                    dve.wait_ge(SB["abs"], g + 1)
                    nc.vector.tensor_scalar(sb_z, pa[:, :, 0:TRI], HD ** -0.5, None, ALU.mult).then_inc(SB["zs"], 1)
                if s == 3:
                    dve.wait_ge(SB["zs"], g + 1)
                    dve.wait_ge(SB["ln"], g + 1)
                    nc.vector.scalar_tensor_tensor(sb_sp, sb_z, 0.0, sb_l, ALU.max, ALU.add).then_inc(SB["sp"], 1)
                if s == 7:
                    dve.wait_ge(SB["cum"], g + 1)
                    tt(sb_z, sb_z, pa[:, :, 0:TRI], ALU.subtract).then_inc(SB["u"], 1)
                if s == 11:
                    split_out(SB, g, 4)
            project(PH["gate0"], side=side_sb, mid=gates_of(PH["gate0"]))
            dve.wait_ge(gate_done, 16)
            project(PH["branch0"], branch(1))
            project(PH["qi"])
            project(PH["kiwi"])

            wi = small[:, 176:192].rearrange("p (t h) -> p t h", t=NT)

            def side_index(j):
                if j in (0, 1):
                    if j == 0:
                        dve.wait_ge(block_out, PH["qi"].b0 + 2)
                    rope(qi[:, j, :], IH, ID // 2, 1, j, rope_a, rope_b)
                if j == 2:
                    dve.wait_ge(block_out, PH["kiwi"].b0 + 1)
                    nc.vector.tensor_scalar(wi, ki_wi[:, :, ID:ID + IH], IH ** -0.5, None, ALU.mult).then_inc(dve_own, 1)
                    own[0] += 1
                    rope(ki_wi[:, 0, 0:ID], 1, ID // 2, 1, 0, rope_a, rope_b)
                    rope(ki_wi[:, 1, 0:ID], 1, ID // 2, 1, 1, rope_a, rope_b, IX["roped"])
                if j in (10, 13):
                    t = (j - 10) // 3
                    dve.wait_ge(IX["relu"], t + 1)
                    n = P * (t + 1)
                    sc = score[:, t * P:t * P + n]
                    for h in range(IH):
                        v, w = logits[:, h * n:(h + 1) * n], wi[:, t, h:h + 1]
                        if h == 0:
                            ins = nc.vector.tensor_scalar(sc, v, w, None, ALU.mult)
                        else:
                            ins = nc.vector.scalar_tensor_tensor(sc, v, w, sc, ALU.mult, ALU.add)
                        if h < IH - 1:
                            link(ins)
                    ins.then_inc(IX["score"], 1)
                if j == 14:
                    dve.wait_ge(IX["score"], 2)
                    link(nc.vector.memset(score[0:CH, CH:P], NEG_INADMISSIBLE))
                    link(nc.vector.memset(score[0:CH, TRI - CH:TRI], NEG_INADMISSIBLE))
                    link(nc.vector.tensor_copy(left, score))
            project(PH["qb"], side=side_index)

            def top_round():
                for t, c in enumerate(TRIS):
                    m = small[:, 192 + 8 * t:200 + 8 * t]
                    own[0] += 1
                    nc.vector.max(m, left[:, c]).then_inc(dve_own, 1)
                dve.wait_ge(dve_own, own[0])
                for t, c in enumerate(TRIS):
                    m = small[:, 192 + 8 * t:200 + 8 * t]
                    own[0] += 1
                    nc.vector.match_replace(left[:, c], m, left[:, c], NEG_TAKEN).then_inc(dve_own, 1)
                dve.wait_ge(dve_own, own[0])

            def head_scale(n, rows, g, at, hs):
                for t, h in hs:
                    v = rows[:, t, h * HD:(h + 1) * HD]
                    own[0] += 1
                    nc.vector.scalar_tensor_tensor(v, v, small[:, at + 8 * t + h:at + 8 * t + h + 1],
                                                   qk_gain[:, g, :], ALU.mult, ALU.mult).then_inc(dve_own, 1)
                dve.wait_ge(dve_own, own[0])

            def head_steps(n, rows, g, at, j):
                if j == 2:
                    head_inverse(n, dsa_sq.rearrange("p t (h d) -> p t h d", d=HD), at, HEADS, HD)
                if j == 4:
                    norm_at(dve, n, "rstd", 1)
                if 4 <= j < 8:
                    t, h0 = (j - 4) // 2, 4 * ((j - 4) % 2)
                    head_scale(n, rows, g, at, [(t, h0 + k) for k in range(4)])
                if j in (9, 10, 11, 12):
                    t, half = (j - 9) // 2, (j - 9) % 2
                    rope(rows[:, t, half * 512:(half + 1) * 512], 4, HD // 2, 0, t, rope_a, rope_b,
                         HEADN["scaled"] if j == 12 else None)

            def side_dsaq(j):
                head_steps("dsaq", val, 0, 64, j)
                if j < TOPK // 8:
                    top_round()
                if j == TOPK // 8:
                    link(tt(chosen, left, score, ALU.is_equal))
                    nc.vector.tensor_scalar(chosen, chosen, HIDDEN, None, ALU.mult).then_inc(IX["chosen"], 1)
            project(PH["kb"], side=side_dsaq)
            project(PH["vb"], side=lambda j: head_steps("dsak", kb_rows, 1, 80, j))

            def causal_attention(a, g, s, p, mask, scale):
                if s == 0:
                    dve.wait_ge(ATT[a]["scores"], g + 1)
                    link(nc.vector.scalar_tensor_tensor(p, pa[:, :, 0:TRI], scale,
                                                        mask.unsqueeze(1).to_broadcast([P, 4, TRI]),
                                                        ALU.mult, ALU.add))
                    negative_max(a, g, p, 1.0, TRIS)
                if s == 1:
                    normalise(a, g, p, TRIS)

            def side_dsa(j):
                g, s = (0, j) if j < 13 else (1, j - 13)
                if j >= 26:
                    return
                if j == 0:
                    dve.wait_ge(IX["chosen"], 1)
                if s in (3, 7):
                    causal_attention("dsa", g, (s - 3) // 4, probs, chosen, HD ** -0.5)
                if s == 12:
                    split_out(ATT["dsa"], g, 4)
            project(PH["gate1"], side=side_dsa, mid=gates_of(PH["gate1"]))
            dve.wait_ge(gate_done, 24)
            project(PH["branch1"], branch(2))
            for k in range(4):
                dve.wait_ge(merged_hi, k + 1)
                tt(h_lo[:, 4 * k:4 * k + 4, :], merged[:, 4 * k:4 * k + 4, :],
                   h_hi[:, 4 * k:4 * k + 4, :].bitcast(F32), ALU.subtract).then_inc(merged_ready, 1)

            def add_to_x(b, r):
                v = xT[:, bass.ds(b * 2, 2), :]
                tt(v, v, blk[:, r, :, 0:S], ALU.add).then_inc(block_out, 1)
            dve.wait_ge(turned_out, 12)
            project(PH["wout"], add_to_x)

            norm("ffn", 1, xT, squares, KD, "ffn_norm")
            for k in range(4):
                norm("ffn", 2 + k, xT, squares, KD, "ffn_norm", h_hi, h_lo)

            def conv_taps(f):
                g0 = FFN[f][0]

                def go(b, r):
                    dve.wait_ge(conv_mid, b * 2 + (2 * g0 + 2))
                    for c in range(2):
                        nc.vector.scalar_tensor_tensor(conv[:, r, c, 1:S], blk[:, r, c, 0:S - 1],
                                                       col("conv_w1", b + (c * KF + g0)), conv[:, r, c, 1:S],
                                                       ALU.mult, ALU.add).then_inc(conv_one, 1)
                    dve.wait_ge(conv_one, b * 2 + (2 * g0 + 2))
                    nc.vector.scalar_tensor_tensor(conv[:, r, 0, 2:S], blk[:, r, 0, 0:S - 2],
                                                   col("conv_w0", b + g0), conv[:, r, 0, 2:S],
                                                   ALU.mult, ALU.add).then_inc(conv_out, 1)
                    nc.vector.scalar_tensor_tensor(conv[:, r, 1, 2:S], blk[:, r, 1, 0:S - 2],
                                                   col("conv_w0", b + (KF + g0)), conv[:, r, 1, 2:S],
                                                   ALU.mult, ALU.add).then_inc(block_out, 1)
                return go

            def conv_rest(f):
                ph, g0 = PH[f"up{f}"], FFN[f][0]

                def product(b, r):
                    dve.wait_ge(silu_out, b + (g0 + 1))
                    dve.wait_ge(block_out, b + (ph.b0 + 1))
                    tt(ff[:, r, :], gated[:, r, :], conv[:, r, 1, :], ALU.mult).then_inc(ff_out, 1)

                def remainder(b, r):
                    dve.wait_ge(ff_hi, b + (g0 + 1))
                    v = bass.ds(b, 1)
                    tt(u_lo[:, v, :], ff[:, r:r + 1, :], u_hi[:, v, :].bitcast(F32),
                       ALU.subtract).then_inc(ff_ready, 1)

                def mid(j, i):
                    b = i * (ph.period // ph.bt) + j // ph.bt
                    if isinstance(b, int) and b == 0:
                        return
                    r = (ph.b0 + j // ph.bt + 1) % 2
                    if j % ph.bt == 1:
                        product(b - 1, r)
                    if j % ph.bt == 2:
                        remainder(b - 1, r)
                return mid, product, remainder
            for f in range(3):
                ph = PH[f"up{f}"]
                mid, product, remainder = conv_rest(f)
                project(ph, conv_taps(f), mid=mid, first=1)
                r = (ph.b0 + ph.blocks - 1) % 2
                product(ph.blocks - 1, r)
                remainder(ph.blocks - 1, r)
                project(PH[f"down{f}"], add_to_x)

            norm("pre0", 1, xT, squares, KD, "l0_pre")
            for k in range(4):
                norm("pre0", 2 + k, xT, squares, KD, "l0_pre", h_hi, h_lo)
            nc.vector.memset(lowT[0:32, :], 1.0).then_inc(GL["bias_row"], 1)
            project(PH["decay"])
            project(PH["glaqk"])
            b8 = pa[:, :, :].rearrange("p b (c s) -> p (b c) s", c=2)
            last = small[:, 96:128].rearrange("p (c n) -> p c n", c=2 * GH)
            decay = small[:, 128:160].rearrange("p (c n) -> p c n", c=2 * GH)

            def side_decay(j):
                if j == 5:
                    dve.wait_ge(GL["l"], 1)
                    v = g_la.rearrange("p t (b c) -> p (t b) c", b=2)
                    nc.vector.scalar_tensor_tensor(v, pa[:, :, :], 0.0, v, ALU.min, ALU.subtract).then_inc(GL["la"], 1)
                if j == 8:
                    dve.wait_ge(GL["cum"], 1)
                    nc.vector.tensor_copy(last, b8[:, :, CH - 1:S:CH]).then_inc(GL["last"], 1)
                if j == 9:
                    dve.wait_ge(GL["eb"], 1)
                    dve.wait_ge(block_out, PH["glav"].b0)
                    nc.vector.scalar_tensor_tensor(g_q, g_q, GK ** -0.5, g_e, ALU.mult, ALU.mult).then_inc(GL["q"], 1)
                if j == 12:
                    dve.wait_ge(GL["enb"], 1)
                    tt(g_ke, g_k, g_e, ALU.mult).then_inc(GL["ke"], 1)
                if j == 13:
                    dve.wait_ge(GL["ke"], 1)
                    dve.wait_ge(GL["last"], 1)
                    for c in range(2 * GH):
                        tt(g_e[:, c, :].rearrange("p (n s) -> p n s", n=4),
                           last[:, c, :].unsqueeze(2).to_broadcast([P, 4, CH]),
                           b8[:, c, :].rearrange("p (n s) -> p n s", n=4), ALU.subtract).then_inc(GL["diff"], 1)
                if j == 16:
                    dve.wait_ge(GL["el"], 2)
                    tt(g_k, g_k, g_e, ALU.mult).then_inc(GL["kl"], 1)
            project(PH["glav"], side=side_decay)

            def side_gla(j):
                if j in (1, 3, 5):
                    n = (j - 1) // 2
                    dve.wait_ge(GL["rows"], n + 1)
                    if n == 0:
                        dve.wait_ge(GL["kl"], 1)
                    else:
                        for c in range(2 * GH):
                            own[0] += 1
                            nc.vector.tensor_scalar(g_ke[:, c, 0:n * CH], g_ke[:, c, 0:n * CH],
                                                    decay[:, c, n:n + 1], None, ALU.mult).then_inc(dve_own, 1)
                        dve.wait_ge(dve_own, own[0])
                    v = slice(n * CH, (n + 1) * CH)
                    nc.vector.tensor_copy(g_ke[:, :, v], g_k[:, :, v]).then_inc(GL["step"], 1)
                if j == 19:
                    dve.wait_ge(GL["sum"], 1)
                    inverse(g_rstd.rearrange("p (b c) s -> p b (c s)", b=2), pa[:, 0:2, :], GV).then_inc(GL["inv"], 1)
                if 21 <= j < 25:
                    dve.wait_ge(GL["rstd"], 1)
                    h = j - 21
                    for c in range(4):
                        v = g_o[:, 4 * h + c, :]
                        own[0] += 1
                        nc.vector.scalar_tensor_tensor(v, v, col("g_onorm", c), g_rstd[:, h, :],
                                                       ALU.mult, ALU.mult).then_inc(dve_own, 1)
            project(PH["glagate"], side=side_gla)
            dve.wait_ge(block_out, PH["glagate"].b0 + 8)
            dve.wait_ge(dve_own, own[0])
            for k in range(4):
                v = slice(4 * k, 4 * k + 4)
                tt(g_o[:, v, :], g_o[:, v, :], g_gate[:, v, :], ALU.mult).then_inc(GL["on"], 1)
                dve.wait_ge(GL["hi"], k + 1)
                tt(u_lo[:, v, :], g_o[:, v, :], u_hi[:, v, :].bitcast(F32), ALU.subtract).then_inc(GL["ready"], 1)
            project(PH["glaout"])

            norm("post0", 1, y_gla, squares, KD, "l0_post")
            for k in range(4):
                norm("post0", 2 + k, y_gla, squares, KD, "l0_post", add=True)
            norm("pre1", 1, xT, squares, KD, "l1_pre")
            for k in range(4):
                norm("pre1", 2 + k, xT, squares, KD, "l1_pre", h_hi, h_lo)
            project(PH["latent"])
            project(PH["krope"])
            for n, at, gain in (("qa", 0, "g_qa"), ("kva", KL, "g_kva")):
                v = slice(at, at + KL)
                norm(n, 1, latent[:, v, :], latent_sq[:, v, :], KL, gain, dim=LRANK)
                for k in range(4):
                    norm(n, 2 + k, latent[:, v, :], latent_sq[:, v, :], KL, gain, u_hi[:, v], u_lo[:, v], dim=LRANK)
            for t in range(NT):
                rope(k_rope[:, t, 0:LR], 1, LR // 2, 2, t, l_rope_a, l_rope_b)
            nc.vector.tensor_copy(k_rope[:, :, LR:2 * LR], k_rope[:, :, 0:LR]).then_inc(ML["k_roped"], 1)
            project(PH["qrope"])
            dve.wait_ge(block_out, PH["qrope"].b0 + 4)
            for t in range(NT):
                rope(q_rope[:, t, :], LH, LR // 2, 2, t, l_rope_a, l_rope_b, ML["q_roped"] if t else None)
            for r in range(2):
                project(PH[f"qnope{r}"])
                project(PH[f"kv{r}"])

                def side_mla(j, r=r):
                    g, s = (0, j) if j < 8 else (1, j - 8)
                    if j == 1:
                        dve.wait_ge(consts, 6)
                    if s in (1, 4):
                        causal_attention("mla", 2 * r + g, int(s == 4), lprobs, causal, (LN + LR) ** -0.5)
                project(PH[f"mlagate{r}"], side=side_mla)
                dve.wait_ge(block_out, PH[f"mlagate{r}"].b0 + 4)
                dve.wait_ge(ML["out"], 2 * (r + 1))
                v = slice(8 * r, 8 * r + 8)
                tt(l_o[:, v, :], l_o[:, v, :], l_gate, ALU.mult).then_inc(ML["gated"], 1)
            for k in range(4):
                dve.wait_ge(ML["hi"], k + 1)
                v = slice(4 * k, 4 * k + 4)
                tt(u_lo[:, v, :], l_o[:, v, :], u_hi[:, v, :].bitcast(F32), ALU.subtract).then_inc(ML["ready"], 1)
            project(PH["mlaout"])
            norm("post1", 1, y_mla, squares, KD, "l1_post")
            for k in range(4):
                norm("post1", 2 + k, y_mla, squares, KD, "l1_post", add=True)


_INS = ["x", "mem", "positions", "attn_norm", "mem_norm", "w_in", "b_gate", "dsa_q_norm", "dsa_k_norm",
        "mem_q_norm", "mem_k_norm", "w_mem_kv", "w_branch", "w_out", "ffn_norm", "w_up", "conv_w",
        "conv_b", "w_down", "positions_2", "l0_pre_norm_2", "l0_gla_w_in_2", "l0_gla_w_gk2_2",
        "l0_gla_b_gk_2", "l0_gla_g_onorm_2", "l0_gla_w_out_2", "l0_post_norm_2", "l1_pre_norm_2",
        "l1_mla_w_in_2", "l1_mla_g_qa_2", "l1_mla_w_qb_2", "l1_mla_g_kva_2", "l1_mla_w_kvb_2",
        "l1_mla_w_out_2", "l1_post_norm_2"]


def kernel(**inputs):
    import concourse.bacc as _bacc
    from concourse.bass_utils import run_bass_kernel_spmd as _run

    nc = _bacc.Bacc("TRN2", target_bir_lowering=False, num_devices=1)
    arrays, args = {}, []
    named = [(name, np.ascontiguousarray(inputs[name])) for name in _INS]
    for half in (64, 32):
        freq = (10000.0 ** (-np.arange(half, dtype=np.float64) / half)).astype(np.float32)
        named.append((f"inv{half}", freq))
    for name, a in named:
        arrays[f"in_{name}_dram"] = a
        args.append(nc.dram_tensor(f"in_{name}_dram", a.shape, mybir.dt.from_np(a.dtype),
                                   kind="ExternalInput").ap())
    out = nc.dram_tensor("out_0_dram", (1, S, D), F32, kind="ExternalOutput").ap()
    build_program(nc, *args, out)
    r = _run(nc, [arrays], core_ids=[0])
    return r.results[0]["out_0_dram"]
```

```python
from contextlib import ExitStack
from math import lcm

import numpy as np

import concourse.bass as bass
from concourse import mybir

P = 128
ALU = mybir.AluOpType
ACT = mybir.ActivationFunctionType
F32 = mybir.dt.float32
F32R = mybir.dt.float32r
I32 = mybir.dt.int32
AX = mybir.AxisListType

EPS = 1e-6
HIDDEN = -1e30
NEG_INADMISSIBLE = -3.0e38
NEG_TAKEN = -3.4e38

RING = 4
TK, TC = 4, 256
PSUM_RING = 2


class Phase:

    def __init__(self, name, kind, blocks, ktiles, cols, src):
        self.name, self.kind, self.blocks, self.ktiles = name, kind, blocks, ktiles
        self.cols, self.src = cols, src
        self.bt = len(ktiles)
        self.n = blocks * self.bt
        self.period = lcm(PSUM_RING * self.bt, RING)


class Plan:

    def __init__(self, phases):
        self.phases = {}
        self.shape = []
        self.end_of = []
        b = 0
        for ph in phases:
            ph.t0, ph.b0 = len(self.shape), b
            for j in range(ph.n):
                nk = ph.ktiles[j % ph.bt]
                self.shape.append((nk, ph.cols, len(ph.src(j // ph.bt, j % ph.bt))))
            b += ph.blocks
            self.phases[ph.name] = ph
        self.tiles = len(self.shape)
        total = [0] * RING
        self.landed = []
        for t, (_, _, dmas) in enumerate(self.shape):
            total[t % RING] += 16 * dmas
            self.landed.append(total[t % RING])

    def rounds(self, ph, ahead):
        n = 0
        while (n + 1) * ph.period <= ph.n:
            for j in range(ph.period):
                a, b = ph.t0 + j + ahead, ph.t0 + n * ph.period + j + ahead
                if b >= self.tiles or self.shape[a] != self.shape[b]:
                    return n
                if self.landed[b] - self.landed[a] != n * (self.landed[a + ph.period] - self.landed[a]):
                    return n
            n += 1
        return n

    def landed_at(self, t, period, i):
        if isinstance(i, int):
            return self.landed[t + i * period]
        return i * (self.landed[t + period] - self.landed[t]) + self.landed[t]


def steps(eng, plan, ph, ahead, whole, tile, from_round=0):
    n = 0 if whole else plan.rounds(ph, ahead)
    if n - from_round >= 2:
        for i in range(from_round):
            for j in range(ph.period):
                tile(j, i)
        with eng.Fori(from_round, n) as i:
            for j in range(ph.period):
                tile(j, i)
    else:
        n = 0
    for t in range(n * ph.period, ph.n):
        tile(t % ph.period, t // ph.period)


D = 2048
S = 256
KD = D // P
NT = S // P
W = 1024
KW = W // P
HEADS, HD = 8, 128
IH, ID = 8, 64
TOPK = S // 4
MH, MD = 4, 256
DFF = 5504
KF = DFF // P
GATE0 = 3 * W + 3 * W + W + IH * ID + ID + IH
DECAY_RANK = 16
GH, GK, GV = 4, 256, 512
CH = 64
GTAU = 16.0
LH, LR, LN, LV = 16, 64, 128, 128
LRANK = 512
KL = LRANK // P
ROUNDER = 1.5 * 2.0 ** 23
TURN = (6.28125, float(np.float32(round((2 * np.pi - 6.28125) * 2 ** 21) / 2 ** 21)))
TURN += (2 * np.pi - sum(TURN),)
PI_BELOW = 3.1415925
TRI = 384

ROWS = {}
_at = 0
for _name, _n in (("attn_norm", KD), ("mem_norm", KD), ("b_gate", 3 * KD), ("ffn_norm", KD),
                  ("l0_pre", KD), ("l0_post", KD),
                  ("l1_pre", KD), ("l1_post", KD), ("g_qa", KL), ("g_kva", KL), ("g_onorm", GV // P),
                  ("mem_q_norm", MD // P), ("mem_k_norm", MD // P),
                  ("conv_w0", 2 * KF), ("conv_w1", 2 * KF), ("conv_w2", 2 * KF), ("conv_b", 2 * KF)):
    ROWS[_name] = (_at, _n)
    _at += _n
NVEC = _at
STAGES = [("attn_norm", "mem_norm", "b_gate", "ffn_norm", "l0_pre", "l0_post"),
          ("l1_pre", "l1_post", "g_qa", "g_kva", "g_onorm", "mem_q_norm", "mem_k_norm"),
          ("conv_w0",), ("conv_w1",), ("conv_w2",), ("conv_b",)]


def build_program(nc, x, mem, positions, attn_norm, mem_norm, w_in, b_gate, dsa_q_norm, dsa_k_norm,
                  mem_q_norm, mem_k_norm, w_mem_kv, w_branch, w_out, ffn_norm, w_up, conv_w, conv_b,
                  w_down, positions_2, l0_pre, gla_w_in, gla_w_gk2, gla_b_gk, g_onorm, gla_w_out,
                  l0_post, l1_pre, mla_w_in, g_qa, w_qb, g_kva, w_kvb, mla_w_out, l1_post,
                  inv64, inv32, out):

    def rows_of(w):
        return w.rearrange("(k p) n -> p k n", p=P)

    def cols_from(w, col0, kts, cols=TC, width=TC):
        w3 = rows_of(w)
        k0 = [sum(kts[:j]) for j in range(len(kts))]

        def src(b, kt):
            return [(slice(0, cols), w3[:, k0[kt]:k0[kt] + kts[kt], bass.ds(b * width + col0, cols)])]
        return src

    def pair_from(w, kts, col_a, col_b, step):
        w3 = rows_of(w)

        def src(b, kt):
            k = slice(TK * kt, TK * kt + kts[kt])
            return [(slice(0, P), w3[:, k, bass.ds(b * step + col_a, P)]),
                    (slice(P, 2 * P), w3[:, k, bass.ds(b * step + col_b, P)])]
        return src

    K16, K8, K4 = [TK] * 4, [TK] * 2, [TK]
    win, wup = w_in[0], w_up[0]
    down = [w_down[0][0:16 * P, :], w_down[0][16 * P:32 * P, :], w_down[0][32 * P:KF * P, :]]
    ROPE0 = LN

    def qrope_src(b, kt):
        w3 = rows_of(w_qb)
        hw = LN + LR
        return [(slice(LR * h, LR * h + LR), w3[:, 0:TK, bass.ds(b * (4 * hw) + h * hw + ROPE0, LR)])
                for h in range(4)]

    phases = [
        Phase("memk", "tm", 4, K16, TC, cols_from(w_mem_kv[0], 0, K16)),
        Phase("memv", "tm", 4, K16, TC, cols_from(w_mem_kv[0], W, K16)),
        Phase("qm", "tm", 4, K16, TC, cols_from(win, 6 * W, K16)),
        Phase("gate2", "fm", 8, K16, TC, cols_from(win, GATE0 + 2 * D, K16)),
        Phase("branch2", "fm", 8, K8, TC, cols_from(w_branch[0, 2], 0, K8)),
        Phase("sbqk", "fm", 8, K16, TC, cols_from(win, 0, K16)),
        Phase("sbv", "tm", 4, K16, TC, cols_from(win, 2 * W, K16)),
        Phase("gate0", "fm", 8, K16, TC, cols_from(win, GATE0, K16)),
        Phase("branch0", "fm", 8, K8, TC, cols_from(w_branch[0, 0], 0, K8)),
        Phase("qi", "tm", 2, K16, TC, cols_from(win, 7 * W, K16)),
        Phase("kiwi", "tm", 1, K16, ID + IH, cols_from(win, 7 * W + IH * ID, K16, ID + IH)),
        Phase("qb", "tm", 4, K16, TC, cols_from(win, 3 * W, K16)),
        Phase("kb", "tm", 4, K16, TC, cols_from(win, 4 * W, K16)),
        Phase("vb", "tm", 4, K16, TC, cols_from(win, 5 * W, K16)),
        Phase("gate1", "fm", 8, K16, TC, cols_from(win, GATE0 + D, K16)),
        Phase("branch1", "fm", 8, K8, TC, cols_from(w_branch[0, 1], 0, K8)),
        Phase("wout", "fm", 8, K16, TC, cols_from(w_out[0], 0, K16)),
    ]
    FFN = [(0, 16), (16, 16), (32, KF - 32)]
    for f, (c0, nf) in enumerate(FFN):
        kts = [min(TK, nf - k) for k in range(0, nf, TK)]
        phases += [
            Phase(f"up{f}", "fm", nf, K16, TC, pair_from(wup, K16, c0 * P, DFF + c0 * P, P)),
            Phase(f"down{f}", "fm", 8, kts, TC, cols_from(down[f], 0, kts)),
        ]
    phases += [
        Phase("glaqk", "fm", 8, K16, TC, cols_from(gla_w_in, 0, K16)),
        Phase("decay", "tm", 1, K16, DECAY_RANK, cols_from(gla_w_in, 3 * D, K16, DECAY_RANK)),
        Phase("glav", "tm", 8, K16, TC, cols_from(gla_w_in, D, K16)),
        Phase("glagate", "fm", 8, K16, TC, cols_from(gla_w_in, 2 * D, K16)),
        Phase("glaout", "fm", 8, K16, TC, cols_from(gla_w_out, 0, K16)),
        Phase("latent", "fm", 4, K16, TC, cols_from(mla_w_in, 0, K16)),
        Phase("krope", "tm", 1, K16, LR, cols_from(mla_w_in, 2 * LRANK, K16, LR)),
        Phase("qrope", "tm", 4, K4, TC, qrope_src),
    ]
    for r in range(2):
        hw = LN + LR
        phases += [
            Phase(f"qnope{r}", "fm", 4, K4, TC,
                  pair_from(w_qb, K4, 8 * r * hw, 8 * r * hw + hw, 2 * hw)),
            Phase(f"kv{r}", "kv", 8, K4, TC, cols_from(w_kvb, 8 * r * TC, K4)),
            Phase(f"mlagate{r}", "fm", 4, K16, TC,
                  cols_from(mla_w_in, 2 * LRANK + LR + r * 8 * P, K16)),
        ]
    phases += [Phase("mlaout", "fm", 8, K16, TC, cols_from(mla_w_out, 0, K16))]
    plan = Plan(phases)
    PH = plan.phases

    def chunk_rows(v, n):
        return v.rearrange("(c p) -> c p", p=P)

    VEC_SRC = {n: chunk_rows(v, n) for n, v in (
        ("attn_norm", attn_norm[0]), ("mem_norm", mem_norm[0]), ("b_gate", b_gate[0]),
        ("ffn_norm", ffn_norm[0]), ("l0_pre", l0_pre), ("l0_post", l0_post), ("l1_pre", l1_pre),
        ("l1_post", l1_post), ("g_qa", g_qa), ("g_kva", g_kva), ("g_onorm", g_onorm),
        ("mem_q_norm", mem_q_norm[0]), ("mem_k_norm", mem_k_norm[0]), ("conv_w0", conv_w[0, 0]),
        ("conv_w1", conv_w[0, 1]), ("conv_w2", conv_w[0, 2]), ("conv_b", conv_b[0]))}
    N_VEC_DMAS = len(VEC_SRC)

    with ExitStack() as ctx:
        def sb(name, shape, dt=F32):
            return ctx.enter_context(nc.sbuf_tensor(name, shape, dt))

        def sem(name):
            return ctx.enter_context(nc.semaphore(name))

        weight_raw = sb("weight_raw", [P, RING, TK, TC])
        weight_hi = sb("weight_hi", [P, RING, TK, TC], F32R)
        weight_lo = sb("weight_lo", [P, RING, TK, TC], F32R)
        xT = sb("xT", [P, KD, S])
        h_hi, h_lo = (sb(n, [P, KD, S], F32R) for n in ("h_hi", "h_lo"))
        u_hi, u_lo = (sb(n, [P, KD, S], F32R) for n in ("u_hi", "u_lo"))
        ident = sb("ident", [P, P])
        ones = sb("ones", [P, P])
        tri_ge = sb("tri_ge", [P, P])
        tri_chunk = sb("tri_chunk", [P, P])
        vec = sb("vec", [P, NVEC])
        small = sb("small", [P, 208])
        rstd = sb("rstd", [P, S])
        arena = sb("arena", [P, 18048])

        def area(at, *shape):
            n = int(np.prod(shape))
            v = arena[:, at:at + n]
            if len(shape) == 1:
                return v
            names = "abcd"[:len(shape)]
            return v.rearrange(f"p ({' '.join(names)}) -> p {' '.join(names)}",
                               **{k: s for k, s in zip(names, shape)})

        blk = ctx.enter_context(nc.psum_tensor("blk", [P, PSUM_RING, 2, 512], F32))
        pa = ctx.enter_context(nc.psum_tensor("pa", [P, 4, 512], F32))

        rows_x = area(0, NT, D)
        rows_mem = area(4096, NT, D)
        memT = area(8192, KD, S)
        squares = area(12288, KD, S)
        sum_sq = squares[:, 8:12]
        update = squares[:, 12:16]
        stage = area(16384, len(STAGES), P)
        angle, turns = area(17152, 256), area(17408, 256)
        gates = xT
        merged = area(0, KD, S)
        mem_k, mem_q = area(4096, NT, MH, MD), area(6144, NT, MH, MD)
        mem_v = area(8192, NT, MH, MD)
        mem_kT, mem_qT = area(10240, KW, S), area(12288, KW, S)
        mem_sq = area(14336, NT, MH, MD)
        mem_p = area(14336, 4, 512)
        mem_pT = area(4096, 4, 512)
        qkT = area(4096, 2 * KW, S)
        val = area(8192, NT, W)
        T = 10240
        sb_z, sb_l, sb_sp = (area(T + n * 4 * TRI, 4, TRI) for n in range(3))
        qi, ki_wi = area(T, NT, IH * ID), area(T + 1024, NT, ID + IH)
        qiT, kiT = area(T + 2048, IH, S), area(T + 4096, S)
        logits = area(T + 4352, 2048)
        rope_a, rope_b = area(T + 4352, 1024), area(T + 5376, 1024)
        score, left, chosen = (area(T + 6400 + n * TRI, TRI) for n in range(3))
        kb_rows = area(T, NT, W)
        dsa_sq = area(T + 2048, NT, W)
        probs, probsT = area(T, 4, TRI), area(T + 4 * TRI, 4, TRI)
        conv = area(0, 2, 2, S)
        gated = area(1024, 2, S)
        ff = area(1536, 2, S)
        conv_in = area(2048, 2, 2, S)
        g_q, g_k, g_v = area(0, 2 * GH, S), area(2048, 2 * GH, S), area(4096, NT, D)
        g_gate = area(8192, KD, S)
        g_la = area(12288, NT, W)
        g_ke = area(12288, 2 * GH, S)
        g_e = area(14336, 2 * GH, S)
        g_a = area(14336, 4, TRI)
        g_rstd = area(16384, GH, S)
        w_decay = area(16384, W)
        low_rows = area(17408, NT, DECAY_RANK)
        lowT = area(17440, S)
        g_o = area(0, KD, S)
        y_gla = area(4096, KD, S)
        latent = area(0, 2 * KL, S)
        q_nope, k_nope, l_v = area(0, KW, S), area(2048, KW, S), area(4096, NT, W)
        l_o, l_gate = area(6144, KD, S), area(10240, KW, S)
        q_rope = area(6144, NT, LH * LR)
        q_ropeT = area(12288, KW, S)
        l_rope_a, l_rope_b = area(14336, 1024), area(15360, 1024)
        causal = area(17408, TRI)
        k_rope, k_ropeT = area(4096, NT, 2 * LR), area(17792, S)
        lprobs, lprobsT = area(14336, 4, TRI), area(15872, 4, TRI)
        y_mla = area(0, KD, S)
        rows_out = area(4096, NT, D)
        pos_i = sb("pos_i", [P, 2 * NT], I32)
        pos_f = sb("pos_f", [P, 2 * NT])
        inv = sb("inv", [P, 96])
        qk_gain = sb("qk_gain", [P, 2, HD])
        cos, sin = sb("cos", [P, 256]), sb("sin", [P, 256])

        def table(t, which, tt):
            at, half = ((0, 64), (128, 32), (192, 32))[which]
            return t[:, at + tt * half:at + (tt + 1) * half]

        def col(name, c, n=1):
            return vec[:, bass.ds(ROWS[name][0] + c, n)]

        RSTD = {n: rstd[:] for n in ("ffn", "pre0", "post0", "pre1", "post1", "x")}
        RSTD["qa"] = vec[:, ROWS["conv_w0"][0]:ROWS["conv_w0"][0] + S]
        RSTD["kva"] = qk_gain.rearrange("p a b -> p (a b)")
        RSTD_COL = {n: small[:, 56 + 2 * k:58 + 2 * k]
                    for k, n in enumerate(("mem", "pre0", "pre1", "qa"))}
        RSTD_COL["kva"] = small[:, 56:58]

        weight_landed = [sem(f"weight_landed{r}") for r in range(RING)]
        hi_made, lo_made = sem("hi_made"), sem("lo_made")
        tile_used = sem("tile_used")
        block_out = sem("block_out")
        mem_in = [sem(f"mem_in{k}") for k in range(4)]
        x_in, vec_in, more_vec_in, small_in = sem("x_in"), sem("more_vec_in"), sem("vec_in"), sem("small_in")
        again_in, decay_in, stored = sem("again_in"), sem("decay_in"), sem("stored")
        consts = sem("consts")
        act_own, dve_own, pool_own = sem("act_own"), sem("dve_own"), sem("pool_own")
        vec_turned, vec_ready = sem("vec_turned"), sem("vec_ready")
        turned, turned_out = sem("turned"), sem("turned_out")
        silu_done = sem("silu_done")
        angles, sines, tables = sem("angles"), sem("sines"), sem("tables")
        NORM = {k: sem(f"norm_{k}") for k in ("sq", "acc", "sum", "inv", "rstd", "hn", "hi", "done")}
        HEADN = {k: sem(f"head_norm_{k}") for k in ("sq", "inv", "rstd", "scaled", "turned", "out")}
        x_update, x_new = sem("x_update"), sem("x_new")
        base, at = {}, dict.fromkeys(NORM, 0)
        for n, units, chunks in (("mem", 4, KD), ("x", 4, 0), ("ffn", 8, KD), ("pre0", 8, KD),
                                 ("post0", 8, 0), ("pre1", 4, KD), ("qa", 2, KL), ("kva", 2, KL),
                                 ("post1", 8, 0)):
            base[n] = dict(at)
            old = n == "x"
            for k, inc in (("sq", units), ("acc", units - (n in ("post0", "post1"))), ("sum", 1), ("inv", 1), ("rstd", 1),
                           ("hn", KD * old), ("hi", chunks + 4 * old), ("done", chunks + 4 * old)):
                at[k] += inc
        at = dict.fromkeys(HEADN, 0)
        for n, parts in (("memk", 2), ("memq", 2), ("dsaq", 1), ("dsak", 1)):
            base[n] = dict(at)
            for k in HEADN:
                at[k] += parts if k in ("scaled", "out") else 1

        def norm_at(eng, n, k, v):
            eng.wait_ge((HEADN if n in ("memk", "memq", "dsaq", "dsak") else NORM)[k], base[n][k] + v)

        ATT = {k: {x: sem(f"attend_{k}_{x}") for x in ("scores", "masked", "exp", "probs", "turned",
                                               "probsT", "pv", "hi", "lo")}
               for k in ("mem", "dsa", "mla")}
        SB = {x: sem(f"sb_{x}") for x in ("z", "abs", "exp", "zs", "ln", "sp", "spm", "cum", "u",
                                         "um", "a", "pv", "hi", "lo")}
        IX = {x: sem(f"index_{x}") for x in ("roped", "turned", "qT", "kturned", "kT", "logits",
                                            "relu", "score", "chosen")}
        merged_out, merged_hi, merged_ready = sem("merged_out"), sem("merged_hi"), sem("merged_ready")
        gate_done = sem("gate_done")
        conv_mid, conv_one, conv_val, conv_out, silu_out, ff_out, ff_hi, ff_ready = (
            sem(n) for n in ("conv_mid", "conv_one", "conv_val", "conv_out", "silu_out", "ff_out", "ff_hi", "ff_ready"))
        GL = {x: sem(f"gla_{x}") for x in ("low", "lowT", "gk", "abs", "l", "la", "cum", "last", "eb",
                                          "q", "enb", "ke", "diff", "el", "kl", "rows", "step", "a",
                                          "am", "o", "oout", "sq", "acc", "sum", "inv", "rstd", "on", "scaled",
                                          "hi", "ready", "bias_row")}
        ML = {x: sem(f"mla_{x}") for x in ("k_roped", "kturned", "kT", "q_roped", "qturned", "qT",
                                          "out", "gated", "hi", "ready")}
        oturned, orows = sem("oturned"), sem("orows")

        block = ctx.enter_context(nc.Block())

        @block.sync
        def _(sp):
            def load_vectors(g, landed):
                at = 0
                for n in STAGES[g]:
                    sp.dma_start(stage[at:at + ROWS[n][1], g, :], VEC_SRC[n]).then_inc(landed, 16)
                    at += ROWS[n][1]

            load_vectors(0, vec_in)
            for k in range(4):
                v = slice(4 * k * P, 4 * (k + 1) * P)
                sp.dma_start(rows_mem[:, :, v],
                             mem[0, :, v].rearrange("(t p) d -> p t d", p=P)).then_inc(mem_in[k], 16)

            def load(ph):
                def tile(j, i):
                    t = ph.t0 + j
                    if not isinstance(i, int):
                        sp.wait_ge(lo_made, i * ph.period + (t - RING + 1))
                    elif t + i * ph.period >= RING:
                        sp.wait_ge(lo_made, t + i * ph.period - RING + 1)
                    b = i * (ph.period // ph.bt) + j // ph.bt
                    nk = ph.ktiles[j % ph.bt]
                    for c, dram in ph.src(b, j % ph.bt):
                        sp.dma_start(weight_raw[:, t % RING, 0:nk, c], dram).then_inc(
                            weight_landed[t % RING], 16)
                    if ph.t0 == 0 and isinstance(i, int) and j + i * ph.period == RING - 1:
                        sp.dma_start(rows_x, x[0].rearrange("(t p) d -> p t d", p=P)).then_inc(x_in, 16)
                        for g in range(1, len(STAGES)):
                            load_vectors(g, more_vec_in)
                steps(sp, plan, ph, 0, False, tile, from_round=int(ph.t0 == 0))

            for ph in phases:
                load(ph)
                if ph.name == "gate1":
                    sp.wait_ge(ATT["dsa"]["lo"], 2)
                    sp.dma_start(area(4096, NT, D), x[0].rearrange("(t p) d -> p t d", p=P)).then_inc(again_in, 16)
                if ph.name == "up2":
                    sp.dma_start(w_decay[0:DECAY_RANK, :], gla_w_gk2).then_inc(decay_in, 16)
                    sp.dma_start(w_decay[DECAY_RANK:DECAY_RANK + 1, :],
                                 gla_b_gk.rearrange("(a n) -> a n", a=1)).then_inc(decay_in, 16)
            for r in range(4):
                sp.wait_ge(orows, r + 1)
                v = slice(4 * r * P, 4 * (r + 1) * P)
                sp.dma_start(out[0, :, v].rearrange("(t p) d -> p t d", p=P),
                             rows_out[:, :, v]).then_inc(stored, 16)
            sp.wait_ge(stored, 16 * 4)

        @block.gpsimd
        def _(pool):
            own = [0]

            def link(ins):
                own[0] += 1
                ins.then_inc(pool_own, 1)
                pool.wait_ge(pool_own, own[0])

            link(nc.gpsimd.memset(ident[:], 0.0))
            nc.gpsimd.affine_select(out=ident[:], in_=ident[:], compare_op=ALU.not_equal, fill=1.0,
                                    base=0, pattern=[[-1, P]], channel_multiplier=1).then_inc(consts, 1)
            nc.gpsimd.memset(ones[:], 1.0).then_inc(consts, 1)
            link(nc.gpsimd.memset(tri_ge[:], 1.0))
            nc.gpsimd.affine_select(out=tri_ge[:], in_=tri_ge[:], compare_op=ALU.is_ge, fill=0.0,
                                    base=0, pattern=[[-1, P]], channel_multiplier=1).then_inc(consts, 1)
            link(nc.gpsimd.memset(tri_chunk[:], 1.0 / GTAU))
            link(nc.gpsimd.affine_select(out=tri_chunk[:], in_=tri_chunk[:], compare_op=ALU.is_ge,
                                         fill=0.0, base=0, pattern=[[1, P]], channel_multiplier=-1))
            nc.gpsimd.memset(tri_chunk[0:CH, CH:P], 0.0).then_inc(consts, 1)
            pool.dma_start(pos_i[:, 0:NT], positions.rearrange("a (t p) -> p (a t)", p=P),
                           allow_slow_non_contiguous=True).then_inc(small_in, 16)
            pool.dma_start(pos_i[:, NT:2 * NT], positions_2.rearrange("a (t p) -> p (a t)", p=P),
                           allow_slow_non_contiguous=True).then_inc(small_in, 16)
            pool.dma_start(inv[:, 0:64], inv64.partition_broadcast(P)).then_inc(small_in, 16)
            pool.dma_start(inv[:, 64:96], inv32.partition_broadcast(P)).then_inc(small_in, 16)
            pool.dma_start(qk_gain[:, 0, :], dsa_q_norm[0].partition_broadcast(P)).then_inc(small_in, 16)
            pool.dma_start(qk_gain[:, 1, :], dsa_k_norm[0].partition_broadcast(P)).then_inc(small_in, 16)

            def diagonal(v, base, fill, signal):
                for c in (0, 2 * P):
                    b = v[:, :, c:c + P]
                    nc.gpsimd.affine_select(out=b, in_=b, compare_op=ALU.is_ge, fill=fill,
                                            base=base, pattern=[[0, 4], [1, P]],
                                            channel_multiplier=-1).then_inc(signal, 1)

            def sum_squares(n, units, chunks):
                for u in units:
                    norm_at(pool, n, "sq", u + 1)
                    v, total = squares[:, u % 2 * 4:u % 2 * 4 + chunks, :], sum_sq[:, 0:chunks, :]
                    if u == 0:
                        if base[n]["sum"]:
                            norm_at(pool, n, "sum", 0)
                        nc.gpsimd.tensor_copy(total, v).then_inc(NORM["acc"], 1)
                    else:
                        norm_at(pool, n, "acc", u)
                        nc.gpsimd.tensor_tensor(total, total, v, ALU.add).then_inc(NORM["acc"], 1)

            sum_squares("mem", range(4), 4)
            for u in range(4):
                norm_at(pool, "x", "sq", u + 1)
                if u == 0:
                    pool.sem_inc(NORM["acc"], 1)
                else:
                    norm_at(pool, "x", "acc", u)
                    nc.gpsimd.tensor_tensor(squares[:, 0:4, :], squares[:, 0:4, :],
                                            squares[:, 4 * u:4 * u + 4, :], ALU.add).then_inc(NORM["acc"], 1)
            for g in range(2):
                pool.wait_ge(SB["sp"], g + 1)
                diagonal(sb_sp, -1, 0.0, SB["spm"])
                pool.wait_ge(SB["u"], g + 1)
                diagonal(sb_z, -1, HIDDEN, SB["um"])
            sum_squares("ffn", range(8), 2)
            sum_squares("pre0", range(8), 2)
            pool.wait_ge(GL["a"], 1)
            diagonal(g_a, 0, 0.0, GL["am"])
            link(nc.gpsimd.memset(causal, 0.0))
            for c in (0, 2 * P):
                nc.gpsimd.affine_select(out=causal[:, c:c + P], in_=causal[:, c:c + P],
                                        compare_op=ALU.is_ge, fill=HIDDEN, base=0,
                                        pattern=[[-1, P]], channel_multiplier=1).then_inc(consts, 1)
            pool.wait_ge(GL["sq"], 1)
            v = squares.rearrange("p (h c) s -> p h c s", h=GH)
            for c in range(1, 4):
                nc.gpsimd.tensor_tensor(v[:, :, 0, :], v[:, :, 0, :], v[:, :, c, :],
                                        ALU.add).then_inc(GL["acc"], 1)
                pool.wait_ge(GL["acc"], c)
            for k in range(3):
                pool.wait_ge(silu_done, 2 * (k + 1))
                pool.wait_ge(GL["scaled"], 4 * (k + 1))
                v = slice(4 * k, 4 * k + 4)
                nc.gpsimd.tensor_tensor(g_o[:, v, :], g_o[:, v, :], g_gate[:, v, :],
                                        ALU.mult).then_inc(GL["on"], 1)
            sum_squares("post0", range(7), 2)
            sum_squares("pre1", range(4), 4)
            sum_squares("qa", range(2), 2)
            sum_squares("kva", range(2), 2)
            sum_squares("post1", range(7), 2)

        @block.tensor
        def _(pe):
            def project(ph, x_hi, x_lo, side=None, x_wait=None, lead=None):
                def tile(j, i):
                    t = ph.t0 + j
                    kt, jb = j % ph.bt, j // ph.bt
                    b = ph.b0 + jb
                    nb = ph.period // ph.bt
                    pe.wait_ge(lo_made, i * ph.period + (t + 1))
                    if kt == 0:
                        if not isinstance(i, int) or b + i * nb >= PSUM_RING:
                            pe.wait_ge(block_out, i * nb + (b - PSUM_RING + 1))
                    if isinstance(i, int) and i * nb + jb == 0 and x_wait is not None:
                        x_wait(kt)
                    nk = ph.ktiles[kt]
                    hi, lo = weight_hi[:, t % RING], weight_lo[:, t % RING]
                    for c in range(2):
                        tok = slice(c * P, c * P + P)
                        if ph.kind == "fm":
                            o = blk[:, b % PSUM_RING, c, 0:S]
                            ops = [(w[:, k, c * P:c * P + P], v[:, TK * kt + k, :])
                                   for k in range(nk) for w, v in ((hi, x_hi), (hi, x_lo), (lo, x_hi))]
                            groups = [(o, ops)]
                        elif ph.kind == "tm":
                            o = blk[:, b % PSUM_RING, c, 0:ph.cols]
                            ops = [(v[:, TK * kt + k, tok], w[:, k, 0:ph.cols])
                                   for k in range(nk) for w, v in ((hi, x_hi), (lo, x_hi), (hi, x_lo))]
                            groups = [(o, ops)]
                        elif c == 0:
                            groups = [(blk[:, b % PSUM_RING, 0, 0:S],
                                       [(w[:, k, 0:P], v[:, k, :])
                                        for k in range(nk) for w, v in ((hi, x_hi), (hi, x_lo), (lo, x_hi))])]
                        else:
                            groups = [(blk[:, b % PSUM_RING, 1, q * P:q * P + P],
                                       [(v[:, k, q * P:q * P + P], w[:, k, P:2 * P])
                                        for k in range(nk) for w, v in ((hi, x_hi), (lo, x_hi), (hi, x_lo))])
                                      for q in range(NT)]
                        for o, ops in groups:
                            for m, (lhsT, rhs) in enumerate(ops):
                                mm = nc.tensor.matmul(o, lhsT, rhs, start=(kt == 0 and m == 0),
                                                      stop=(kt == ph.bt - 1 and m == len(ops) - 1))
                    mm.then_inc(tile_used, 1)
                    if side is not None:
                        side(j + i * ph.period)
                    if lead is not None and isinstance(i, int):
                        lead(j + i * ph.period)
                steps(pe, plan, ph, 0, side is not None, tile,
                      from_round=int(ph.t0 == 0 or x_wait is not None))

            def turn_rows(rows, r, done):
                if done + r >= 2:
                    pe.wait_ge(turned_out, done + r - 1)
                for c in range(4):
                    for t in range(NT):
                        mm = nc.tensor.transpose(
                            pa[:, 2 * (r % 2) + c // 2, (c % 2) * S + t * P:(c % 2) * S + (t + 1) * P],
                            rows[:, t, (4 * r + c) * P:(4 * r + c + 1) * P], ident[:])
                mm.then_inc(turned, 1)

            def norm_sum(n, chunks, rows=True, total=sum_sq, units=4):
                norm_at(pe, n, "acc", units)
                for c in range(chunks * (n != "mem")):
                    mm = nc.tensor.matmul(pa[:, 0, 0:S], ones[:], total[:, c, :], start=(c == 0),
                                          stop=(c == chunks - 1))
                if rows:
                    for t in range(NT):
                        for c in range(chunks):
                            mm = nc.tensor.matmul(pa[:, 0, S + t:S + t + 1], total[:, c, t * P:(t + 1) * P],
                                                  ones[:, 0:1], start=(c == 0), stop=(c == chunks - 1))
                mm.then_inc(NORM["sum"], 1)

            def post_sum(n):
                norm_at(pe, n, "acc", 7)
                for c in range(2):
                    nc.tensor.matmul(pa[:, 0, 0:S], ones[:], sum_sq[:, c, :], start=(c == 0), stop=False)
                norm_at(pe, n, "sq", 8)
                for c in range(2):
                    mm = nc.tensor.matmul(pa[:, 0, 0:S], ones[:], squares[:, 4 + c, :], start=False,
                                          stop=(c == 1))
                mm.then_inc(NORM["sum"], 1)

            def norm_ready(n, chunks=TK):
                def wait(kt):
                    norm_at(pe, n, "done", chunks * (kt + 1))
                return wait

            def turn_heads(src, signal, width=P):
                for c in range(KW):
                    for t in range(NT):
                        mm = nc.tensor.transpose(
                            pa[:, c // 2, (c % 2) * S + t * P:(c % 2) * S + (t + 1) * P],
                            src[:, t, c * P:(c + 1) * P], ident[:])
                mm.then_inc(signal, 1)

            def causal_pv(probs_T, values, heads, signal):
                for h in range(4):
                    v = slice((heads + h) * P, (heads + h + 1) * P)
                    nc.tensor.matmul(pa[:, h, 0:S], values[:, 0, v], probs_T[:, h, 0:S],
                                     start=True, stop=False)
                    mm = nc.tensor.matmul(pa[:, h, P:S], values[:, 1, v], probs_T[:, h, S:TRI],
                                          start=False, stop=True)
                mm.then_inc(signal, 1)

            def causal_turn(p, signal):
                for h in range(4):
                    for c in range(3):
                        mm = nc.tensor.transpose(pa[:, h, c * P:(c + 1) * P], p[:, h, c * P:(c + 1) * P],
                                                 ident[:])
                mm.then_inc(signal, 1)

            pe.wait_ge(consts, 1)

            def turn_vectors(stages, bank):
                for k, g in enumerate(stages):
                    n = sum(ROWS[v][1] for v in STAGES[g])
                    mm = nc.tensor.transpose(pa[:, bank + k // 4, (k % 4) * P:(k % 4) * P + n], stage[0:n, g, :],
                                             ident[0:n, 0:n])
                mm.then_inc(vec_turned, 1)

            pe.wait_ge(vec_in, 16 * len(STAGES[0]))
            turn_vectors((0,), 2)
            for r in range(4):
                pe.wait_ge(mem_in[r], 16)
                if r == 1:
                    pe.wait_ge(vec_ready, 1)
                turn_rows(rows_mem, r, 0)

            def side_x(j):
                if j == 2:
                    pe.wait_ge(consts, 4)
                    norm_sum("mem", 4)
                if 3 <= j < 7:
                    if j == 3:
                        pe.wait_ge(x_in, 16)
                        norm_at(pe, "mem", "inv", 1)
                    turn_rows(rows_x, j - 3, 4)
                if j == 7:
                    pe.wait_ge(turned_out, 8)
                    pe.wait_ge(more_vec_in, 16 * (N_VEC_DMAS - len(STAGES[0])))
                    turn_vectors(range(1, len(STAGES)), 2)
                if j == 11:
                    norm_sum("x", 4, rows=False, total=squares)
            project(PH["memk"], u_hi, u_lo, side=side_x, x_wait=norm_ready("mem"))

            def side_memk(j):
                if j == 13:
                    pe.wait_ge(vec_ready, len(STAGES))
                    norm_at(pe, "memk", "scaled", 2)
                    turn_heads(mem_k.rearrange("p t h d -> p t (h d)"), HEADN["turned"])
            project(PH["memv"], u_hi, u_lo, side=side_memk)
            project(PH["qm"], h_hi, h_lo, x_wait=norm_ready("x", 1))

            def side_mem(j):
                if j == 6:
                    norm_at(pe, "memk", "out", 2)
                    norm_at(pe, "memq", "scaled", 2)
                    turn_heads(mem_q.rearrange("p t h d -> p t (h d)"), HEADN["turned"])
                if j == 9:
                    norm_at(pe, "memq", "out", 2)
                    for h in range(MH):
                        for t in range(NT):
                            for c in range(2):
                                mm = nc.tensor.matmul(pa[:, h, t * S:(t + 1) * S],
                                                      mem_qT[:, 2 * h + c, t * P:(t + 1) * P],
                                                      mem_kT[:, 2 * h + c, :], start=(c == 0), stop=(c == 1))
                    mm.then_inc(ATT["mem"]["scores"], 1)
                if j == 16:
                    pe.wait_ge(ATT["mem"]["probs"], 1)
                    for h in range(MH):
                        for k in range(2):
                            for t in range(NT):
                                mm = nc.tensor.transpose(pa[:, h, k * S + t * P:k * S + (t + 1) * P],
                                                         mem_p[:, h, t * S + k * P:t * S + (k + 1) * P],
                                                         ident[:])
                    mm.then_inc(ATT["mem"]["turned"], 1)
                if j == 19:
                    pe.wait_ge(ATT["mem"]["probsT"], 1)
                    for h in range(MH):
                        for v in range(2):
                            for k in range(2):
                                mm = nc.tensor.matmul(pa[:, h, v * S:(v + 1) * S],
                                                      mem_v[:, k, h, v * P:(v + 1) * P],
                                                      mem_pT[:, h, k * S:(k + 1) * S],
                                                      start=(k == 0), stop=(k == 1))
                    mm.then_inc(ATT["mem"]["pv"], 1)
            project(PH["gate2"], h_hi, h_lo, side=side_mem)

            def out_ready(signal, n):
                def wait(kt):
                    if kt == 0:
                        pe.wait_ge(signal, n)
                return wait
            project(PH["branch2"], u_hi, u_lo, x_wait=out_ready(ATT["mem"]["lo"], 1))
            project(PH["sbqk"], h_hi, h_lo)
            project(PH["sbv"], h_hi, h_lo)

            def side_sb(j):
                g, s = (0, j) if j < 13 else (1, j - 13)
                if s == 0:
                    pe.wait_ge(block_out, PH["gate0"].b0)
                    if g == 0:
                        pe.wait_ge(ATT["mem"]["lo"], 1)
                    else:
                        pe.wait_ge(SB["lo"], g)
                    for h in range(4):
                        c = 4 * g + h
                        nc.tensor.matmul(pa[:, h, 0:S], qkT[:, KW + c, 0:P], qkT[:, c, :],
                                         start=True, stop=True)
                        mm = nc.tensor.matmul(pa[:, h, S:TRI], qkT[:, KW + c, P:S], qkT[:, c, P:S],
                                              start=True, stop=True)
                    mm.then_inc(SB["z"], 1)
                if s == 6:
                    pe.wait_ge(SB["spm"], 2 * (g + 1))
                    pe.wait_ge(SB["zs"], g + 1)
                    for h in range(4):
                        nc.tensor.matmul(pa[:, h, 0:S], tri_ge[:], sb_sp[:, h, 0:S], start=True, stop=False)
                        nc.tensor.matmul(pa[:, h, P:S], ones[:], sb_sp[:, h, S:TRI], start=False, stop=True)
                        mm = nc.tensor.matmul(pa[:, h, S:TRI], tri_ge[:], sb_sp[:, h, S:TRI],
                                              start=True, stop=True)
                    mm.then_inc(SB["cum"], 1)
                if s == 10:
                    pe.wait_ge(SB["a"], g + 1)
                    causal_pv(sb_l, val, 4 * g, SB["pv"])
            project(PH["gate0"], h_hi, h_lo, side=side_sb)
            project(PH["branch0"], u_hi, u_lo, x_wait=out_ready(SB["lo"], 2))
            project(PH["qi"], h_hi, h_lo)
            project(PH["kiwi"], h_hi, h_lo)

            def index_logits(t):
                keys = P * (t + 1)
                for h in range(IH):
                    o = pa[:, h // 4, (h % 4) * P:(h % 4 + 1) * P] if t == 0 else \
                        pa[:, h // 2, (h % 2) * S:(h % 2 + 1) * S]
                    mm = nc.tensor.matmul(o, qiT[0:ID, h, t * P:(t + 1) * P], kiT[0:ID, 0:keys],
                                          start=True, stop=True)
                mm.then_inc(IX["logits"], 1)

            def side_index(j):
                if j == 4:
                    pe.wait_ge(IX["roped"], 1)
                    pe.wait_ge(SB["lo"], 2)
                    for h in range(IH):
                        for t in range(NT):
                            mm = nc.tensor.transpose(
                                pa[0:ID, h // 2, (h % 2) * S + t * P:(h % 2) * S + (t + 1) * P],
                                qi[:, t, h * ID:(h + 1) * ID], ident[:])
                    mm.then_inc(IX["turned"], 1)
                if j == 6:
                    pe.wait_ge(IX["qT"], 1)
                    for t in range(NT):
                        mm = nc.tensor.transpose(pa[0:ID, 0, t * P:(t + 1) * P], ki_wi[:, t, 0:ID], ident[:])
                    mm.then_inc(IX["kturned"], 1)
                if j == 8:
                    pe.wait_ge(IX["kT"], 1)
                    index_logits(0)
                if j == 11:
                    pe.wait_ge(IX["relu"], 1)
                    index_logits(1)
            project(PH["qb"], h_hi, h_lo, side=side_index)

            def side_dsaq(j):
                if j == 15:
                    pe.wait_ge(IX["relu"], 2)
                    norm_at(pe, "dsaq", "scaled", 1)
                    turn_heads(val, HEADN["turned"])
            project(PH["kb"], h_hi, h_lo, side=side_dsaq)

            def side_dsak(j):
                if j == 15:
                    norm_at(pe, "dsaq", "out", 1)
                    norm_at(pe, "dsak", "scaled", 1)
                    turn_heads(kb_rows, HEADN["turned"])
            project(PH["vb"], h_hi, h_lo, side=side_dsak)

            def causal_attention(a, g, s, first_free, score_ops, probs_, probsT_, values, v0):
                if s == 0:
                    pe.wait_ge(*first_free)
                    for h in range(4):
                        for t, (q, k, o) in enumerate(((slice(0, P), slice(0, P), slice(0, P)),
                                                       (slice(P, S), slice(0, S), slice(P, TRI)))):
                            ops = score_ops(h, q, k)
                            for m, (lhsT, rhs) in enumerate(ops):
                                mm = nc.tensor.matmul(pa[:, h, o], lhsT, rhs, start=(m == 0),
                                                      stop=(m == len(ops) - 1))
                    mm.then_inc(ATT[a]["scores"], 1)
                if s == 1:
                    pe.wait_ge(ATT[a]["probs"], g + 1)
                    causal_turn(probs_, ATT[a]["turned"])
                if s == 2:
                    pe.wait_ge(ATT[a]["probsT"], g + 1)
                    causal_pv(probsT_, values, v0, ATT[a]["pv"])

            def side_dsa(j):
                g, s = (0, j) if j < 13 else (1, j - 13)
                part = {1: 0, 9: 1, 11: 2}.get(s)
                if part is None or j >= 26:
                    return
                if j == 1:
                    pe.wait_ge(block_out, PH["gate1"].b0)
                causal_attention("dsa", g, part,
                                 (HEADN["out"], base["dsak"]["out"] + 1) if g == 0 else (ATT["dsa"]["lo"], g),
                                 lambda h, q, k: [(qkT[:, 4 * g + h, q], qkT[:, KW + 4 * g + h, k])],
                                 probs, probsT, val, 4 * g)
            project(PH["gate1"], h_hi, h_lo, side=side_dsa)
            project(PH["branch1"], u_hi, u_lo, x_wait=out_ready(ATT["dsa"]["lo"], 2))
            def turn_x(j):
                if j == 0:
                    pe.wait_ge(again_in, 16)
                if j < 4:
                    turn_rows(area(4096, NT, D), j, 8)

            def merged_wait(kt):
                pe.wait_ge(merged_ready, kt + 1)
            project(PH["wout"], h_hi, h_lo, x_wait=merged_wait, lead=turn_x)

            for f in range(3):
                first = norm_ready("ffn") if f == 0 else None
                if f == 0:
                    def side_sum(j):
                        if j == 2:
                            norm_sum("ffn", 2, rows=False, units=8)
                    project(PH["up0"], u_hi, u_lo, x_wait=first, side=side_sum)
                else:
                    project(PH[f"up{f}"], u_hi, u_lo)

                def ff_wait(kt, f=f):
                    pe.wait_ge(ff_ready, min(FFN[f][0] + TK * (kt + 1), FFN[f][0] + FFN[f][1]))
                project(PH[f"down{f}"], h_hi, h_lo, x_wait=ff_wait)

            def side_sum(j):
                if j == 2:
                    norm_sum("pre0", 2, units=8)
            project(PH["glaqk"], u_hi, u_lo, x_wait=norm_ready("pre0"), lead=side_sum)
            project(PH["decay"], u_hi, u_lo)

            def side_decay(j):
                if j == 0:
                    pe.wait_ge(block_out, PH["decay"].b0 + 1)
                    for t in range(NT):
                        mm = nc.tensor.transpose(pa[0:DECAY_RANK, 0, t * P:(t + 1) * P], low_rows[:, t, :],
                                                 ident[:])
                    mm.then_inc(GL["low"], 1)
                if j == 1:
                    pe.wait_ge(GL["lowT"], 1)
                    pe.wait_ge(decay_in, 32)
                    for t in range(NT):
                        for c in range(2):
                            mm = nc.tensor.matmul(pa[:, 2 * t + c, :], lowT[0:DECAY_RANK + 1, t * P:(t + 1) * P],
                                                  w_decay[0:DECAY_RANK + 1, c * 512:(c + 1) * 512],
                                                  start=True, stop=True)
                    mm.then_inc(GL["gk"], 1)
                if j == 8:
                    pe.wait_ge(GL["la"], 1)
                    for c in range(2 * GH):
                        for t in range(NT):
                            mm = nc.tensor.matmul(
                                pa[:, c // 2, (c % 2) * S + t * P:(c % 2) * S + (t + 1) * P],
                                g_la[:, t, c * P:(c + 1) * P], tri_chunk[:], start=True, stop=True)
                    mm.then_inc(GL["cum"], 1)
                if j in (19, 22, 25, 28):
                    n = (j - 19) // 3
                    if n == 0:
                        pe.wait_ge(GL["kl"], 1)
                    else:
                        pe.wait_ge(GL["step"], n)
                    for h in range(GH):
                        for t in range(n // 2 + 1):
                            at = n * CH if t == 0 else S + (n - 2) * CH
                            for c in range(2):
                                mm = nc.tensor.matmul(pa[:, h, at:at + CH],
                                                      g_ke[:, 2 * h + c, t * P:(t + 1) * P],
                                                      g_q[:, 2 * h + c, n * CH:(n + 1) * CH],
                                                      start=(c == 0), stop=(c == 1))
                    mm.then_inc(GL["rows"], 1)
            project(PH["glav"], u_hi, u_lo, side=side_decay)

            def side_gla(j):
                if j in (2, 5):
                    r = (j - 2) // 3
                    if r == 0:
                        pe.wait_ge(GL["am"], 2)
                        pe.wait_ge(block_out, PH["glagate"].b0)
                    else:
                        pe.wait_ge(GL["oout"], r)
                    for c in range(2 * 4):
                        h, o = 2 * r + c // 4, pa[:, c // 2, (c % 2) * S:(c % 2 + 1) * S]
                        v = slice((8 * r + c) * P, (8 * r + c + 1) * P)
                        nc.tensor.matmul(o, g_v[:, 0, v], g_a[:, h, 0:S], start=True, stop=False)
                        mm = nc.tensor.matmul(pa[:, c // 2, (c % 2) * S + P:(c % 2 + 1) * S], g_v[:, 1, v],
                                              g_a[:, h, S:TRI], start=False, stop=True)
                    mm.then_inc(GL["o"], 1)
                if j == 11:
                    pe.wait_ge(GL["acc"], 3)
                    for h in range(GH):
                        mm = nc.tensor.matmul(pa[:, h // 2, (h % 2) * S:(h % 2 + 1) * S], ones[:],
                                              squares[:, 4 * h, :], start=True, stop=True)
                    mm.then_inc(GL["sum"], 1)
            project(PH["glagate"], u_hi, u_lo, side=side_gla)

            def gla_ready(kt):
                pe.wait_ge(GL["ready"], kt + 1 if kt < 3 else 5)
            project(PH["glaout"], h_hi, h_lo, x_wait=gla_ready)

            post_sum("post0")

            def side_sum(j):
                if j == 3:
                    norm_sum("pre1", 4)
                if j == 12:
                    norm_sum("qa", 2, units=2)
            project(PH["latent"], u_hi, u_lo, x_wait=norm_ready("pre1"), side=side_sum)

            def side_sum(j):
                if j == 2:
                    norm_at(pe, "qa", "inv", 1)
                    norm_sum("kva", 2, units=2)
            project(PH["krope"], u_hi, u_lo, side=side_sum)
            project(PH["qrope"], h_hi, h_lo, x_wait=norm_ready("qa"))
            pe.wait_ge(ML["k_roped"], 1)
            norm_at(pe, "kva", "inv", 1)
            for t in range(NT):
                mm = nc.tensor.transpose(pa[:, 0, t * P:(t + 1) * P], k_rope[:, t, :], ident[:])
            mm.then_inc(ML["kturned"], 1)

            def turn_q():
                pe.wait_ge(ML["q_roped"], 1)
                pe.wait_ge(ML["kT"], 1)
                turn_heads(q_rope, ML["qturned"])

            for r in range(2):
                project(PH[f"qnope{r}"], h_hi, h_lo)
                if r == 0:
                    norm_at(pe, "kva", "done", 4)
                project(PH[f"kv{r}"], h_hi[:, KL:2 * KL], h_lo[:, KL:2 * KL])
                if r == 0:
                    turn_q()

                def side_mla(j, r=r):
                    g, s = (0, j) if j < 8 else (1, j - 8)
                    part = {0: 0, 6: 1, 7: 2}.get(s)
                    if part is None:
                        return
                    if j == 0:
                        pe.wait_ge(block_out, PH[f"mlagate{r}"].b0)
                    if j == 0 and r == 0:
                        free = (ML["qT"], 1)
                    else:
                        free = (ML["out"], 2 * r + g)

                    def ops(h, q, k):
                        c = 4 * g + h
                        half = slice(0, LR) if h % 2 == 0 else slice(LR, 2 * LR)
                        return [(q_nope[:, c, q], k_nope[:, c, k]),
                                (q_ropeT[half, 4 * r + c // 2, q], k_ropeT[half, k])]
                    causal_attention("mla", 2 * r + g, part, free, ops, lprobs, lprobsT, l_v, 4 * g)
                project(PH[f"mlagate{r}"], u_hi, u_lo, side=side_mla)

            def mla_ready(kt):
                pe.wait_ge(ML["ready"], kt + 1)
            project(PH["mlaout"], h_hi, h_lo, x_wait=mla_ready)
            post_sum("post1")
            for r in range(4):
                pe.wait_ge(x_new, 4 + r + 1)
                norm_at(pe, "post1", "inv", 1)
                if r >= 2:
                    pe.wait_ge(orows, r - 1)
                for t in range(NT):
                    for c in range(4):
                        mm = nc.tensor.transpose(pa[:, 2 * (r % 2) + t, c * P:(c + 1) * P],
                                                 xT[:, 4 * r + c, t * P:(t + 1) * P], ident[:])
                mm.then_inc(oturned, 1)

        @block.scalar
        def _(act):
            own = [0]

            def link(ins):
                own[0] += 1
                ins.then_inc(act_own, 1)
                act.wait_ge(act_own, own[0])

            def split_hi(t, period, i):
                nk, cols, _ = plan.shape[t + i * period if isinstance(i, int) else t]
                r = t % RING
                act.wait_ge(weight_landed[r], plan.landed_at(t, period, i))
                nc.scalar.activation(weight_hi[:, r, 0:nk, 0:cols], weight_raw[:, r, 0:nk, 0:cols],
                                     ACT.Copy).then_inc(hi_made, 1)

            def project(ph, out_of_psum=None, side=None, mid=None, lead=None):
                if out_of_psum is not None:
                    act.wait_ge(block_out, ph.b0)

                def tile(j, i):
                    t = ph.t0 + j
                    act.wait_ge(tile_used, i * ph.period + (t + 1))
                    if not isinstance(i, int) or t + i * ph.period + RING < plan.tiles:
                        split_hi(t + RING, ph.period, i)
                    if j % ph.bt == ph.bt - 1 and out_of_psum is not None:
                        b = i * (ph.period // ph.bt) + j // ph.bt
                        out_of_psum(b, (ph.b0 + j // ph.bt) % PSUM_RING).then_inc(block_out, 1)
                    if mid is not None:
                        mid(j, i)
                    if side is not None:
                        side(j + i * ph.period)
                    if lead is not None and isinstance(i, int):
                        lead(j + i * ph.period)
                steps(act, plan, ph, RING, side is not None, tile,
                      from_round=int(mid is not None or lead is not None))

            def rows_to(dst, cols=TC, n=None):
                def go(b, r):
                    if n is not None:
                        if isinstance(b, int) and b == 0:
                            norm_at(act, n, "rstd", 1)
                        for t in range(NT):
                            ins = nc.scalar.activation(dst[:, t:t + 1, bass.ds(b * cols, cols)],
                                                       blk[:, r, t:t + 1, 0:cols], ACT.Copy,
                                                       scale=RSTD_COL[n][:, t:t + 1])
                        return ins
                    return nc.scalar.activation(dst[:, :, bass.ds(b * cols, cols)], blk[:, r, :, 0:cols], ACT.Copy)
                return go

            def chunks_to(dst):
                def go(b, r):
                    return nc.scalar.activation(dst[:, bass.ds(b * 2, 2), :], blk[:, r, :, 0:S], ACT.Copy)
                return go

            def gate_tanh(g):
                def go(b, r):
                    for c in range(2):
                        ins = nc.scalar.activation(gates[:, bass.ds(b * 2 + c, 1), :], blk[:, r, c:c + 1, 0:S],
                                                   ACT.Tanh, bias=col("b_gate", b * 2 + (g * KD + c)), scale=0.5)
                    return ins
                return go

            def silu_of(dst, b0, b, before=0):
                act.wait_ge(block_out, b0 + b + 1)
                v = dst[:, 2 * b:2 * b + 2, :]
                nc.scalar.activation(v, v, ACT.Silu).then_inc(silu_done, 1)

            def turned_rows_out(r, done, dst):
                act.wait_ge(turned, done + r + 1)
                nc.scalar.activation(dst[:, 4 * r:4 * r + 4, :].rearrange("p (b c) s -> p b (c s)", b=2),
                                     pa[:, 2 * (r % 2):2 * (r % 2) + 2, :], ACT.Copy).then_inc(turned_out, 1)

            def unit_norm(n, u, src, chunks, gain=None, x_hi=None, c0=0):
                if gain is not None:
                    for c in range(chunks):
                        nc.scalar.activation(x_hi[:, c0 + c, :], src[:, c, :], ACT.Copy,
                                             scale=col(gain, c0 + c)).then_inc(NORM["hi"], 1)
                if u >= 2:
                    norm_at(act, n, "acc", u - 1)
                elif base[n]["sum"] and u == 0:
                    norm_at(act, n, "sum", 0)
                nc.scalar.activation(squares[:, u % 2 * 4:u % 2 * 4 + chunks, :], src, ACT.Square).then_inc(NORM["sq"], 1)

            def root(n, col_too=True):
                norm_at(act, n, "inv", 1)
                if n != "mem":
                    ins = nc.scalar.activation(RSTD[n], RSTD[n], ACT.Sqrt)
                if col_too:
                    ins = nc.scalar.activation(RSTD_COL[n], RSTD_COL[n], ACT.Sqrt)
                ins.then_inc(NORM["rstd"], 1)

            def norm(n, s, src, sq, chunks, x_hi=None):
                q = chunks // 4
                if s == 0:
                    for k in range(4):
                        nc.scalar.activation(sq[:, k * q:(k + 1) * q, :], src[:, k * q:(k + 1) * q, :],
                                             ACT.Square).then_inc(NORM["sq"], 1)
                elif s == 1:
                    norm_at(act, n, "inv", 1)
                    nc.scalar.activation(rstd[:], rstd[:], ACT.Sqrt).then_inc(NORM["rstd"], 1)
                elif x_hi is not None:
                    k = s - 2
                    norm_at(act, n, "hn", (k + 1) * q)
                    nc.scalar.activation(x_hi[:, k * q:(k + 1) * q, :], sq[:, k * q:(k + 1) * q, :],
                                         ACT.Copy).then_inc(NORM["hi"], 1)

            def head_norm(n, s, src, sq, at, heads):
                if s == 0:
                    nc.scalar.activation(sq, src, ACT.Square).then_inc(HEADN["sq"], 1)
                else:
                    norm_at(act, n, "inv", 1)
                    nc.scalar.activation(small[:, at:at + NT * heads], small[:, at:at + NT * heads],
                                         ACT.Sqrt).then_inc(HEADN["rstd"], 1)

            def mem_turned_out(n, gain, dst):
                norm_at(act, n, "turned", 1)
                for c in range(2):
                    nc.scalar.activation(dst[:, c:KW:2, :], pa[:, :, c * S:(c + 1) * S], ACT.Copy,
                                         scale=col(gain, c)).then_inc(HEADN["out"], 1)

            def heads_turned_out(signal, value, done, dst):
                act.wait_ge(signal, value)
                nc.scalar.activation(dst.rearrange("p (b c) s -> p b (c s)", b=4), pa[:, :, :],
                                     ACT.Copy).then_inc(done, 1)

            act.wait_ge(vec_turned, 1)
            N0 = sum(ROWS[n][1] for n in STAGES[0])
            link(nc.scalar.activation(vec[:, 0:N0], pa[:, 2, 0:N0], ACT.Copy))
            nc.scalar.activation(col("b_gate", 0, 3 * KD), col("b_gate", 0, 3 * KD), ACT.Copy,
                                 scale=0.5).then_inc(vec_ready, 1)
            for r in range(4):
                act.wait_ge(turned_out, r + 1)
                unit_norm("mem", r, memT[:, 4 * r:4 * r + 4, :], 4, "mem_norm", u_hi, 4 * r)
                split_hi(r, 1, 0)

            def side_x(j):
                if j == 2:
                    root("mem")
                if 3 <= j < 7:
                    turned_rows_out(j - 3, 4, xT)
                if j == 7:
                    act.wait_ge(turned_out, 8)
                    norm_at(act, "mem", "sum", 1)
                    norm("x", 0, xT, squares, KD)
                if j == 8:
                    act.wait_ge(vec_turned, 2)
                    at = N0
                    for k in range(len(STAGES) - 1):
                        n = sum(ROWS[v][1] for v in STAGES[k + 1])
                        nc.scalar.activation(vec[:, at:at + n], pa[:, 2 + k // 4, (k % 4) * P:(k % 4) * P + n],
                                             ACT.Copy).then_inc(vec_ready, 1)
                        at += n
                if j == 12:
                    norm("x", 1, xT, squares, KD)
                if j == 9:
                    act.wait_ge(angles, 1)
                    nc.scalar.activation(sin[:], angle, ACT.Sin).then_inc(sines, 1)
                    nc.scalar.activation(cos[:], angle, ACT.Sin, scale=0.5).then_inc(sines, 1)
                if j in (13, 15):
                    norm("x", 2 + (j - 13) // 2, xT, squares, KD, h_hi)
            project(PH["memk"], rows_to(mem_k.rearrange("p t h d -> p t (h d)"), n="mem"), side=side_x)

            def side_memk(j):
                if j in (1, 3):
                    norm("x", 4 + j // 2, xT, squares, KD, h_hi)
                if j == 5:
                    act.wait_ge(block_out, PH["memv"].b0)
                    norm_at(act, "x", "done", 4)
                    head_norm("memk", 0, mem_k, mem_sq, 0, MH)
                if j == 7:
                    head_norm("memk", 1, mem_k, mem_sq, 0, MH)
                if j == 14:
                    mem_turned_out("memk", "mem_k_norm", mem_kT)
            project(PH["memv"], rows_to(mem_v.rearrange("p t h d -> p t (h d)"), n="mem"), side=side_memk)
            project(PH["qm"], rows_to(mem_q.rearrange("p t h d -> p t (h d)")))

            def split_out(a, g, n):
                act.wait_ge(a["pv"], g + 1)
                if n == 8:
                    nc.scalar.activation(u_hi[:, 0:KW, :].rearrange("p (b c) s -> p b (c s)", b=4), pa[:, :, :],
                                         ACT.Copy).then_inc(a["hi"], 1)
                else:
                    nc.scalar.activation(u_hi[:, 4 * g:4 * g + 4, :], pa[:, :, 0:S],
                                         ACT.Copy).then_inc(a["hi"], 1)

            def exps(a, g, src, dst, scale, cols):
                act.wait_ge(ATT[a]["masked"], g + 1)
                for h in range(4):
                    for t, c in enumerate(cols):
                        nc.scalar.activation(dst[:, h, c], src[:, h, c], ACT.Exp,
                                             bias=small[:, 32 + 4 * t + h:33 + 4 * t + h], scale=scale,
                                             accum_out=small[:, 40 + 4 * t + h:41 + 4 * t + h]).then_inc(
                                                 ATT[a]["exp"], 1)

            def probs_turned_out(a, g, dst, width):
                act.wait_ge(ATT[a]["turned"], g + 1)
                nc.scalar.activation(dst, pa[:, :, 0:width], ACT.Copy).then_inc(ATT[a]["probsT"], 1)

            def side_mem(j):
                if j == 1:
                    act.wait_ge(block_out, PH["gate2"].b0)
                    norm_at(act, "memk", "scaled", 2)
                    head_norm("memq", 0, mem_q, mem_sq, 8, MH)
                if j == 3:
                    head_norm("memq", 1, mem_q, mem_sq, 8, MH)
                if j == 7:
                    mem_turned_out("memq", "mem_q_norm", mem_qT)
                if j == 11:
                    exps("mem", 0, pa, mem_p, MD ** -0.5, (slice(0, S), slice(S, 2 * S)))
                if j == 17:
                    probs_turned_out("mem", 0, mem_pT, 512)
                if j == 20:
                    split_out(ATT["mem"], 0, 8)
            project(PH["gate2"], gate_tanh(2), side=side_mem)
            project(PH["branch2"])
            project(PH["sbqk"], chunks_to(qkT))
            project(PH["sbv"], rows_to(val))

            def side_sb(j):
                g, s = (0, j) if j < 13 else (1, j - 13)
                if j >= 26:
                    return
                if s == 1:
                    act.wait_ge(SB["z"], g + 1)
                    nc.scalar.activation(sb_l, pa[:, :, 0:TRI], ACT.Abs, scale=HD ** -0.5).then_inc(SB["abs"], 1)
                if s == 2:
                    act.wait_ge(SB["abs"], g + 1)
                    link(nc.scalar.activation(sb_l, sb_l, ACT.Exp, scale=-1.0))
                    nc.scalar.activation(sb_l, sb_l, ACT.Ln, bias=1.0).then_inc(SB["ln"], 1)
                if s == 8:
                    act.wait_ge(SB["um"], 2 * (g + 1))
                    nc.scalar.activation(sb_l, sb_z, ACT.Exp).then_inc(SB["a"], 1)
                if s == 11:
                    split_out(SB, g, 4)
            project(PH["gate0"], gate_tanh(0), side=side_sb)
            project(PH["branch0"])
            project(PH["qi"], rows_to(qi))
            project(PH["kiwi"], rows_to(ki_wi, ID + IH))

            def side_index(j):
                if j == 5:
                    act.wait_ge(IX["turned"], 1)
                    nc.scalar.activation(qiT[0:ID].rearrange("p (b c) s -> p b (c s)", b=4), pa[0:ID, :, :],
                                         ACT.Copy).then_inc(IX["qT"], 1)
                if j == 7:
                    act.wait_ge(IX["kturned"], 1)
                    nc.scalar.activation(kiT[0:ID, :], pa[0:ID, 0, 0:S], ACT.Copy).then_inc(IX["kT"], 1)
                if j == 9:
                    act.wait_ge(IX["logits"], 1)
                    nc.scalar.activation(logits[:, 0:IH * P].rearrange("p (b c) -> p b c", b=2), pa[:, 0:2, :],
                                         ACT.Relu, scale=ID ** -0.5).then_inc(IX["relu"], 1)
                if j == 12:
                    act.wait_ge(IX["logits"], 2)
                    act.wait_ge(IX["score"], 1)
                    nc.scalar.activation(logits.rearrange("p (b c) -> p b c", b=4), pa[:, :, :],
                                         ACT.Relu, scale=ID ** -0.5).then_inc(IX["relu"], 1)
            project(PH["qb"], rows_to(val), side=side_index)

            def heads(v):
                return v.rearrange("p t (h d) -> p t h d", d=HD)

            def side_dsaq(j):
                if j == 1:
                    act.wait_ge(block_out, PH["kb"].b0)
                    act.wait_ge(IX["score"], 2)
                    head_norm("dsaq", 0, heads(val), heads(dsa_sq), 64, HEADS)
                if j == 3:
                    head_norm("dsaq", 1, None, None, 64, HEADS)
                if j == 15:
                    heads_turned_out(HEADN["turned"], base["dsaq"]["turned"] + 1, HEADN["out"], qkT[:, 0:KW, :])
            project(PH["kb"], rows_to(kb_rows), side=side_dsaq)

            def side_dsak(j):
                if j == 1:
                    act.wait_ge(block_out, PH["vb"].b0)
                    norm_at(act, "dsaq", "scaled", 1)
                    head_norm("dsak", 0, heads(kb_rows), heads(dsa_sq), 80, HEADS)
                if j == 3:
                    head_norm("dsak", 1, None, None, 80, HEADS)
                if j == 15:
                    heads_turned_out(HEADN["turned"], base["dsak"]["turned"] + 1, HEADN["out"], qkT[:, KW:2 * KW, :])
            project(PH["vb"], rows_to(val), side=side_dsak)

            def causal_attention(a, g, s, p, pT):
                if s == 0:
                    exps(a, g, p, p, 1.0, (slice(0, P), slice(P, TRI)))
                if s == 1:
                    probs_turned_out(a, g, pT, TRI)

            def side_dsa(j):
                g, s = (0, j) if j < 13 else (1, j - 13)
                if j >= 26:
                    return
                if s == 5:
                    causal_attention("dsa", g, 0, probs, probsT)
                if s == 10:
                    causal_attention("dsa", g, 1, probs, probsT)
                if s == 12:
                    split_out(ATT["dsa"], g, 4)
            project(PH["gate1"], gate_tanh(1), side=side_dsa)

            def round_merged(k):
                act.wait_ge(merged_out, 8 + 2 * (k + 1))
                nc.scalar.activation(h_hi[:, 4 * k:4 * k + 4, :], merged[:, 4 * k:4 * k + 4, :],
                                     ACT.Copy).then_inc(merged_hi, 1)

            project(PH["branch1"], side=lambda j: round_merged(j // 4 - 1) if j % 4 == 0 and j > 0 else None)
            round_merged(3)

            def x_block(n, gain, b0, b):
                act.wait_ge(block_out, b0 + b + 1)
                unit_norm(n, b, xT[:, 2 * b:2 * b + 2, :], 2, gain, u_hi, 2 * b)

            def side_ffn(j):
                if j < 4:
                    turned_rows_out(j, 8, xT)
                if j % 4 == 0 and j > 0:
                    x_block("ffn", "ffn_norm", PH["wout"].b0, j // 4 - 1)
            project(PH["wout"], side=side_ffn)
            x_block("ffn", "ffn_norm", PH["wout"].b0, 7)


            def conv_steps(f):
                ph, g0 = PH[f"up{f}"], FFN[f][0]

                def conv_taps(b, r):
                    if not isinstance(b, int) or b + g0 >= 2:
                        act.wait_ge(ff_out, b + (g0 - 1))
                    act.wait_ge(block_out, b + (ph.b0 + 1))
                    for c in range(2):
                        at = c * KF + g0
                        nc.scalar.activation(conv[:, r, c, :], conv_in[:, r, c, :], ACT.Identity,
                                             bias=col("conv_b", b + at), scale=col("conv_w2", b + at)).then_inc(conv_mid, 1)

                def silu(b, r):
                    act.wait_ge(conv_out, b + (g0 + 1))
                    nc.scalar.activation(gated[:, r, :], conv[:, r, 0, :], ACT.Silu).then_inc(silu_out, 1)

                def round_hi(b, r):
                    act.wait_ge(ff_out, b + (g0 + 1))
                    nc.scalar.activation(h_hi[:, bass.ds(b, 1), :], ff[:, r:r + 1, :], ACT.Copy).then_inc(ff_hi, 1)

                def mid(j, i):
                    b = i * (ph.period // ph.bt) + j // ph.bt
                    if isinstance(b, int) and b == 0:
                        return
                    r = (ph.b0 + j // ph.bt + 1) % 2
                    if j % ph.bt == 0:
                        conv_taps(b - 1, r)
                    if j % ph.bt == 2:
                        silu(b - 1, r)
                    if j % ph.bt == 3:
                        round_hi(b - 1, r)
                return mid, conv_taps, silu, round_hi
            for f in range(3):
                ph = PH[f"up{f}"]
                mid, conv_taps, silu, round_hi = conv_steps(f)

                def side_root(j):
                    if j == 2:
                        root("ffn", col_too=False)
                project(ph, mid=mid, side=side_root if f == 0 else None)
                r = (ph.b0 + ph.blocks - 1) % 2
                conv_taps(ph.blocks - 1, r)
                silu(ph.blocks - 1, r)
                round_hi(ph.blocks - 1, r)
                if f < 2:
                    project(PH[f"down{f}"])

            def side_pre0(j):
                bt = PH["down2"].bt
                if j % bt == 0 and j > 0:
                    x_block("pre0", "l0_pre", PH["down2"].b0, j // bt - 1)
            project(PH["down2"], side=side_pre0)
            x_block("pre0", "l0_pre", PH["down2"].b0, 7)

            project(PH["glaqk"], lead=lambda j: root("pre0") if j == 2 else None)
            project(PH["decay"], rows_to(low_rows, DECAY_RANK, "pre0"))
            allpa = pa[:, :, :]

            def in_banks(v):
                return v.rearrange("p (b c) s -> p b (c s)", b=4)

            def side_decay(j):
                if j == 0:
                    act.wait_ge(GL["low"], 1)
                    act.wait_ge(GL["bias_row"], 1)
                    nc.scalar.activation(lowT[0:DECAY_RANK, :], pa[0:DECAY_RANK, 0, 0:S], ACT.Copy).then_inc(GL["lowT"], 1)
                if j == 2:
                    act.wait_ge(GL["gk"], 1)
                    link(nc.scalar.activation(g_la.rearrange("p t (b c) -> p (t b) c", b=2), allpa, ACT.Abs))
                if j == 3:
                    link(nc.scalar.activation(g_la, g_la, ACT.Exp, scale=-1.0))
                if j == 4:
                    nc.scalar.activation(g_la, g_la, ACT.Ln, bias=1.0).then_inc(GL["l"], 1)
                if j == 9:
                    act.wait_ge(GL["last"], 1)
                    nc.scalar.activation(in_banks(g_e), allpa, ACT.Exp).then_inc(GL["eb"], 1)
                if j == 12:
                    act.wait_ge(GL["q"], 1)
                    nc.scalar.activation(in_banks(g_e), allpa, ACT.Exp, scale=-1.0).then_inc(GL["enb"], 1)
                if j == 15:
                    act.wait_ge(GL["diff"], 2 * GH)
                    nc.scalar.activation(g_e, g_e, ACT.Exp).then_inc(GL["el"], 1)
                    act.wait_ge(GL["last"], 1)
                    nc.scalar.activation(small[:, 128:160], small[:, 96:128], ACT.Exp).then_inc(GL["el"], 1)
                if j == 29:
                    act.wait_ge(GL["rows"], 4)
                    nc.scalar.activation(g_a, pa[:, :, 0:TRI], ACT.Copy).then_inc(GL["a"], 1)
            project(PH["glav"], rows_to(g_v, n="pre0"), side=side_decay)

            def round_gated_gla(k):
                act.wait_ge(GL["on"], k + 1)
                v = slice(4 * k, 4 * k + 4) if k < 3 else slice(2 * k + 6, 2 * k + 8)
                nc.scalar.activation(h_hi[:, v, :], g_o[:, v, :], ACT.Copy).then_inc(GL["hi"], 1)

            def side_gla(j):
                if j in (3, 6):
                    r = (j - 3) // 3
                    act.wait_ge(GL["o"], r + 1)
                    nc.scalar.activation(in_banks(g_o[:, 8 * r:8 * r + 8, :]), allpa, ACT.Copy).then_inc(GL["oout"], 1)
                if j == 7:
                    act.wait_ge(GL["oout"], 2)
                    nc.scalar.activation(squares, g_o, ACT.Square).then_inc(GL["sq"], 1)
                if j == 15:
                    act.wait_ge(GL["inv"], GH)
                    nc.scalar.activation(g_rstd, g_rstd, ACT.Sqrt).then_inc(GL["rstd"], 1)
                if j % 4 == 0 and j > 0:
                    silu_of(g_gate, PH["glagate"].b0, j // 4 - 1)
                if j in (18, 20, 26, 30):
                    round_gated_gla({18: 0, 20: 1, 26: 2, 30: 3}[j])
            project(PH["glagate"], side=side_gla)
            silu_of(g_gate, PH["glagate"].b0, 7)
            round_gated_gla(4)

            def y_out(n, y, gain):
                def go(b, r):
                    unit_norm(n, b, blk[:, r, :, 0:S], 2)
                    for c in range(2):
                        ins = nc.scalar.activation(y[:, 2 * b + c, :], blk[:, r, c, 0:S], ACT.Copy,
                                                   scale=col(gain, 2 * b + c))
                    return ins
                return go
            project(PH["glaout"], y_out("post0", y_gla, "l0_post"), side=lambda j: None)

            root("post0", col_too=False)
            for k in range(4):
                act.wait_ge(x_new, k + 1)
                unit_norm("pre1", k, xT[:, 4 * k:4 * k + 4, :], 4, "l1_pre", u_hi, 4 * k)

            def latent_block(b):
                act.wait_ge(block_out, PH["latent"].b0 + b + 1)
                n, at = (("qa", 0), ("kva", KL))[b // 2]
                unit_norm(n, b % 2, latent[:, 2 * b:2 * b + 2, :], 2, "g_" + n, h_hi[:, at:at + KL], 2 * (b % 2))

            def side_latent(j):
                if j == 3:
                    root("pre1")
                if j in (5, 9, 13):
                    latent_block((j - 5) // 4)
                if j == 14:
                    root("qa")
            project(PH["latent"], side=side_latent)

            def side_kva(j):
                if j == 0:
                    latent_block(3)
                if j == 3:
                    root("kva")
            project(PH["krope"], rows_to(k_rope[:, :, 0:LR], LR, "pre1"), side=side_kva)
            project(PH["qrope"], rows_to(q_rope, n="qa"))
            act.wait_ge(ML["kturned"], 1)
            nc.scalar.activation(k_ropeT, pa[:, 0, 0:S], ACT.Copy).then_inc(ML["kT"], 1)

            def round_gated(k):
                act.wait_ge(ML["gated"], k + 1)
                nc.scalar.activation(h_hi[:, 4 * k:4 * k + 4, :], l_o[:, 4 * k:4 * k + 4, :], ACT.Copy).then_inc(ML["hi"], 1)

            for r in range(2):
                project(PH[f"qnope{r}"])
                project(PH[f"kv{r}"])
                if r == 0:
                    heads_turned_out(ML["qturned"], 1, ML["qT"], q_ropeT)

                def side_mla(j, r=r):
                    g, s = (0, j) if j < 8 else (1, j - 8)
                    if s == 2:
                        causal_attention("mla", 2 * r + g, 0, lprobs, lprobsT)
                    if s == 6:
                        causal_attention("mla", 2 * r + g, 1, lprobs, lprobsT)
                    if s == 7:
                        act.wait_ge(ATT["mla"]["pv"], 2 * r + g + 1)
                        nc.scalar.activation(l_o[:, 4 * (2 * r + g):4 * (2 * r + g) + 4, :], pa[:, :, 0:S],
                                             ACT.Copy).then_inc(ML["out"], 1)
                    if j % 4 == 0 and j > 0:
                        silu_of(l_gate, PH[f"mlagate{r}"].b0, j // 4 - 1)
                    if r == 1 and j in (7, 9, 12):
                        round_gated({7: 0, 9: 1, 12: 2}[j])
                project(PH[f"mlagate{r}"], side=side_mla)
                silu_of(l_gate, PH[f"mlagate{r}"].b0, 3)
            round_gated(3)
            project(PH["mlaout"], y_out("post1", y_mla, "l1_post"), side=lambda j: None)
            root("post1", col_too=False)
            for r in range(4):
                act.wait_ge(oturned, r + 1)
                nc.scalar.activation(rows_out[:, :, 4 * r * P:4 * (r + 1) * P], pa[:, 2 * (r % 2):2 * (r % 2) + 2, :],
                                     ACT.Copy).then_inc(orows, 1)

        @block.vector
        def _(dve):
            own = [0]

            def link(ins):
                own[0] += 1
                ins.then_inc(dve_own, 1)
                dve.wait_ge(dve_own, own[0])

            def tt(out_, a, b, op):
                return nc.vector.tensor_tensor(out_, a, b, op)

            def split_lo(t, i, period):
                nk, cols, _ = plan.shape[t + i * period if isinstance(i, int) else t]
                r = t % RING
                dve.wait_ge(hi_made, i * period + (t + 1))
                tt(weight_lo[:, r, 0:nk, 0:cols], weight_raw[:, r, 0:nk, 0:cols],
                   weight_hi[:, r, 0:nk, 0:cols].bitcast(F32), ALU.subtract).then_inc(lo_made, 1)

            def project(ph, out_of_psum=None, side=None, mid=None, first=0, lead=None):
                if out_of_psum is not None:
                    dve.wait_ge(block_out, ph.b0)

                def tile(j, i):
                    t = ph.t0 + j
                    if j % ph.bt == ph.bt - 1 and out_of_psum is not None:
                        dve.wait_ge(tile_used, i * ph.period + (t + 1))
                        out_of_psum(i * (ph.period // ph.bt) + j // ph.bt, (ph.b0 + j // ph.bt) % PSUM_RING)
                    if not isinstance(i, int) or t + i * ph.period + RING < plan.tiles:
                        split_lo(t + RING, i, ph.period)
                    if mid is not None:
                        mid(j, i)
                    if side is not None:
                        side(j + i * ph.period)
                    if lead is not None and isinstance(i, int):
                        lead(j + i * ph.period)
                steps(dve, plan, ph, RING, side is not None, tile, from_round=max(first, int(lead is not None)))

            def inverse(out_, src, dim):
                link(nc.vector.tensor_scalar(out_, src, 1.0 / dim, EPS, ALU.mult, ALU.add))
                return nc.vector.reciprocal(out_, out_)

            def norm_inverse(n, dim=D, col_too=True):
                norm_at(dve, n, "sum", 1)
                if n != "mem":
                    ins = inverse(RSTD[n], pa[:, 0, 0:S], dim)
                if col_too:
                    ins = inverse(RSTD_COL[n], pa[:, 0, S:S + NT], dim)
                ins.then_inc(NORM["inv"], 1)

            def unit_norm(n, chunks, src, gain, x_hi, x_lo):
                for c in chunks:
                    norm_at(dve, n, "hi", c + 1)
                    nc.vector.scalar_tensor_tensor(x_lo[:, c, :], src[:, c, :], col(gain, c),
                                                   x_hi[:, c, :].bitcast(F32), ALU.mult,
                                                   ALU.subtract).then_inc(NORM["done"], 1)

            def x_normed(k):
                norm_at(dve, "x", "rstd", 1)
                for c in range(4 * k, 4 * k + 4):
                    nc.vector.scalar_tensor_tensor(squares[:, c, :], xT[:, c, :], col("attn_norm", c),
                                                   rstd[:], ALU.mult, ALU.mult).then_inc(NORM["hn"], 1)

            def x_rest(k):
                norm_at(dve, "x", "hi", k + 1)
                part = slice(4 * k, 4 * k + 4)
                tt(h_lo[:, part, :], squares[:, part, :], h_hi[:, part, :].bitcast(F32),
                   ALU.subtract).then_inc(NORM["done"], 1)

            def y_times_rstd(n, y, before, k):
                norm_at(dve, n, "rstd", 1)
                if before + k > 0:
                    dve.wait_ge(x_new, before + k)
                tt(update, y[:, 4 * k:4 * k + 4, :], RSTD[n].unsqueeze(1).to_broadcast([P, 4, S]),
                   ALU.mult).then_inc(x_update, 1)

            def y_added(before, k):
                dve.wait_ge(x_update, before + k + 1)
                v = xT[:, 4 * k:4 * k + 4, :]
                tt(v, v, update, ALU.add).then_inc(x_new, 1)

            def scaled_to(dst, n):
                def go(b, r):
                    if isinstance(b, int) and b == 0:
                        norm_at(dve, n, "rstd", 1)
                    tt(dst[:, bass.ds(b * 2, 2), :], blk[:, r, :, 0:S],
                       RSTD[n].unsqueeze(1).to_broadcast([P, 2, S]), ALU.mult).then_inc(block_out, 1)
                return go

            def head_inverse(n, sq, at, heads, dim):
                norm_at(dve, n, "sq", 1)
                v = small[:, at:at + NT * heads]
                link(nc.vector.reduce_sum(v.rearrange("p (t h) -> p t h", t=NT), sq, AX.X))
                inverse(v, v, dim).then_inc(HEADN["inv"], 1)

            def mem_scale(n, rows, at, t):
                norm_at(dve, n, "rstd", 1)
                tt(rows[:, t], rows[:, t],
                   small[:, at + 4 * t:at + 4 * t + 4].unsqueeze(2).to_broadcast([P, MH, MD]),
                   ALU.mult).then_inc(HEADN["scaled"], 1)

            def rope(v, heads, half, which, t, a, b, signal=None):
                v4 = v.rearrange("p (h two j) -> p h two j", h=heads, two=2)
                a4 = a[:, 0:2 * heads * half].rearrange("p (h two j) -> p h two j", h=heads, two=2)
                b4 = b[:, 0:2 * heads * half].rearrange("p (h two j) -> p h two j", h=heads, two=2)
                c, s = (table(w, which, t).unsqueeze(1).to_broadcast([P, heads, half]) for w in (cos, sin))
                for two in range(2):
                    tt(a4[:, :, two, :], v4[:, :, two, :], c, ALU.mult).then_inc(dve_own, 1)
                    tt(b4[:, :, two, :], v4[:, :, 1 - two, :], s, ALU.mult).then_inc(dve_own, 1)
                own[0] += 4
                dve.wait_ge(dve_own, own[0])
                first = tt(v4[:, :, 0, :], a4[:, :, 0, :], b4[:, :, 0, :], ALU.subtract)
                last = tt(v4[:, :, 1, :], a4[:, :, 1, :], b4[:, :, 1, :], ALU.add)
                own[0] += 1
                first.then_inc(dve_own, 1)
                if signal is None:
                    link(last)
                else:
                    dve.wait_ge(dve_own, own[0])
                    last.then_inc(signal, 1)

            def mem_out(r):
                dve.wait_ge(turned, r + 1)
                nc.vector.tensor_copy(memT[:, 4 * r:4 * r + 4, :].rearrange("p (b c) s -> p b (c s)", b=2),
                                      pa[:, 2 * (r % 2):2 * (r % 2) + 2, :]).then_inc(turned_out, 1)

            mem_out(0)
            dve.wait_ge(vec_ready, 1)
            for r in range(4):
                if r < 3:
                    mem_out(r + 1)
                unit_norm("mem", range(4 * r, 4 * r + 4), memT, "mem_norm", u_hi, u_lo)
                split_lo(r, 0, 1)

            def make_angles():
                dve.wait_ge(small_in, 16 * 6)
                link(nc.vector.tensor_copy(pos_f[:], pos_i[:]))
                for at, half, f0, p0 in ((0, 64, 0, 0), (128, 32, 64, 0), (192, 32, 64, NT)):
                    for t in range(NT):
                        a = at + t * half
                        nc.vector.tensor_scalar(angle[:, a:a + half], inv[:, f0:f0 + half],
                                                pos_f[:, p0 + t:p0 + t + 1], None, ALU.mult).then_inc(dve_own, 1)
                        own[0] += 1
                dve.wait_ge(dve_own, own[0])
                link(nc.vector.tensor_scalar(turns, angle, 1.0 / (2.0 * np.pi), ROUNDER, ALU.mult, ALU.add))
                link(nc.vector.tensor_scalar(turns, turns, -ROUNDER, None, ALU.add))
                for part in TURN:
                    link(nc.vector.scalar_tensor_tensor(angle, turns, -part, angle, ALU.mult, ALU.add))
                nc.vector.tensor_scalar(angle, angle, PI_BELOW, -PI_BELOW, ALU.min, ALU.max).then_inc(angles, 1)

            def make_cosines():
                dve.wait_ge(sines, 2)
                link(tt(cos[:], cos[:], cos[:], ALU.mult))
                link(nc.vector.tensor_scalar(cos[:], cos[:], -2.0, 1.0, ALU.mult, ALU.add))

            def side_x(j):
                if j == 2:
                    norm_inverse("mem")
                if j == 5:
                    make_angles()
                if j == 10:
                    make_cosines()
                if j == 11:
                    norm_inverse("x", col_too=False)
                if j == 12:
                    x_normed(0)
                if j == 14:
                    x_rest(0)
                    x_normed(1)
            project(PH["memk"], side=side_x)

            def side_memk(j):
                if j in (0, 2, 4):
                    x_rest(1 + j // 2)
                    if j < 4:
                        x_normed(2 + j // 2)
                if j == 6:
                    head_inverse("memk", mem_sq, 0, MH, MD)
                if j in (8, 9):
                    mem_scale("memk", mem_k, 0, j - 8)
            project(PH["memv"], side=side_memk)
            project(PH["qm"])

            def gates_of(ph):
                def mid(j, i):
                    if j % ph.bt == ph.bt - 1:
                        b = i * (ph.period // ph.bt) + j // ph.bt
                        v = gates[:, bass.ds(b * 2, 2), :]
                        dve.wait_ge(block_out, b + (ph.b0 + 1))
                        nc.vector.tensor_scalar(v, v, 0.5, 0.5, ALU.mult, ALU.add).then_inc(gate_done, 1)
                return mid

            def negative_max(a, g, src, scale, cols):
                m = small[:, 160:168].rearrange("p (t h) -> p t h", t=NT)
                for t, c in enumerate(cols):
                    own[0] += 1
                    nc.vector.tensor_reduce(m[:, t, :], src[:, :, c], AX.X, ALU.max).then_inc(dve_own, 1)
                dve.wait_ge(dve_own, own[0])
                if g > 0:
                    dve.wait_ge(ATT[a]["exp"], 8 * g)
                nc.vector.tensor_scalar(small[:, 32:40], small[:, 160:168], -scale, None,
                                        ALU.mult).then_inc(ATT[a]["masked"], 1)

            def normalise(a, g, p, cols):
                dve.wait_ge(ATT[a]["exp"], 8 * (g + 1))
                link(nc.vector.reciprocal(small[:, 48:56], small[:, 40:48]))
                for t, c in enumerate(cols):
                    n = c.stop - c.start
                    ins = tt(p[:, :, c], p[:, :, c],
                             small[:, 48 + 4 * t:52 + 4 * t].unsqueeze(2).to_broadcast([P, 4, n]), ALU.mult)
                    if t == 0:
                        own[0] += 1
                        ins.then_inc(dve_own, 1)
                dve.wait_ge(dve_own, own[0])
                ins.then_inc(ATT[a]["probs"], 1)

            def split_out(a, g, n):
                dve.wait_ge(a["hi"], g + 1)
                if n == 8:
                    v = (slice(0, KW), pa[:, :, :].rearrange("p b (c s) -> p (b c) s", c=2))
                else:
                    v = (slice(4 * g, 4 * g + 4), pa[:, :, 0:S])
                tt(u_lo[:, v[0], :], v[1], u_hi[:, v[0], :].bitcast(F32), ALU.subtract).then_inc(a["lo"], 1)

            HALVES = (slice(0, S), slice(S, 2 * S))
            TRIS = (slice(0, P), slice(P, TRI))

            def side_mem(j):
                if j == 2:
                    head_inverse("memq", mem_sq, 8, MH, MD)
                if j in (3, 4):
                    mem_scale("memq", mem_q, 8, j - 3)
                if j == 10:
                    dve.wait_ge(ATT["mem"]["scores"], 1)
                    negative_max("mem", 0, pa, MD ** -0.5, HALVES)
                if j == 14:
                    normalise("mem", 0, mem_p, HALVES)
                if j == 21:
                    split_out(ATT["mem"], 0, 8)
            project(PH["gate2"], side=side_mem, mid=gates_of(PH["gate2"]))

            def branch(n):
                def go(b, r):
                    g, m = gates[:, bass.ds(b * 2, 2), :], merged[:, bass.ds(b * 2, 2), :]
                    if n == 0:
                        tt(m, blk[:, r, :, 0:S], g, ALU.mult).then_inc(block_out, 1)
                        return
                    tt(g, blk[:, r, :, 0:S], g, ALU.mult).then_inc(block_out, 1)
                    dve.wait_ge(block_out, b + (PH[("branch2", "branch0", "branch1")[n]].b0 + 1))
                    tt(m, m, g, ALU.add).then_inc(merged_out, 1)
                return go
            dve.wait_ge(gate_done, 8)
            project(PH["branch2"], branch(0))
            project(PH["sbqk"])
            project(PH["sbv"])

            def side_sb(j):
                g, s = (0, j) if j < 13 else (1, j - 13)
                if j >= 26:
                    return
                if s == 1:
                    dve.wait_ge(SB["abs"], g + 1)
                    nc.vector.tensor_scalar(sb_z, pa[:, :, 0:TRI], HD ** -0.5, None, ALU.mult).then_inc(SB["zs"], 1)
                if s == 2:
                    dve.wait_ge(SB["zs"], g + 1)
                    dve.wait_ge(SB["ln"], g + 1)
                    nc.vector.scalar_tensor_tensor(sb_sp, sb_z, 0.0, sb_l, ALU.max, ALU.add).then_inc(SB["sp"], 1)
                if s == 7:
                    dve.wait_ge(SB["cum"], g + 1)
                    tt(sb_z, sb_z, pa[:, :, 0:TRI], ALU.subtract).then_inc(SB["u"], 1)
                if s == 11:
                    split_out(SB, g, 4)
            project(PH["gate0"], side=side_sb, mid=gates_of(PH["gate0"]))
            dve.wait_ge(gate_done, 16)
            project(PH["branch0"], branch(1))
            project(PH["qi"])
            project(PH["kiwi"])

            wi = small[:, 176:192].rearrange("p (t h) -> p t h", t=NT)

            def side_index(j):
                if j in (0, 1):
                    if j == 0:
                        dve.wait_ge(block_out, PH["qi"].b0 + 2)
                    rope(qi[:, j, :], IH, ID // 2, 1, j, rope_a, rope_b)
                if j == 2:
                    dve.wait_ge(block_out, PH["kiwi"].b0 + 1)
                    nc.vector.tensor_scalar(wi, ki_wi[:, :, ID:ID + IH], IH ** -0.5, None, ALU.mult).then_inc(dve_own, 1)
                    own[0] += 1
                    rope(ki_wi[:, 0, 0:ID], 1, ID // 2, 1, 0, rope_a, rope_b)
                    rope(ki_wi[:, 1, 0:ID], 1, ID // 2, 1, 1, rope_a, rope_b, IX["roped"])
                if j in (10, 13):
                    t = (j - 10) // 3
                    dve.wait_ge(IX["relu"], t + 1)
                    n = P * (t + 1)
                    sc = score[:, t * P:t * P + n]
                    for h in range(IH):
                        v, w = logits[:, h * n:(h + 1) * n], wi[:, t, h:h + 1]
                        if h == 0:
                            ins = nc.vector.tensor_scalar(sc, v, w, None, ALU.mult)
                        else:
                            ins = nc.vector.scalar_tensor_tensor(sc, v, w, sc, ALU.mult, ALU.add)
                        if h < IH - 1:
                            link(ins)
                    ins.then_inc(IX["score"], 1)
                if j == 14:
                    dve.wait_ge(IX["score"], 2)
                    link(nc.vector.memset(score[0:CH, CH:P], NEG_INADMISSIBLE))
                    link(nc.vector.memset(score[0:CH, TRI - CH:TRI], NEG_INADMISSIBLE))
                    link(nc.vector.tensor_copy(left, score))
            project(PH["qb"], side=side_index)

            def top_round():
                for t, c in enumerate(TRIS):
                    m = small[:, 192 + 8 * t:200 + 8 * t]
                    own[0] += 1
                    nc.vector.max(m, left[:, c]).then_inc(dve_own, 1)
                dve.wait_ge(dve_own, own[0])
                for t, c in enumerate(TRIS):
                    m = small[:, 192 + 8 * t:200 + 8 * t]
                    own[0] += 1
                    nc.vector.match_replace(left[:, c], m, left[:, c], NEG_TAKEN).then_inc(dve_own, 1)
                dve.wait_ge(dve_own, own[0])

            def head_scale(n, rows, g, at, hs):
                for t, h in hs:
                    v = rows[:, t, h * HD:(h + 1) * HD]
                    own[0] += 1
                    nc.vector.scalar_tensor_tensor(v, v, small[:, at + 8 * t + h:at + 8 * t + h + 1],
                                                   qk_gain[:, g, :], ALU.mult, ALU.mult).then_inc(dve_own, 1)
                dve.wait_ge(dve_own, own[0])

            def head_steps(n, rows, g, at, j):
                if j == 2:
                    head_inverse(n, dsa_sq.rearrange("p t (h d) -> p t h d", d=HD), at, HEADS, HD)
                if j == 4:
                    norm_at(dve, n, "rstd", 1)
                if j in (4, 5, 7, 9):
                    t, half = {4: (0, 0), 5: (0, 1), 7: (1, 0), 9: (1, 1)}[j]
                    head_scale(n, rows, g, at, [(t, 4 * half + k) for k in range(4)])
                if j in (6, 8, 10, 12):
                    t, half = (j - 6) // 4, (j - 6) // 2 % 2
                    rope(rows[:, t, half * 512:(half + 1) * 512], 4, HD // 2, 0, t, rope_a, rope_b,
                         HEADN["scaled"] if j == 12 else None)

            def side_dsaq(j):
                head_steps("dsaq", val, 0, 64, j)
                if j in (0, 1, 3, 11, 13, 15):
                    top_round()

            def side_dsak(j):
                head_steps("dsak", kb_rows, 1, 80, j)
                if j in (0, 1):
                    top_round()
                if j == 3:
                    link(tt(chosen, left, score, ALU.is_equal))
                    nc.vector.tensor_scalar(chosen, chosen, HIDDEN, None, ALU.mult).then_inc(IX["chosen"], 1)
            project(PH["kb"], side=side_dsaq)
            project(PH["vb"], side=side_dsak)

            def causal_attention(a, g, s, p, mask, scale):
                if s == 0:
                    dve.wait_ge(ATT[a]["scores"], g + 1)
                    link(nc.vector.scalar_tensor_tensor(p, pa[:, :, 0:TRI], scale,
                                                        mask.unsqueeze(1).to_broadcast([P, 4, TRI]),
                                                        ALU.mult, ALU.add))
                    negative_max(a, g, p, 1.0, TRIS)
                if s == 1:
                    normalise(a, g, p, TRIS)

            def side_dsa(j):
                g, s = (0, j) if j < 13 else (1, j - 13)
                if j >= 26:
                    return
                if j == 0:
                    dve.wait_ge(IX["chosen"], 1)
                if s in (3, 7):
                    causal_attention("dsa", g, (s - 3) // 4, probs, chosen, HD ** -0.5)
                if s == 12:
                    split_out(ATT["dsa"], g, 4)
            project(PH["gate1"], side=side_dsa, mid=gates_of(PH["gate1"]))
            dve.wait_ge(gate_done, 24)

            def merged_rest(k):
                dve.wait_ge(merged_hi, k + 1)
                tt(h_lo[:, 4 * k:4 * k + 4, :], merged[:, 4 * k:4 * k + 4, :],
                   h_hi[:, 4 * k:4 * k + 4, :].bitcast(F32), ALU.subtract).then_inc(merged_ready, 1)
            project(PH["branch1"], branch(2),
                    side=lambda j: merged_rest((j - 5) // 4) if j in (5, 9, 13) else None)
            merged_rest(3)

            def add_to_x(b, r):
                v = xT[:, bass.ds(b * 2, 2), :]
                tt(v, v, blk[:, r, :, 0:S], ALU.add).then_inc(block_out, 1)

            def first_add_to_x(b, r):
                if b == 0:
                    dve.wait_ge(turned_out, 12)
                add_to_x(b, r)

            def side_lo(n, gain, bt):
                def side(j):
                    if j % bt == 0 and j > 0:
                        b = j // bt - 1
                        unit_norm(n, (2 * b, 2 * b + 1), xT, gain, u_hi, u_lo)
                return side
            project(PH["wout"], first_add_to_x, side=side_lo("ffn", "ffn_norm", 4))
            unit_norm("ffn", (14, 15), xT, "ffn_norm", u_hi, u_lo)


            def conv_scale(f):
                ph, g0 = PH[f"up{f}"], FFN[f][0]

                def go(b, r):
                    if isinstance(b, int) and b + g0 == 0:
                        norm_at(dve, "ffn", "rstd", 1)
                    tt(conv_in[:, r], blk[:, r, :, 0:S], RSTD["ffn"].unsqueeze(1).to_broadcast([P, 2, S]),
                       ALU.mult).then_inc(block_out, 1)
                return go

            def conv_rest(f):
                ph, g0 = PH[f"up{f}"], FFN[f][0]

                def taps(b, r):
                    dve.wait_ge(conv_mid, b * 2 + (2 * g0 + 2))
                    for c in range(2):
                        nc.vector.scalar_tensor_tensor(conv[:, r, c, 1:S], conv_in[:, r, c, 0:S - 1],
                                                       col("conv_w1", b + (c * KF + g0)), conv[:, r, c, 1:S],
                                                       ALU.mult, ALU.add).then_inc(conv_one, 1)
                    dve.wait_ge(conv_one, b * 2 + (2 * g0 + 2))
                    for c in range(2):
                        nc.vector.scalar_tensor_tensor(conv[:, r, c, 2:S], conv_in[:, r, c, 0:S - 2],
                                                       col("conv_w0", b + (c * KF + g0)), conv[:, r, c, 2:S],
                                                       ALU.mult, ALU.add).then_inc(
                                                           conv_out if c == 0 else conv_val, 1)

                def product(b, r):
                    dve.wait_ge(silu_out, b + (g0 + 1))
                    dve.wait_ge(conv_val, b + (g0 + 1))
                    tt(ff[:, r, :], gated[:, r, :], conv[:, r, 1, :], ALU.mult).then_inc(ff_out, 1)

                def remainder(b, r):
                    dve.wait_ge(ff_hi, b + (g0 + 1))
                    v = bass.ds(b, 1)
                    tt(h_lo[:, v, :], ff[:, r:r + 1, :], h_hi[:, v, :].bitcast(F32),
                       ALU.subtract).then_inc(ff_ready, 1)

                def mid(j, i):
                    b = i * (ph.period // ph.bt) + j // ph.bt
                    if isinstance(b, int) and b == 0:
                        return
                    r = (ph.b0 + j // ph.bt + 1) % 2
                    if j % ph.bt == 0 and not (isinstance(b, int) and b == 1):
                        remainder(b - 2, 1 - r)
                    if j % ph.bt == 1:
                        taps(b - 1, r)
                    if j % ph.bt == 3:
                        product(b - 1, r)
                return mid, taps, product, remainder
            for f in range(3):
                ph = PH[f"up{f}"]
                mid, taps, product, remainder = conv_rest(f)

                def side_inverse(j):
                    if j == 2:
                        norm_inverse("ffn", col_too=False)
                if f == 0:
                    project(ph, conv_scale(f), mid=mid, side=side_inverse)
                else:
                    project(ph, conv_scale(f), mid=mid, first=1)
                r = (ph.b0 + ph.blocks - 1) % 2
                remainder(ph.blocks - 2, 1 - r)
                taps(ph.blocks - 1, r)
                product(ph.blocks - 1, r)
                remainder(ph.blocks - 1, r)
                if f < 2:
                    project(PH[f"down{f}"], add_to_x)
            project(PH["down2"], add_to_x, side=side_lo("pre0", "l0_pre", PH["down2"].bt))
            unit_norm("pre0", (14, 15), xT, "l0_pre", u_hi, u_lo)

            nc.vector.memset(lowT[0:32, :], 1.0).then_inc(GL["bias_row"], 1)
            project(PH["glaqk"], scaled_to(area(0, 4 * GH, S), "pre0"),
                    lead=lambda j: norm_inverse("pre0") if j == 2 else None)
            project(PH["decay"])
            b8 = pa[:, :, :].rearrange("p b (c s) -> p (b c) s", c=2)
            last = small[:, 96:128].rearrange("p (c n) -> p c n", c=2 * GH)
            decay = small[:, 128:160].rearrange("p (c n) -> p c n", c=2 * GH)

            def side_decay(j):
                if j == 5:
                    dve.wait_ge(GL["l"], 1)
                    v = g_la.rearrange("p t (b c) -> p (t b) c", b=2)
                    nc.vector.scalar_tensor_tensor(v, pa[:, :, :], 0.0, v, ALU.min, ALU.subtract).then_inc(GL["la"], 1)
                if j == 9:
                    dve.wait_ge(GL["cum"], 1)
                    nc.vector.tensor_copy(last, b8[:, :, CH - 1:S:CH]).then_inc(GL["last"], 1)
                if j == 10:
                    dve.wait_ge(GL["eb"], 1)
                    dve.wait_ge(block_out, PH["glav"].b0)
                    nc.vector.scalar_tensor_tensor(g_q, g_q, GK ** -0.5, g_e, ALU.mult, ALU.mult).then_inc(GL["q"], 1)
                if j == 13:
                    dve.wait_ge(GL["enb"], 1)
                    tt(g_ke, g_k, g_e, ALU.mult).then_inc(GL["ke"], 1)
                if j == 14:
                    dve.wait_ge(GL["ke"], 1)
                    dve.wait_ge(GL["last"], 1)
                    for c in range(2 * GH):
                        tt(g_e[:, c, :].rearrange("p (n s) -> p n s", n=4),
                           last[:, c, :].unsqueeze(2).to_broadcast([P, 4, CH]),
                           b8[:, c, :].rearrange("p (n s) -> p n s", n=4), ALU.subtract).then_inc(GL["diff"], 1)
                if j == 17:
                    dve.wait_ge(GL["el"], 2)
                    tt(g_k, g_k, g_e, ALU.mult).then_inc(GL["kl"], 1)
                if j in (20, 23, 26):
                    n = (j - 20) // 3
                    dve.wait_ge(GL["rows"], n + 1)
                    if n == 0:
                        dve.wait_ge(GL["kl"], 1)
                    else:
                        for c in range(2 * GH):
                            own[0] += 1
                            nc.vector.tensor_scalar(g_ke[:, c, 0:n * CH], g_ke[:, c, 0:n * CH],
                                                    decay[:, c, n:n + 1], None, ALU.mult).then_inc(dve_own, 1)
                        dve.wait_ge(dve_own, own[0])
                    v = slice(n * CH, (n + 1) * CH)
                    nc.vector.tensor_copy(g_ke[:, :, v], g_k[:, :, v]).then_inc(GL["step"], 1)
            project(PH["glav"], side=side_decay)

            def side_gla(j):
                if j == 12:
                    dve.wait_ge(GL["sum"], 1)
                    link(nc.vector.tensor_scalar(g_rstd.rearrange("p (b c) s -> p b (c s)", b=2), pa[:, 0:2, :],
                                                 1.0 / GV, EPS, ALU.mult, ALU.add))
                if 12 <= j < 12 + GH:
                    v = g_rstd[:, j - 12, :]
                    nc.vector.reciprocal(v, v).then_inc(GL["inv"], 1)
                if 16 <= j < 20:
                    dve.wait_ge(GL["rstd"], 1)
                    h = j - 16
                    for c in range(4):
                        v = g_o[:, 4 * h + c, :]
                        nc.vector.scalar_tensor_tensor(v, v, col("g_onorm", c), g_rstd[:, h, :],
                                                       ALU.mult, ALU.mult).then_inc(GL["scaled"], 1)
                if j == 29:
                    gate_gla(3)
                if j in (19, 21, 27, 31):
                    gla_rest({19: 0, 21: 1, 27: 2, 31: 3}[j])

            def gla_part(k):
                return slice(4 * k, 4 * k + 4) if k < 3 else slice(2 * k + 6, 2 * k + 8)

            def gate_gla(k):
                dve.wait_ge(silu_done, k + 4)
                dve.wait_ge(GL["on"], k)
                dve.wait_ge(GL["scaled"], KD)
                v = gla_part(k)
                tt(g_o[:, v, :], g_o[:, v, :], g_gate[:, v, :], ALU.mult).then_inc(GL["on"], 1)

            def gla_rest(k):
                dve.wait_ge(GL["hi"], k + 1)
                v = gla_part(k)
                tt(h_lo[:, v, :], g_o[:, v, :], h_hi[:, v, :].bitcast(F32), ALU.subtract).then_inc(GL["ready"], 1)
            project(PH["glagate"], scaled_to(g_gate, "pre0"), side=side_gla)
            gate_gla(4)
            gla_rest(4)
            project(PH["glaout"])

            norm_inverse("post0", col_too=False)
            for k in range(4):
                y_times_rstd("post0", y_gla, 0, k)
                if k > 0:
                    unit_norm("pre1", range(4 * k - 4, 4 * k), xT, "l1_pre", u_hi, u_lo)
                y_added(0, k)
            unit_norm("pre1", range(12, 16), xT, "l1_pre", u_hi, u_lo)

            def latent_block(b):
                n, at = (("qa", 0), ("kva", KL))[b // 2]
                unit_norm(n, (2 * (b % 2), 2 * (b % 2) + 1), latent[:, at:at + KL], "g_" + n,
                          h_hi[:, at:at + KL], h_lo[:, at:at + KL])

            def side_latent(j):
                if j == 2:
                    norm_inverse("pre1")
                if j in (5, 9, 13):
                    latent_block((j - 5) // 4)
                if j == 13:
                    norm_inverse("qa", dim=LRANK)
            project(PH["latent"], scaled_to(latent, "pre1"), side=side_latent)

            def side_kva(j):
                if j == 0:
                    latent_block(3)
                if j == 2:
                    norm_inverse("kva", dim=LRANK)
            project(PH["krope"], side=side_kva)
            dve.wait_ge(block_out, PH["krope"].b0 + 1)
            for t in range(NT):
                rope(k_rope[:, t, 0:LR], 1, LR // 2, 2, t, l_rope_a, l_rope_b)
            nc.vector.tensor_copy(k_rope[:, :, LR:2 * LR], k_rope[:, :, 0:LR]).then_inc(ML["k_roped"], 1)
            project(PH["qrope"])

            def gate_quarter(k):
                dve.wait_ge(silu_done, 8 + 2 * (k + 1))
                dve.wait_ge(ML["out"], k + 1)
                v = slice(4 * k, 4 * k + 4)
                g = slice(4 * (k % 2), 4 * (k % 2) + 4)
                tt(l_o[:, v, :], l_o[:, v, :], l_gate[:, g, :], ALU.mult).then_inc(ML["gated"], 1)

            def gated_rest(k):
                dve.wait_ge(ML["hi"], k + 1)
                v = slice(4 * k, 4 * k + 4)
                tt(h_lo[:, v, :], l_o[:, v, :], h_hi[:, v, :].bitcast(F32), ALU.subtract).then_inc(ML["ready"], 1)

            for r in range(2):
                def q_rope_part(k):
                    t, half = k // 2, k % 2
                    rope(q_rope[:, t, half * 512:(half + 1) * 512], LH // 2, LR // 2, 2, t, l_rope_a, l_rope_b,
                         ML["q_roped"] if k == 3 else None)
                project(PH[f"qnope{r}"], scaled_to(q_nope, "qa"),
                        side=lambda j, r=r: q_rope_part(j // 2) if r == 0 and j % 2 == 0 else None)

                def kv_out(b, rr):
                    if isinstance(b, int) and b == 0:
                        norm_at(dve, "kva", "rstd", 1)
                    for t in range(NT):
                        nc.vector.tensor_scalar(l_v[:, t:t + 1, bass.ds(b * P, P)],
                                                blk[:, rr, 1:2, t * P:(t + 1) * P], RSTD_COL["kva"][:, t:t + 1],
                                                None, ALU.mult)
                    tt(k_nope[:, bass.ds(b, 1), :], blk[:, rr, 0:1, 0:S], RSTD["kva"].unsqueeze(1),
                       ALU.mult).then_inc(block_out, 1)
                project(PH[f"kv{r}"], kv_out,
                        side=lambda j, r=r: q_rope_part(2 + j // 3) if r == 0 and j in (1, 4) else None)

                def side_mla(j, r=r):
                    g, s = (0, j) if j < 8 else (1, j - 8)
                    if j == 1:
                        dve.wait_ge(consts, 6)
                    if s in (1, 2):
                        causal_attention("mla", 2 * r + g, s - 1, lprobs, causal, (LN + LR) ** -0.5)
                    if j == 10:
                        gate_quarter(2 * r)
                    if r == 1 and j in (8, 10, 13):
                        gated_rest({8: 0, 10: 1, 13: 2}[j])
                project(PH[f"mlagate{r}"], scaled_to(l_gate, "pre1"), side=side_mla)
                gate_quarter(2 * r + 1)
            gated_rest(3)
            project(PH["mlaout"])
            norm_inverse("post1", col_too=False)
            for k in range(4):
                y_times_rstd("post1", y_mla, 4, k)
                y_added(4, k)


_INS = ["x", "mem", "positions", "attn_norm", "mem_norm", "w_in", "b_gate", "dsa_q_norm", "dsa_k_norm",
        "mem_q_norm", "mem_k_norm", "w_mem_kv", "w_branch", "w_out", "ffn_norm", "w_up", "conv_w",
        "conv_b", "w_down", "positions_2", "l0_pre_norm_2", "l0_gla_w_in_2", "l0_gla_w_gk2_2",
        "l0_gla_b_gk_2", "l0_gla_g_onorm_2", "l0_gla_w_out_2", "l0_post_norm_2", "l1_pre_norm_2",
        "l1_mla_w_in_2", "l1_mla_g_qa_2", "l1_mla_w_qb_2", "l1_mla_g_kva_2", "l1_mla_w_kvb_2",
        "l1_mla_w_out_2", "l1_post_norm_2"]


def kernel(**inputs):
    import concourse.bacc as _bacc
    from concourse.bass_utils import run_bass_kernel_spmd as _run

    nc = _bacc.Bacc("TRN2", target_bir_lowering=False, num_devices=1)
    arrays, args = {}, []
    named = [(name, np.ascontiguousarray(inputs[name])) for name in _INS]
    for half in (64, 32):
        freq = (10000.0 ** (-np.arange(half, dtype=np.float64) / half)).astype(np.float32)
        named.append((f"inv{half}", freq))
    for name, a in named:
        arrays[f"in_{name}_dram"] = a
        args.append(nc.dram_tensor(f"in_{name}_dram", a.shape, mybir.dt.from_np(a.dtype),
                                   kind="ExternalInput").ap())
    out = nc.dram_tensor("out_0_dram", (1, S, D), F32, kind="ExternalOutput").ap()
    build_program(nc, *args, out)
    r = _run(nc, [arrays], core_ids=[0])
    return r.results[0]["out_0_dram"]
```
